# Optimizing a Trainium2 kernel written in Bass

```python
import math
import jax, jax.numpy as jnp
from jax import lax
import numpy as np

D_MODEL = 1024
BATCH = 1
SEQ = 512
DEPTH = 2

N_A = (DEPTH + 1) // 2
N_B = DEPTH - N_A

GLA_HEADS = 4
QK_DIM = D_MODEL // 2
V_DIM = D_MODEL
DK = QK_DIM // GLA_HEADS
DV = V_DIM // GLA_HEADS
GATE_RANK = 16
GATE_NORMALIZER = 16.0
CHUNK = 64
A_IN_DIM = 2 * QK_DIM + V_DIM + GATE_RANK + V_DIM

SB_HEADS = 16
SB_HEAD_DIM = D_MODEL // SB_HEADS
SB_DIM = SB_HEADS * SB_HEAD_DIM
Q_BLOCK = 128

N_GROUPS = 4
EXPERTS_PER_GROUP = 4
N_EXPERTS = N_GROUPS * EXPERTS_PER_GROUP
TOP_K = 2
D_EXPERT = D_MODEL // 2

RMS_EPS = 1e-6

kernel_name = "yoco_gla_stickbreaking_hmoe"

def rms_norm(x, g):
    xf = x.astype(jnp.float32)
    y = xf * lax.rsqrt(jnp.mean(xf * xf, axis=-1, keepdims=True) + RMS_EPS)
    return (y * g.astype(jnp.float32)).astype(x.dtype)

def gla_mixer(u, w_in, w_gk2, b_gk2, o_norm, w_out):
    B, S, _ = u.shape
    n = S // CHUNK
    proj = u @ w_in
    q, k, v, gk_lr, g = jnp.split(
        proj, [QK_DIM, 2 * QK_DIM, 2 * QK_DIM + V_DIM, 2 * QK_DIM + V_DIM + GATE_RANK], axis=-1)
    gk = jax.nn.log_sigmoid((gk_lr @ w_gk2 + b_gk2).astype(jnp.float32)) / GATE_NORMALIZER

    def to_chunks(t, dh):
        return t.reshape(B, n, CHUNK, GLA_HEADS, dh).transpose(0, 3, 1, 2, 4).astype(jnp.float32)

    q = to_chunks(q, DK) * (DK ** -0.5)
    k = to_chunks(k, DK)
    v = to_chunks(v, DV)
    gk = to_chunks(gk, DK)
    b = jnp.cumsum(gk, axis=3)
    q_dec = q * jnp.exp(b)
    k_inv = k * jnp.exp(-b)

    causal = jnp.tril(jnp.ones((CHUNK, CHUNK), dtype=bool))
    att = jnp.where(causal, jnp.einsum('bhnid,bhnjd->bhnij', q_dec, k_inv), 0.0)
    o_intra = jnp.einsum('bhnij,bhnje->bhnie', att, v)

    b_last = b[:, :, :, -1, :]
    k_to_end = k * jnp.exp(b_last[:, :, :, None, :] - b)
    upd = jnp.einsum('bhncd,bhnce->bhnde', k_to_end, v)

    def step(state, inp):
        dec, u_n = inp
        return dec[..., None] * state + u_n, state

    init = jnp.zeros((B, GLA_HEADS, DK, DV), jnp.float32)
    _, prev = lax.scan(step, init, (jnp.moveaxis(jnp.exp(b_last), 2, 0), jnp.moveaxis(upd, 2, 0)))
    prev = jnp.moveaxis(prev, 0, 2)
    o = o_intra + jnp.einsum('bhncd,bhnde->bhnce', q_dec, prev)

    o = rms_norm(o, o_norm)
    o = o.transpose(0, 2, 3, 1, 4).reshape(B, S, V_DIM)
    o = o * jax.nn.silu(g.astype(jnp.float32))
    return o.astype(u.dtype) @ w_out

def stick_breaking_attention(q, k, v):
    S = q.shape[2]
    scale = 1.0 / math.sqrt(SB_HEAD_DIM)
    outs = []
    for blk in range(S // Q_BLOCK):
        t0 = blk * Q_BLOCK
        L = t0 + Q_BLOCK
        qb = q[:, :, t0:L].astype(jnp.float32)
        kb = k[:, :, :L].astype(jnp.float32)
        vb = v[:, :, :L].astype(jnp.float32)
        z = jnp.einsum('bhtd,bhsd->bhts', qb, kb) * scale
        tpos = t0 + jnp.arange(Q_BLOCK)
        spos = jnp.arange(L)
        mask = spos[None, :] < tpos[:, None]
        log_om = jnp.where(mask, jax.nn.log_sigmoid(-z), 0.0)
        log_beta = jax.nn.log_sigmoid(z)
        suffix = lax.cumsum(log_om, axis=3, reverse=True) - log_om
        a = jnp.where(mask, jnp.exp(log_beta + suffix), 0.0)
        outs.append(jnp.einsum('bhts,bhsd->bhtd', a, vb))
    return jnp.concatenate(outs, axis=2)

def stick_breaking_mixer(u, k, v, w_q, w_out):
    B, S, _ = u.shape
    q = (u @ w_q).reshape(B, S, SB_HEADS, SB_HEAD_DIM).transpose(0, 2, 1, 3)
    o = stick_breaking_attention(q, k, v)
    o = o.transpose(0, 2, 1, 3).reshape(B, S, SB_DIM).astype(u.dtype)
    return o @ w_out

def hier_moe(t, w_group, b_group, w_expert, b_expert, w_gate, w_up, w_down):
    T = t.shape[0]
    g_logits = (t @ w_group + b_group).astype(jnp.float32)
    g_prob = jax.nn.softmax(g_logits, axis=-1)
    g_w, g_idx = lax.top_k(g_prob, 1)
    e_logits = (t @ w_expert + b_expert).astype(jnp.float32).reshape(T, N_GROUPS, EXPERTS_PER_GROUP)
    e_sel = jnp.take_along_axis(e_logits, g_idx[:, :, None], axis=1)[:, 0]
    e_prob = jax.nn.softmax(e_sel, axis=-1)
    e_w, e_idx = lax.top_k(e_prob, TOP_K)
    e_w = e_w / jnp.sum(e_w, axis=-1, keepdims=True)
    weights = g_w * e_w
    global_idx = g_idx * EXPERTS_PER_GROUP + e_idx
    combine = jnp.einsum('tk,tke->te', weights, jax.nn.one_hot(global_idx, N_EXPERTS, dtype=jnp.float32))
    y = jnp.zeros(t.shape, jnp.float32)
    for e in range(N_EXPERTS):
        hdn = jax.nn.silu(t @ w_gate[e]) * (t @ w_up[e])
        y = y + combine[:, e:e + 1] * (hdn @ w_down[e]).astype(jnp.float32)
    return y.astype(t.dtype)

def setup_inputs(seed: int = 0) -> dict:
    key = jax.random.key(seed)
    ks = iter(jax.random.split(key, 32))
    f32 = jnp.float32

    def nrm(shape, scale):
        return jax.random.normal(next(ks), shape, f32) * scale

    def gain(shape):
        return 1.0 + 0.01 * jax.random.normal(next(ks), shape, f32)

    D = D_MODEL
    return {
        "x": jax.random.normal(next(ks), (BATCH, SEQ, D), f32),
        "a_norm": gain((N_A, D)),
        "a_w_in": nrm((N_A, D, A_IN_DIM), D ** -0.5),
        "a_w_gk2": nrm((N_A, GATE_RANK, QK_DIM), GATE_RANK ** -0.5),
        "a_b_gk2": nrm((N_A, QK_DIM), 0.01),
        "a_o_norm": gain((N_A, DV)),
        "a_w_out": nrm((N_A, V_DIM, D), V_DIM ** -0.5),
        "kv_norm": gain((D,)),
        "w_kv": nrm((D, 2 * SB_DIM), D ** -0.5),
        "b_norm": gain((N_B, D)),
        "b_w_q": nrm((N_B, D, SB_DIM), D ** -0.5),
        "b_w_out": nrm((N_B, SB_DIM, D), SB_DIM ** -0.5),
        "m_norm": gain((DEPTH, D)),
        "m_w_group": nrm((DEPTH, D, N_GROUPS), D ** -0.5),
        "m_b_group": nrm((DEPTH, N_GROUPS), 0.01),
        "m_w_expert": nrm((DEPTH, D, N_EXPERTS), D ** -0.5),
        "m_b_expert": nrm((DEPTH, N_EXPERTS), 0.01),
        "m_w_gate": nrm((DEPTH, N_EXPERTS, D, D_EXPERT), D ** -0.5),
        "m_w_up": nrm((DEPTH, N_EXPERTS, D, D_EXPERT), D ** -0.5),
        "m_w_down": nrm((DEPTH, N_EXPERTS, D_EXPERT, D), D_EXPERT ** -0.5),
        "final_norm": gain((D,)),
    }

def reference(x, a_norm, a_w_in, a_w_gk2, a_b_gk2, a_o_norm, a_w_out, kv_norm, w_kv,
              b_norm, b_w_q, b_w_out, m_norm, m_w_group, m_b_group, m_w_expert, m_b_expert,
              m_w_gate, m_w_up, m_w_down, final_norm):
    B, S, D = x.shape
    h = x
    k_shared = None
    v_shared = None
    for layer in range(DEPTH):
        if layer < N_A:
            h = h + gla_mixer(rms_norm(h, a_norm[layer]), a_w_in[layer], a_w_gk2[layer],
                              a_b_gk2[layer], a_o_norm[layer], a_w_out[layer])
        else:
            if layer == N_A:
                kv = rms_norm(h, kv_norm) @ w_kv
                k_s, v_s = jnp.split(kv, 2, axis=-1)
                k_shared = k_s.reshape(B, S, SB_HEADS, SB_HEAD_DIM).transpose(0, 2, 1, 3)
                v_shared = v_s.reshape(B, S, SB_HEADS, SB_HEAD_DIM).transpose(0, 2, 1, 3)
            j = layer - N_A
            h = h + stick_breaking_mixer(rms_norm(h, b_norm[j]), k_shared, v_shared, b_w_q[j], b_w_out[j])
        t = rms_norm(h, m_norm[layer]).reshape(B * S, D)
        h = h + hier_moe(t, m_w_group[layer], m_b_group[layer], m_w_expert[layer], m_b_expert[layer],
                         m_w_gate[layer], m_w_up[layer], m_w_down[layer]).reshape(B, S, D)
    return rms_norm(h, final_norm)


_drawn_inputs = setup_inputs


def setup_inputs(seed=0):
    import zlib

    import numpy as np

    out = dict(_drawn_inputs(seed))
    spreads = {}
    factors = {'a_b_gk2': 3.748,
     'kv_norm': 4.57,
     'b_norm': 7.94,
     'm_b_group': 2.79,
     'm_b_expert': 3.998,
     'final_norm': 5.898}
    for name, (base, spread) in spreads.items():
        noise = np.random.default_rng([zlib.crc32(name.encode()), seed]).standard_normal(out[name].shape)
        drawn = base * np.exp(spread * noise) if base else spread * noise
        out[name] = __import__('jax').numpy.asarray(drawn.astype(out[name].dtype))
    for name, factor in factors.items():
        out[name] = (out[name] * factor).astype(out[name].dtype)
    return out
```

```python
from contextlib import ExitStack

import concourse.bass as bass
from concourse import mybir

F32 = mybir.dt.float32
F32R = mybir.dt.float32r
BF16 = mybir.dt.bfloat16
I32 = mybir.dt.int32
U32 = mybir.dt.uint32
ALU = mybir.AluOpType
ACT = mybir.ActivationFunctionType
AX = mybir.AxisListType

P = 128
D = 1024
T = 512
NT = T // P
KT = D // P
EPS = 1e-6
LAYERS = 2

GH, DK, DV, RANK, CHUNK = 4, 128, 256, 16, 64
GATE_NORM = 16.0
QK = GH * DK
GK0 = 2 * QK + D
G0 = GK0 + RANK
NCH = T // CHUNK

SH, SD = 16, 64
ZW = [T - P * i for i in range(NT)]
ZO = [0, T, 2 * T, 2 * T - P]
ZC = 2 * T + 2 * P

NG, EG = 4, 4
NE = NG * EG
F = 512
NR = NG + NE
CAP = 96
MAX_OVER = 10
ROWS = (NE + MAX_OVER) * CAP
STEPS_OVER = (T - 1) // CAP

BK = 4
BN = 512
BW = BK * BN
RAW = 4
SPLIT = 2
N_CONSTS = 2
A_BLOCKS = 16
E_BLOCKS = 6
L_BLOCKS = A_BLOCKS + NE * E_BLOCKS


class Chain:

    def __init__(self, eng, sem):
        self.eng, self.sem, self.n = eng, sem, 0

    def __call__(self, ins):
        ins.then_inc(self.sem, 1)
        self.n = self.n + 1
        self.eng.wait_ge(self.sem, self.n)


def trunk(nc, x, a_norm, a_w_in, a_w_gk2, a_b_gk2, a_o_norm, a_w_out, kv_norm, w_kv, b_norm, b_w_q,
          b_w_out, m_norm, m_w_group, m_b_group, m_w_expert, m_b_expert, m_w_gate, m_w_up, m_w_down,
          final_norm, out):
    with ExitStack() as ctx:
        def sb(name, shape, dt=F32):
            return ctx.enter_context(nc.sbuf_tensor(name, shape, dt))

        def sem(name):
            return ctx.enter_context(nc.semaphore(name))

        table = nc.dram_tensor("token_table", [ROWS, D], F32).ap()
        h = sb("h", [P, NT, D])
        xn = sb("xn", [P, NT, D])
        xT_hi = sb("xT_hi", [P, KT, T], F32R)
        xT_lo = sb("xT_lo", [P, KT, T], F32R)
        raw = sb("raw", [P, RAW, BW])
        w_hi = sb("w_hi", [P, SPLIT, BW], F32R)
        w_lo = sb("w_lo", [P, SPLIT, BW], F32R)
        s_hi = sb("s_hi", [P, ZC], F32R)
        s_lo = sb("s_lo", [P, ZC], F32R)
        r_hi = sb("r_hi", [P, KT, NR], F32R)
        r_lo = sb("r_lo", [P, KT, NR], F32R)
        gain = sb("gain", [P, D])
        pad = sb("pad", [P, 14336 + DV])
        zeros = sb("zeros", [P, 256])
        ident = sb("ident", [P, P])
        ident_b = sb("ident_b", [P, P], BF16)
        neg_mask = sb("neg_mask", [P, P], BF16)
        before = sb("before", [P, P], BF16)
        ones_b = sb("ones_b", [P, P], BF16)
        neg_tri = sb("neg_tri", [P, P], F32R)
        neg_one = sb("neg_one", [P, P], F32R)
        lr_raw = sb("lr_raw", [P, KT, RANK])
        bgk = sb("bgk", [P, GH])
        r_raw = sb("r_raw", [P, LAYERS, KT, NR])
        r_bias = sb("r_bias", [P, LAYERS, NR])
        ss = sb("ss", [P, 16])
        ms = sb("ms", [P, 16])
        y0 = sb("y0", [P, 16])
        y1 = sb("y1", [P, 16])
        rstd = sb("rstd", [P, 16])
        decay = sb("decay", [P, GH, NCH])
        w12 = sb("w12", [P, 2, NT])
        pos = sb("pos", [P, 2, NT], U32)
        over = sb("over", [1, MAX_OVER + 1], I32)

        def region(start, width):
            return pad[:, start:start + width]

        qT = region(0, 2048).rearrange("p (h t) -> p h t", h=GH)
        kT = region(2048, 2048).rearrange("p (h t) -> p h t", h=GH)
        kinv = region(4096, 2048).rearrange("p (h t) -> p h t", h=GH)
        gate = region(6144, 2048).rearrange("p (h t) -> p h t", h=GH)
        lrT = pad[0:RANK, 4096:4096 + T]
        wgk2 = pad[0:RANK, 4096 + T:4096 + 2 * T]
        v = region(8192, 4096).rearrange("p (i n) -> p i n", i=NT)
        state = region(12288, 2048).rearrange("p (b h e) -> p b h e", b=2, h=GH)
        reset = region(12288, T)
        onorm = region(14336, DV)
        sg = region(0, 4096).rearrange("p (i n) -> p i n", i=NT)
        cum = xn[:, 0:2, :].rearrange("p a (b t) -> p (a b) t", b=2)
        kT1 = region(0, 4096).rearrange("p (q t) -> p q t", q=KT)
        qT1 = region(4096, 4096).rearrange("p (q t) -> p q t", q=KT)
        kst = region(12288, 2 * T).rearrange("p (b t) -> p b t", b=2)
        qst = region(12288 + 2 * T, 2 * T).rearrange("p (b t) -> p b t", b=2)
        xnf = xn[:, :, :].rearrange("p i n -> p (i n)")
        vst = xnf[:, 2 * ZC:2 * ZC + 2 * T].rearrange("p (b i e) -> p b i e", b=2, i=NT)
        zt = [xnf[:, 0:ZC], xnf[:, ZC:2 * ZC]]
        xg = pad[0:CAP, 0:2 * D].rearrange("p (b n) -> p b n", b=2)
        sil = pad[0:CAP, 2048:2048 + F]
        hid = pad[0:CAP, 2560:2560 + F]
        y_sb = pad[0:CAP, 3072:3072 + D]
        over_raw = region(4096, BW)
        xg_hi, xg_lo = (t[:, 0:KT * CAP].rearrange("p (k c) -> p k c", k=KT) for t in (s_hi, s_lo))
        ht_hi, ht_lo = (t[:, KT * CAP:(KT + BK) * CAP].rearrange("p (k c) -> p k c", k=BK)
                        for t in (s_hi, s_lo))
        lr_hi, lr_lo = (t[:, 0:KT * P].rearrange("p (k c) -> p k c", k=KT) for t in (s_hi, s_lo))
        rt0 = 6144
        names = "em eq ev oh1 oh2 em2 tmp rank posn".split()
        R = {n: region(rt0 + 64 * i, 64).rearrange("p (i e) -> p i e", i=NT) for i, n in enumerate(names)}
        rt1 = rt0 + 64 * len(names)
        lg = region(rt1, NT * NR).rearrange("p (i e) -> p i e", i=NT)
        rt2 = rt1 + NT * NR
        G4 = {n: region(rt2 + 16 * i, 16).rearrange("p (i e) -> p i e", i=NT)
              for i, n in enumerate("gd geq gv goh gneg".split())}
        rt3 = rt2 + 16 * 5
        V4 = {n: region(rt3 + 4 * i, 4) for i, n in
              enumerate("gm gvm gs gw m1 evm m2 evm2 dd ex s1 rs p1 p2".split())}
        rt4 = rt3 + 4 * 14
        E16 = {n: region(rt4 + 16 * i, 16) for i, n in enumerate("cnt ovn ovend ovbase delta".split())}
        rt5 = rt4 + 16 * 5
        over_cmp = region(rt5, 160).rearrange("p (j e) -> p j e", j=MAX_OVER)
        over_f = region(rt5 + 160, MAX_OVER + 1)
        desc4 = sb("desc4", [P, NG])
        desc16 = sb("desc16", [P, NE])
        first_row = sb("first_row", [P, NE])
        over_row = sb("over_row", [P, NE])
        j_idx = sb("j_idx", [P, MAX_OVER])
        one16 = sb("one16", [P, NE])
        sel_b = sb("sel_b", [P, NT, NE], BF16)

        ps = ctx.enter_context(nc.psum_tensor("ps", [P, 8, 512], F32))
        psf = ps[:, :, :].rearrange("p b n -> p (b n)")

        def sems(names):
            return {n: sem(n) for n in names.split()}

        x_loaded = [sem(f"x_loaded{i}") for i in range(NT)]
        raw_loaded = [sem(f"raw_loaded{i}") for i in range(RAW)]
        out_stored = sem("out_stored")
        A = sems("small_loaded hi_done act_chain ssq_done rs_first xT_hi_done panel_out lr_hi_done "
                 "gate_ln gate_exp ktok_out o_out r_hi_done group_exp second_exp z_exp z_ln L_hi_done "
                 "weights_done oT_hi_done")
        V = sems("lo_done dve_chain ms_ready xn_ready xT_lo_done h_added lr_lo_done lr_out gates_in "
                 "gate_abs gate_cum q_dec k_inv gate_toend k_toend att_out state_done og_ready r_lo_done "
                 "group_diff second_diff sel_ready pos_ready combined z_abs L_done L_lo_done oT_lo_done")
        M = sems("blk_used xT_tr lr_done gates_done ktok_tr att_done upd_done inter_done logits_done "
                 "ranks_done z_done sums_done av_done")
        G = sems("consts pool_chain masked sg_ready staged gain_loaded zeroed scattered")
        gathered = [sem(f"gathered{i}") for i in range(4)]

        def expert_sems(tag):
            names = "x_loaded0 x_loaded1 x_tr x_hi x_lo silu mul h_tr h_hi h_lo y_out y_stored"
            return {n: sem(f"{tag}_{n}") for n in names.split()}

        E = expert_sems("first")
        O = [expert_sems(f"over{l}") for l in range(LAYERS)]
        OW = [{n: sem(f"over{l}_w_{n}") for n in "loaded hi lo used".split()}
              for l in range(LAYERS)]

        block = ctx.enter_context(nc.Block())
        ve, se, te, ge = nc.vector, nc.scalar, nc.tensor, nc.gpsimd

        def number(c, g=0):
            return 12 * g + c

        def raw_count(c, g=0):
            return 16 * (12 // RAW * g + c // RAW + 1)

        def panel(w, col, k0):
            return w[k0 * P:(k0 + BK) * P, col:col + BN].rearrange("(k p) n -> p k n", p=P)

        a_cols = [0, QK, 2 * QK, 2 * QK + BN, G0, G0 + BN]
        halves = (0, BK)
        streams = [[panel(a_w_in[0], c, k0) for c in a_cols for k0 in halves]
                   + [panel(a_w_out[0], c, k0) for c in (0, BN) for k0 in halves],
                   [panel(w_kv, c, k0) for c in range(0, 2 * D, BN) for k0 in halves]
                   + [panel(b_w_q[0], c, k0) for c in (0, BN) for k0 in halves]
                   + [panel(b_w_out[0], c, k0) for c in (0, BN) for k0 in halves]]

        def expert_block(layer, kind, e, half):
            w = {"g": m_w_gate, "u": m_w_up, "d": m_w_down}[kind][layer]
            w = w[bass.ds(e, 1), :, :].rearrange("o k n -> (o k) n")
            if kind == "d":
                return w[:, half * BN:(half + 1) * BN].rearrange("(k p) n -> p k n", p=P)
            return w[half * BK * P:(half + 1) * BK * P, :].rearrange("(k p) n -> p k n", p=P)

        def blocks_of(layer):
            return layer * L_BLOCKS + A_BLOCKS

        PAIRS = (NE - 2) // 2
        LAST = 4 + E_BLOCKS * (NE - 2)

        def panel_banks(p):
            return slice(4 * (p % 2), 4 * (p % 2) + 4)

        def wait_h(eng, event, i):
            if event == 0:
                eng.wait_ge(x_loaded[i], 16)
            elif event % 2:
                eng.wait_ge(V["h_added"], NT * (event // 2) + i + 1)
            else:
                eng.wait_ge(V["combined"], 2 * NT * (event // 2 - 1) + 2 * (i + 1))

        def over_loop(eng, layer, tile):
            eng.wait_ge(V["pos_ready"], layer + 1)
            n = eng.value_load(over[0:1, MAX_OVER:MAX_OVER + 1], min_val=0, max_val=MAX_OVER)
            with eng.If(n > 0):
                with eng.Fori(0, n) as j:
                    tile(j)
            with eng.Else():
                eng.nop()

        @block.sync
        def _(sp):
            def load(src, c, g=0):
                if c >= RAW:
                    sp.wait_ge(V["lo_done"], number(c - RAW + 1, g))
                sp.dma_start(raw[:, c % RAW, :].rearrange("p (k n) -> p k n", k=BK),
                             src).then_inc(raw_loaded[c % RAW], 16)

            for i in range(NT):
                sp.dma_start(h[:, i, :], x[0, i * P:(i + 1) * P, :]).then_inc(x_loaded[i], 16)
            for layer in range(LAYERS):
                for n, src in enumerate(streams[layer]):
                    load(src, layer * L_BLOCKS + n)
                B = blocks_of(layer)
                for n, (kind, half) in enumerate((k, f) for k in "gu" for f in (0, 1)):
                    load(expert_block(layer, kind, 0, half), B + n)

                def step(e, c, g=0):
                    for n, (kind, back, half) in enumerate((k, b, f) for k, b in zip("gud", (0, 0, 1)) for f in (0, 1)):
                        load(expert_block(layer, kind, e - back, half), c + n, g)

                with sp.Fori(0, PAIRS) as g:
                    for k in range(2):
                        step(2 * g + (k + 1), B + 4 + E_BLOCKS * k, g)
                step(NE - 1, B + LAST)
                for half in (0, 1):
                    load(expert_block(layer, "d", NE - 1, half), B + LAST + E_BLOCKS + half)
            for i in range(NT):
                sp.wait_ge(V["xn_ready"], NT * 5 + i + 1)
                sp.dma_start(out[0, i * P:(i + 1) * P, :], xn[:, i, :]).then_inc(out_stored, 16)
            sp.wait_ge(out_stored, 16 * NT)

        @block.scalar
        def _(act):
            def split(c, g=0):
                act.wait_ge(raw_loaded[c % RAW], raw_count(c, g))
                if c >= SPLIT:
                    act.wait_ge(M["blk_used"], number(c - SPLIT + 1, g))
                se.copy(w_hi[:, c % SPLIT, :], raw[:, c % RAW, :]).then_inc(A["hi_done"], 1)

            loads = [(lr_raw[:, :, :], a_w_in[0, :, GK0:GK0 + RANK].rearrange("(k p) r -> p k r", p=P)),
                     (wgk2, a_w_gk2[0]),
                     (bgk[:, :], a_b_gk2[0].rearrange("(h p) -> p h", p=P)),
                     (onorm, a_o_norm[0].partition_broadcast(P))]
            for l in range(LAYERS):
                loads += [(r_raw[:, l, :, 0:NG], m_w_group[l].rearrange("(k p) n -> p k n", p=P)),
                          (r_raw[:, l, :, NG:NR], m_w_expert[l].rearrange("(k p) n -> p k n", p=P)),
                          (r_bias[:, l, 0:NG], m_b_group[l].partition_broadcast(P)),
                          (r_bias[:, l, NG:NR], m_b_expert[l].partition_broadcast(P))]
            with nc.allow_non_contiguous_dma(reason="512 gate biases and 20 router columns a row"):
                for dst, src in loads:
                    act.dma_start(dst, src).then_inc(A["small_loaded"], 16)

            norms = [0]

            def rsqrt_first(width):
                norms[0] += 1
                act.wait_ge(V["ms_ready"], norms[0])
                se.activation(y1[:, 0:width], ms[:, 0:width], ACT.Ln).then_inc(A["act_chain"], 1)
                act.wait_ge(A["act_chain"], norms[0])
                se.activation(y0[:, 0:width], y1[:, 0:width], ACT.Exp, scale=-0.5).then_inc(A["rs_first"], 1)

            def norm_squares(event):
                for i in range(NT):
                    wait_h(act, event, i)
                    se.activation(psf[:, D * i:D * (i + 1)], h[:, i, :], ACT.Square,
                                  accum_out=ss[:, i:i + 1]).then_inc(A["ssq_done"], 1)
                rsqrt_first(NT)

            def transposed_hi(turn):
                for k in range(KT):
                    act.wait_ge(M["xT_tr"], KT * turn + k + 1)
                    se.copy(xT_hi[:, k, :], ps[:, k % 2, :]).then_inc(A["xT_hi_done"], 1)

            def panel_out(p, last_block, dst, func=ACT.Copy, scale=1.0):
                act.wait_ge(M["blk_used"], last_block + 1)
                se.activation(dst, ps[:, panel_banks(p), :], func, scale=scale).then_inc(A["panel_out"], 1)

            split(0)
            split(1)
            act.wait_ge(A["small_loaded"], 16 * len(loads))
            act.wait_ge(G["consts"], 1)
            se.copy(lr_hi[:, :, 0:RANK], lr_raw[:, :, :]).then_inc(A["lr_hi_done"], 1)
            norm_squares(0)
            transposed_hi(0)
            act.wait_ge(V["gate_abs"], 1)
            se.activation(cum, cum, ACT.Exp, scale=-1.0).then_inc(A["gate_ln"], 1)
            act.wait_ge(A["gate_ln"], 1)
            se.activation(cum, cum, ACT.Ln, bias=1.0).then_inc(A["gate_ln"], 1)
            split(2)
            act.wait_ge(V["gate_cum"], GH)
            se.activation(gate, cum, ACT.Exp, scale=1.0 / GATE_NORM).then_inc(A["gate_exp"], 1)
            se.activation(kinv, cum, ACT.Exp, scale=-1.0 / GATE_NORM).then_inc(A["gate_exp"], 1)
            panel_out(0, 1, qT, scale=DK ** -0.5)
            split(3)
            split(4)
            panel_out(1, 3, kT)
            split(5)
            act.wait_ge(V["gate_toend"], 1)
            se.activation(gate, gate, ACT.Exp, scale=1.0 / GATE_NORM).then_inc(A["gate_exp"], 1)
            split(6)
            panel_out(2, 5, v[:, :, 0:BN])
            split(7)
            split(8)
            panel_out(3, 7, v[:, :, BN:2 * BN])
            split(9)
            act.wait_ge(M["ktok_tr"], 1)
            se.copy(gate, ps[:, 0:4, :]).then_inc(A["ktok_out"], 1)
            for i in range(NT):
                act.wait_ge(M["inter_done"], 2 * i + 1)
                se.copy(xn[:, i, :], psf[:, 2048 + 1024 * (i % 2):3072 + 1024 * (i % 2)]).then_inc(A["o_out"], 1)
            rsqrt_first(NT * GH)
            for p in (4, 5):
                split(2 * p + 2)
                panel_out(p, 2 * p + 1, sg[:, :, (p - 4) * BN:(p - 3) * BN], ACT.Silu)
                split(2 * p + 3)
            transposed_hi(1)
            for n in range(A_BLOCKS - 2, A_BLOCKS + 2):
                split(n)

            def x_hi(S, i):
                for f in (0, 1):
                    act.wait_ge(S["x_tr"], 2 * i + (f + 1))
                    se.copy(xg_hi[:, 4 * f:4 * f + 4, :],
                            ps[:, 4 + f, 0:4 * CAP].rearrange("p (k c) -> p k c", k=4)).then_inc(S["x_hi"], 1)

            def silu(S, i, reuse=True):
                if reuse:
                    act.wait_ge(S["mul"], i)
                se.activation(sil, ps[0:CAP, 0, :], ACT.Silu).then_inc(S["silu"], 1)

            def h_hi(S, i):
                act.wait_ge(S["h_tr"], i + 1)
                se.copy(ht_hi, ps[:, 6, 0:BK * CAP].rearrange("p (k c) -> p k c", k=BK)).then_inc(S["h_hi"], 1)

            def y_out(S, i, reuse=True):
                if reuse:
                    act.wait_ge(S["y_stored"], 16 * i)
                se.copy(y_sb, psf[0:CAP, 1024:2048]).then_inc(S["y_out"], 1)

            def experts(layer):
                B, I = blocks_of(layer), NE * layer
                x_hi(E, I)
                split(B + 2)
                split(B + 3)
                silu(E, I, layer > 0)
                split(B + 4)
                split(B + 5)
                x_hi(E, I + 1)
                h_hi(E, I)

                def step(i, c, g, more):
                    split(c + 2, g)
                    split(c + 3, g)
                    silu(E, i)
                    split(c + 4, g)
                    split(c + 5, g)
                    if more:
                        x_hi(E, i + 1)
                    split(c + 6, g)
                    split(c + 7, g)
                    y_out(E, i - 1, not (isinstance(i, int) and i == 1))
                    h_hi(E, i)

                for k in range(2):
                    step(I + 1 + k, B + 4 + E_BLOCKS * k, 0, True)
                with act.Fori(1, PAIRS) as g:
                    for k in range(2):
                        step(2 * g + (I + 1 + k), B + 4 + E_BLOCKS * k, g, True)
                step(I + NE - 1, B + LAST, 0, False)
                act.wait_ge(M["blk_used"], B + NE * E_BLOCKS)
                y_out(E, I + NE - 1)

                S, W = O[layer], OW[layer]

                def tile(j):
                    e = act.value_load(over[0:1, bass.ds(j, 1)], min_val=0, max_val=NE - 1)
                    x_hi(S, j)
                    for b, (kind, half) in enumerate((k, f) for k in "gud" for f in (0, 1)):
                        if b:
                            act.wait_ge(W["lo"], 6 * j + b)
                        act.dma_start(over_raw.rearrange("p (k n) -> p k n", k=BK),
                                      expert_block(layer, kind, e, half)).then_inc(W["loaded"], 16)
                        act.wait_ge(W["loaded"], 96 * j + 16 * (b + 1))
                        if b >= SPLIT:
                            act.wait_ge(W["used"], 6 * j + (b - SPLIT + 1))
                        se.copy(w_hi[:, b % SPLIT, :], over_raw).then_inc(W["hi"], 1)
                        if b == 3:
                            silu(S, j, False)
                            h_hi(S, j)
                    act.wait_ge(W["used"], 6 * j + 6)
                    y_out(S, j, False)
                    act.wait_ge(S["y_stored"], 16 * j + 16)
                    se.copy(y1[:, 0:1], ms[:, 0:1])

                over_loop(act, layer, tile)

            def router(layer):
                se.copy(r_hi[:, :, :], r_raw[:, layer, :, :]).then_inc(A["r_hi_done"], 1)
                act.wait_ge(V["group_diff"], layer + 1)
                se.activation(G4["gd"], G4["gd"], ACT.Exp).then_inc(A["group_exp"], 1)
                act.wait_ge(V["second_diff"], layer + 1)
                se.activation(V4["ex"], V4["dd"], ACT.Exp).then_inc(A["second_exp"], 1)

            norm_squares(1)
            transposed_hi(2)
            router(0)
            experts(0)

            B = L_BLOCKS
            split(B)
            split(B + 1)
            norm_squares(2)
            transposed_hi(3)
            for q, dst in enumerate((kT1[:, 0:4, :], kT1[:, 4:8, :], v[:, :, 0:BN], v[:, :, BN:2 * BN])):
                split(B + 2 * q + 2)
                panel_out(8 + q, B + 2 * q + 1, dst)
                split(B + 2 * q + 3)
            transposed_hi(4)
            for q in (4, 5):
                split(B + 2 * q + 2)
                panel_out(8 + q, B + 2 * q + 1, qT1[:, 4 * (q - 4):4 * (q - 3), :], scale=SD ** -0.5)
                split(B + 2 * q + 3)

            def log_terms(hd, r, first=False):
                act.wait_ge(V["z_abs"], hd + 1)
                se.activation(zt[r], zt[r], ACT.Exp, scale=-1.0).then_inc(A["z_exp"], 1)
                act.wait_ge(A["z_exp"], hd + 1)
                se.activation(zt[r], zt[r], ACT.Ln, bias=1.0).then_inc(A["z_ln"], 1)
                act.wait_ge(V["L_done"], hd + 1)
                if not first:
                    act.wait_ge(M["sums_done"], hd)
                se.copy(s_hi[:, 0:ZC], zt[r]).then_inc(A["L_hi_done"], 1)

            def weights(hd, r):
                act.wait_ge(M["sums_done"], hd + 1)
                se.activation(zt[r], psf[:, 1536 * r:1536 * r + ZC], ACT.Exp).then_inc(A["weights_done"], 1)

            def oT_hi(q, b):
                act.wait_ge(M["av_done"], 2 * q + 2)
                se.copy(xT_hi[:, bass.ds(q, 1), :].rearrange("p o t -> p (o t)"), ps[:, 6 + b, :]).then_inc(A["oT_hi_done"], 1)

            log_terms(0, 0, True)
            log_terms(1, 1)

            def heads(g):
                for r in range(4):
                    weights(4 * g + r, r % 2)
                    log_terms(4 * g + (r + 2), r % 2)
                    if r % 2:
                        oT_hi(2 * g + r // 2, r // 2)

            heads(0)
            with act.Fori(1, 3) as g:
                heads(g)
            for hd in (12, 13):
                weights(hd, hd % 2)
                log_terms(hd + 2, hd % 2)
            oT_hi(6, 0)
            weights(14, 0)
            weights(15, 1)
            oT_hi(7, 1)
            for n in range(A_BLOCKS - 2, A_BLOCKS + 2):
                split(B + n)
            norm_squares(3)
            transposed_hi(5)
            router(1)
            experts(1)
            norm_squares(4)

        @block.vector
        def _(dve):
            link = Chain(dve, V["dve_chain"])

            def split(c, g=0):
                dve.wait_ge(A["hi_done"], number(c + 1, g))
                ve.tensor_tensor(w_lo[:, c % SPLIT, :], raw[:, c % RAW, :], w_hi[:, c % SPLIT, :],
                                 ALU.subtract).then_inc(V["lo_done"], 1)

            norms = [0]

            def refine(width):
                norms[0] += 1
                dve.wait_ge(A["rs_first"], norms[0])
                a, b, m, o = (t[:, 0:width] for t in (y0, y1, ms, rstd))
                link(ve.tensor_tensor(b, a, a, ALU.mult))
                link(ve.tensor_tensor(b, b, m, ALU.mult))
                link(ve.tensor_scalar(b, b, -0.5, 1.5, ALU.mult, ALU.add))
                link(ve.tensor_tensor(o, a, b, ALU.mult))

            def norm_scale(event):
                dve.wait_ge(A["ssq_done"], NT * (event + 1))
                ve.tensor_scalar(ms[:, 0:NT], ss[:, 0:NT], 1.0 / D, EPS, ALU.mult, ALU.add).then_inc(V["ms_ready"], 1)
                refine(NT)

            def normed(use):
                dve.wait_ge(G["gain_loaded"], 16 * (use + 1))
                for i in range(NT):
                    ve.scalar_tensor_tensor(xn[:, i, :], h[:, i, :], rstd[:, i:i + 1], gain[:, :],
                                            ALU.mult, ALU.mult).then_inc(V["xn_ready"], 1)

            def transposed_lo(turn):
                for k in range(KT):
                    dve.wait_ge(A["xT_hi_done"], KT * turn + k + 1)
                    ve.tensor_tensor(xT_lo[:, k, :], ps[:, k % 2, :], xT_hi[:, k, :],
                                     ALU.subtract).then_inc(V["xT_lo_done"], 1)

            def add_panel(p, last_block, half):
                dve.wait_ge(M["blk_used"], last_block + 1)
                for i in range(NT):
                    d = h[:, i, half * BN:(half + 1) * BN]
                    ins = ve.tensor_tensor(d, d, ps[:, 4 * (p % 2) + i, :], ALU.add)
                    if half:
                        ins.then_inc(V["h_added"], 1)

            split(0)
            split(1)
            dve.wait_ge(A["lr_hi_done"], 1)
            ve.tensor_tensor(lr_lo[:, :, 0:RANK], lr_raw[:, :, :], lr_hi[:, :, 0:RANK], ALU.subtract).then_inc(V["lr_lo_done"], 1)
            norm_scale(0)
            normed(0)
            transposed_lo(0)
            dve.wait_ge(M["lr_done"], 1)
            ve.tensor_copy(lrT, ps[0:RANK, 2, :]).then_inc(V["lr_out"], 1)
            dve.wait_ge(M["gates_done"], 1)
            for i in range(GH):
                ve.tensor_scalar(gate[:, i, :], ps[:, 4 + i, :], bgk[:, i:i + 1], None, ALU.add).then_inc(V["gates_in"], 1)
            dve.wait_ge(V["gates_in"], GH)
            ve.scalar_tensor_tensor(cum, gate, -1.0, gate, ALU.mult, ALU.max).then_inc(V["gate_abs"], 1)
            dve.wait_ge(A["gate_ln"], 2)
            link(ve.scalar_tensor_tensor(gate, gate, 0.0, cum, ALU.min, ALU.subtract))
            dve.wait_ge(G["consts"], N_CONSTS)
            for i in range(GH):
                ve.tensor_tensor_scan(cum[:, i, :], reset, gate[:, i, :], 0.0, ALU.mult, ALU.add).then_inc(V["gate_cum"], 1)
            split(2)
            dve.wait_ge(A["gate_exp"], 1)
            dve.wait_ge(A["panel_out"], 1)
            ve.tensor_tensor(qT, qT, gate, ALU.mult).then_inc(V["q_dec"], 1)
            by_chunk = "p h (c t) -> p (h c) t"
            gate_c, cum_c = gate.rearrange(by_chunk, t=CHUNK), cum.rearrange(by_chunk, t=CHUNK)
            link(ve.tensor_copy(decay[:, :, :].rearrange("p h c -> p (h c)").unsqueeze(2), gate_c[:, :, CHUNK - 1:CHUNK]))
            ve.tensor_tensor(gate_c, cum_c[:, :, CHUNK - 1:CHUNK].broadcast_to([P, GH * NCH, CHUNK]), cum_c,
                             ALU.subtract).then_inc(V["gate_toend"], 1)
            split(3)
            split(4)
            dve.wait_ge(A["gate_exp"], 2)
            dve.wait_ge(A["panel_out"], 2)
            ve.tensor_tensor(kinv, kT, kinv, ALU.mult).then_inc(V["k_inv"], 1)
            split(5)
            dve.wait_ge(A["gate_exp"], 3)
            ve.tensor_tensor(kT, kT, gate, ALU.mult).then_inc(V["k_toend"], 1)
            for n in range(6, 10):
                split(n)
            dve.wait_ge(M["att_done"], 1)
            ve.tensor_copy(kT, ps[:, 4:8, :]).then_inc(V["att_out"], 1)
            for c in range(NCH - 1):
                dve.wait_ge(M["upd_done"], c + 1)
                if c >= 2:
                    dve.wait_ge(M["inter_done"], c - 1)
                u = psf[:, 1024 * (c % 2):1024 * (c % 2) + 1024].rearrange("p (h e) -> p h e", h=GH)
                s0, s1 = state[:, c % 2], state[:, (c + 1) % 2]
                if c == 0:
                    ve.tensor_copy(s1, u).then_inc(V["state_done"], GH)
                else:
                    dve.wait_ge(V["state_done"], GH * c)
                    for i in range(GH):
                        ve.scalar_tensor_tensor(s1[:, i, :], s0[:, i, :], decay[:, i, c:c + 1], u[:, i, :],
                                                ALU.mult, ALU.add).then_inc(V["state_done"], 1)
            o_sq = kinv[:, 0:2, :].rearrange("p a t -> p (a t)")
            for i in range(NT):
                dve.wait_ge(A["o_out"], i + 1)
                link(ve.tensor_tensor(o_sq, xn[:, i, :], xn[:, i, :], ALU.mult))
                link(ve.tensor_reduce(ss[:, GH * i:GH * i + GH], o_sq.rearrange("p (h e) -> p h e", h=GH), AX.X, ALU.add))
            ve.tensor_scalar(ms[:, 0:NT * GH], ss[:, 0:NT * GH], 1.0 / DV, EPS, ALU.mult, ALU.add).then_inc(V["ms_ready"], 1)
            refine(NT * GH)
            for n in range(10, 14):
                split(n)
            dve.wait_ge(G["sg_ready"], 1)
            for i in range(NT):
                for j in range(GH):
                    o = xn[:, i, DV * j:DV * (j + 1)]
                    ins = ve.scalar_tensor_tensor(o, o, rstd[:, GH * i + j:GH * i + j + 1],
                                                  sg[:, i, DV * j:DV * (j + 1)], ALU.mult, ALU.mult)
                ins.then_inc(V["og_ready"], 1)
            transposed_lo(1)
            split(14)
            add_panel(6, 13, 0)
            split(15)
            split(16)
            add_panel(7, 15, 1)
            split(17)

            def x_lo(S, i):
                for f in (0, 1):
                    dve.wait_ge(S["x_hi"], 2 * i + (f + 1))
                    ve.tensor_tensor(xg_lo[:, 4 * f:4 * f + 4, :],
                                     ps[:, 4 + f, 0:4 * CAP].rearrange("p (k c) -> p k c", k=4),
                                     xg_hi[:, 4 * f:4 * f + 4, :], ALU.subtract).then_inc(S["x_lo"], 1)

            def mul(S, i, reuse=True):
                dve.wait_ge(S["silu"], i + 1)
                if reuse:
                    dve.wait_ge(S["h_tr"], i)
                ve.tensor_tensor(hid, sil, ps[0:CAP, 1, :], ALU.mult).then_inc(S["mul"], 1)

            def h_lo(S, i):
                dve.wait_ge(S["h_hi"], i + 1)
                ve.tensor_tensor(ht_lo, ps[:, 6, 0:BK * CAP].rearrange("p (k c) -> p k c", k=BK), ht_hi,
                                 ALU.subtract).then_inc(S["h_lo"], 1)

            def experts(layer):
                B, I = blocks_of(layer), NE * layer
                x_lo(E, I)
                for n in range(2, 6):
                    split(B + n)
                dve.wait_ge(M["blk_used"], B + 4)
                mul(E, I, layer > 0)
                x_lo(E, I + 1)
                h_lo(E, I)

                def step(i, c, g, more):
                    for n in range(2, 6):
                        split(c + n, g)
                    mul(E, i)
                    if more:
                        x_lo(E, i + 1)
                    split(c + 6, g)
                    split(c + 7, g)
                    h_lo(E, i)

                with dve.Fori(0, PAIRS) as g:
                    for k in range(2):
                        step(2 * g + (I + 1 + k), B + 4 + E_BLOCKS * k, g, True)
                step(I + NE - 1, B + LAST, 0, False)

                S, W = O[layer], OW[layer]

                def tile(j):
                    x_lo(S, j)
                    for b in range(6):
                        dve.wait_ge(W["hi"], 6 * j + (b + 1))
                        ve.tensor_tensor(w_lo[:, b % SPLIT, :], over_raw, w_hi[:, b % SPLIT, :],
                                         ALU.subtract).then_inc(W["lo"], 1)
                        if b == 3:
                            dve.wait_ge(W["used"], 6 * j + 4)
                            mul(S, j, False)
                            h_lo(S, j)
                    dve.wait_ge(S["y_stored"], 16 * j + 16)
                    ve.tensor_copy(y0[:, 0:1], ss[:, 0:1])

                over_loop(dve, layer, tile)

            def over4(a, n):
                return a.unsqueeze(2).broadcast_to([P, NT, n])

            def per_expert(a):
                return a.unsqueeze(1).broadcast_to([P, NT, NE])

            def router(layer):
                dve.wait_ge(A["r_hi_done"], layer + 1)
                ve.tensor_tensor(r_lo[:, :, :], r_raw[:, layer, :, :], r_hi[:, :, :], ALU.subtract).then_inc(V["r_lo_done"], 1)
                tt, ts, red, stt = ve.tensor_tensor, ve.tensor_scalar, ve.tensor_reduce, ve.scalar_tensor_tensor
                dve.wait_ge(M["logits_done"], layer + 1)
                link(tt(lg, ps[:, 7, 0:NT * NR].rearrange("p (i e) -> p i e", i=NT),
                        r_bias[:, layer, :].unsqueeze(1).broadcast_to([P, NT, NR]), ALU.add))
                lgg = lg[:, :, 0:NG]
                link(red(V4["gm"], lgg, AX.X, ALU.max))
                tt(G4["gd"], lgg, over4(V4["gm"], NG), ALU.subtract).then_inc(V["group_diff"], 1)
                link(tt(G4["geq"], lgg, over4(V4["gm"], NG), ALU.is_equal))
                link(tt(G4["gv"], G4["geq"], desc4[:, :].unsqueeze(1).broadcast_to([P, NT, NG]), ALU.mult))
                link(red(V4["gvm"], G4["gv"], AX.X, ALU.max))
                link(tt(G4["goh"], G4["gv"], over4(V4["gvm"], NG), ALU.is_equal))
                link(ts(G4["gneg"], G4["goh"], 1e30, -1e30, ALU.mult, ALU.add))
                for i in range(NT):
                    em = R["em"][:, i, :].rearrange("p (g e) -> p g e", g=NG)
                    oh, neg = (G4[n][:, i, :].unsqueeze(2).broadcast_to([P, NG, EG]) for n in ("goh", "gneg"))
                    link(tt(em, lg[:, i, NG:NR].rearrange("p (g e) -> p g e", g=NG), oh, ALU.mult))
                    link(tt(em, em, neg, ALU.add))

                def first_max(src, m, oh):
                    link(red(m, src, AX.X, ALU.max))
                    link(tt(R["eq"], src, over4(m, NE), ALU.is_equal))
                    link(tt(R["ev"], R["eq"], per_expert(desc16[:, :]), ALU.mult))
                    link(red(V4["evm"], R["ev"], AX.X, ALU.max))
                    link(tt(oh, R["ev"], over4(V4["evm"], NE), ALU.is_equal))

                first_max(R["em"], V4["m1"], R["oh1"])
                link(stt(R["em2"], R["oh1"], -2e30, R["em"], ALU.mult, ALU.add))
                first_max(R["em2"], V4["m2"], R["oh2"])
                tt(V4["dd"], V4["m2"], V4["m1"], ALU.subtract).then_inc(V["second_diff"], 1)
                tt(sel_b[:, :, :], R["oh1"], R["oh2"], ALU.add).then_inc(V["sel_ready"], 1)
                dve.wait_ge(A["group_exp"], layer + 1)
                link(red(V4["gs"], G4["gd"], AX.X, ALU.add))
                link(ve.reciprocal(V4["gw"], V4["gs"]))
                dve.wait_ge(A["second_exp"], layer + 1)
                link(ts(V4["s1"], V4["ex"], 1.0, None, ALU.add))
                link(ve.reciprocal(V4["rs"], V4["s1"]))
                link(tt(w12[:, 0, :], V4["rs"], V4["gw"], ALU.mult))
                link(tt(w12[:, 1, :], w12[:, 0, :], V4["ex"], ALU.mult))
                dve.wait_ge(M["ranks_done"], layer + 1)
                link(ve.tensor_copy(E16["cnt"], ps[:, 6, NT * NE:(NT + 1) * NE]))
                link(ve.tensor_copy(R["rank"], ps[:, 6, 0:NT * NE].rearrange("p (i e) -> p i e", i=NT)))
                link(ts(E16["ovn"], E16["cnt"], float(CAP), None, ALU.is_gt))
                for k in range(2, STEPS_OVER + 1):
                    link(stt(E16["ovn"], E16["cnt"], float(k * CAP), E16["ovn"], ALU.is_gt, ALU.add))
                link(ve.tensor_tensor_scan(E16["ovend"], one16[:, :], E16["ovn"], 0.0, ALU.mult, ALU.add))
                link(tt(E16["ovbase"], E16["ovend"], E16["ovn"], ALU.subtract))
                link(stt(E16["delta"], E16["ovbase"], float(CAP), over_row[:, :], ALU.mult, ALU.add))
                link(ts(R["tmp"], R["rank"], float(CAP), None, ALU.is_ge))
                link(tt(R["tmp"], R["tmp"], per_expert(E16["delta"]), ALU.mult))
                link(tt(R["posn"], R["rank"], per_expert(first_row[:, :]), ALU.add))
                link(tt(R["posn"], R["posn"], R["tmp"], ALU.add))
                for n, oh in enumerate((R["oh1"], R["oh2"])):
                    link(tt(R["tmp"], oh, R["posn"], ALU.mult))
                    link(red(V4["p1"], R["tmp"], AX.X, ALU.add))
                    link(ve.tensor_copy(pos[:, n, :], V4["p1"]))
                link(tt(over_cmp, E16["ovend"].unsqueeze(1).broadcast_to([P, MAX_OVER, NE]),
                        j_idx[:, :].unsqueeze(2).broadcast_to([P, MAX_OVER, NE]), ALU.is_le))
                link(red(over_f[:, 0:MAX_OVER], over_cmp, AX.X, ALU.add))
                link(ts(over_f[:, 0:MAX_OVER], over_f[:, 0:MAX_OVER], float(NE - 1), None, ALU.min))
                link(ve.tensor_copy(over_f[:, MAX_OVER:MAX_OVER + 1], E16["ovend"][:, NE - 1:NE]))
                ve.tensor_copy(over[:, :], over_f[0:1, :]).then_inc(V["pos_ready"], 1)

            def combine(layer):
                for i in range(NT):
                    for k in range(2):
                        n = 2 * i + k
                        dve.wait_ge(gathered[n % 4], 16 * (2 * layer + n // 4 + 1))
                        if k:
                            dve.wait_ge(V["combined"], 2 * NT * layer + n)
                        ve.scalar_tensor_tensor(h[:, i, :], xn[:, n % 4, :], w12[:, k, i:i + 1], h[:, i, :],
                                                ALU.mult, ALU.add).then_inc(V["combined"], 1)

            norm_scale(1)
            normed(1)
            transposed_lo(2)
            router(0)
            experts(0)

            B = L_BLOCKS
            split(B)
            split(B + 1)
            combine(0)
            norm_scale(2)
            normed(2)
            transposed_lo(3)
            for n in range(2, 10):
                split(B + n)
            normed(3)
            transposed_lo(4)
            for n in range(10, 14):
                split(B + n)

            def log_terms(hd, r, reuse=True):
                z = psf[:, 1536 * r:1536 * r + ZC]
                dve.wait_ge(M["z_done"], hd + 1)
                if reuse:
                    dve.wait_ge(M["av_done"], hd - 1)
                ve.tensor_scalar(zt[r].bitcast(I32), z.bitcast(I32), 0x7FFFFFFF, None,
                                 ALU.bitwise_and).then_inc(V["z_abs"], 1)
                dve.wait_ge(A["z_ln"], hd + 1)
                ve.scalar_tensor_tensor(zt[r], z, 0.0, zt[r], ALU.max, ALU.add).then_inc(V["L_done"], 1)
                dve.wait_ge(A["L_hi_done"], hd + 1)
                ve.tensor_tensor(s_lo[:, 0:ZC], zt[r], s_hi[:, 0:ZC], ALU.subtract).then_inc(V["L_lo_done"], 1)

            def oT_lo(q, b):
                dve.wait_ge(A["oT_hi_done"], q + 1)
                hi, lo = (t[:, bass.ds(q, 1), :].rearrange("p o t -> p (o t)") for t in (xT_hi, xT_lo))
                ve.tensor_tensor(lo, ps[:, 6 + b, :], hi, ALU.subtract).then_inc(V["oT_lo_done"], 1)

            log_terms(0, 0, False)
            log_terms(1, 1, False)

            def heads(g):
                for r in range(4):
                    log_terms(4 * g + (r + 2), r % 2)
                    if r % 2:
                        oT_lo(2 * g + r // 2, r // 2)

            heads(0)
            with dve.Fori(1, 3) as g:
                heads(g)
            for hd in (12, 13):
                log_terms(hd + 2, hd % 2)
            oT_lo(6, 0)
            oT_lo(7, 1)
            split(B + 14)
            add_panel(14, B + 13, 0)
            split(B + 15)
            split(B + 16)
            add_panel(15, B + 15, 1)
            split(B + 17)
            norm_scale(3)
            normed(4)
            transposed_lo(5)
            router(1)
            experts(1)
            combine(1)
            norm_scale(4)
            normed(5)

        @block.tensor
        def _(pe):
            def three(o, a_hi, a_lo, b_hi, b_lo, start, stop):
                te.matmul(o, a_hi, b_hi, start=start, stop=False)
                te.matmul(o, a_hi, b_lo, start=False, stop=False)
                return te.matmul(o, a_lo, b_hi, start=False, stop=stop)

            def transposed(turn, ready):
                ready()
                for k in range(KT):
                    if k >= 2:
                        pe.wait_ge(V["xT_lo_done"], KT * turn + k - 1)
                    for i in range(NT):
                        ins = te.transpose(ps[:, k % 2, P * i:P * (i + 1)], xn[:, i, P * k:P * (k + 1)], ident[:, :])
                    ins.then_inc(M["xT_tr"], 1)
                pe.wait_ge(V["xT_lo_done"], KT * (turn + 1))

            def dense(p, c, feature_major):
                for n in (0, 1):
                    pe.wait_ge(V["lo_done"], c + n + 1)
                    for kk in range(BK):
                        k = BK * n + kk
                        for j in range(4):
                            part = slice(P * j, P * (j + 1))
                            wide = slice(BN * kk, BN * (kk + 1))
                            cols = slice(BN * kk + P * j, BN * kk + P * (j + 1))
                            o = ps[:, 4 * (p % 2) + j, :]
                            s = (c + n) % SPLIT
                            if feature_major:
                                ops = w_hi[:, s, cols], w_lo[:, s, cols], xT_hi[:, k, :], xT_lo[:, k, :]
                            else:
                                ops = xT_hi[:, k, part], xT_lo[:, k, part], w_hi[:, s, wide], w_lo[:, s, wide]
                            ins = three(o, *ops, start=k == 0, stop=k == KT - 1)
                    ins.then_inc(M["blk_used"], 1)

            pe.wait_ge(G["consts"], N_CONSTS)
            transposed(0, lambda: pe.wait_ge(V["xn_ready"], NT))
            pe.wait_ge(V["lr_lo_done"], 1)
            for k in range(KT):
                ins = three(ps[:, 2, :], lr_hi[:, k, :], lr_lo[:, k, :], xT_hi[:, k, :], xT_lo[:, k, :],
                            start=k == 0, stop=k == KT - 1)
            ins.then_inc(M["lr_done"], 1)
            pe.wait_ge(V["lr_out"], 1)
            for i in range(GH):
                ins = te.matmul(ps[:, 4 + i, :], wgk2[:, DK * i:DK * (i + 1)], lrT, start=True, stop=True)
            ins.then_inc(M["gates_done"], 1)
            dense(0, 0, True)
            pe.wait_ge(V["gates_in"], GH)
            dense(1, 2, True)
            pe.wait_ge(A["panel_out"], 1)
            dense(2, 4, False)
            pe.wait_ge(A["panel_out"], 2)
            dense(3, 6, False)
            pe.wait_ge(V["k_toend"], 1)
            pe.wait_ge(A["panel_out"], 3)
            for i in range(NT):
                for j in range(GH):
                    ins = te.transpose(ps[:, i, P * j:P * (j + 1)], kT[:, j, P * i:P * (i + 1)], ident[:, :])
            ins.then_inc(M["ktok_tr"], 1)
            pe.wait_ge(V["k_inv"], 1)
            pe.wait_ge(A["panel_out"], 4)
            for i in range(NT):
                for j in range(GH):
                    t = slice(P * i, P * (i + 1))
                    ins = te.matmul(ps[:, 4 + i, P * j:P * (j + 1)], kinv[:, j, t], qT[:, j, t], start=True, stop=True)
            ins.then_inc(M["att_done"], 1)
            ktok = gate
            att = kT
            pe.wait_ge(A["ktok_out"], 1)
            for i in range(NT):
                for c in (2 * i, 2 * i + 1):
                    if c == NCH - 1:
                        continue
                    if c >= 2:
                        pe.wait_ge(V["state_done"], GH * (c - 1))
                    rows = slice(CHUNK * (c % 2), CHUNK * (c % 2 + 1))
                    for j in range(GH):
                        a = 1024 * (c % 2) + DV * j
                        ins = te.matmul(psf[:, a:a + DV], ktok[rows, i, DK * j:DK * (j + 1)],
                                        v[rows, i, DV * j:DV * (j + 1)], start=True, stop=True)
                    ins.then_inc(M["upd_done"], 1)
                if i == 0:
                    pe.wait_ge(G["masked"], 2)
                if i >= 2:
                    pe.wait_ge(A["o_out"], i - 1)
                o0 = 2048 + 1024 * (i % 2)
                for j in range(GH):
                    te.matmul(psf[:, o0 + DV * j:o0 + DV * (j + 1)], att[:, i, P * j:P * (j + 1)],
                              v[:, i, DV * j:DV * (j + 1)], start=j % 2 == 0, stop=True, skip_group_check=True)
                for c in (2 * i, 2 * i + 1):
                    if c == 0:
                        continue
                    pe.wait_ge(V["state_done"], GH * c)
                    rows = slice(CHUNK * (c % 2), CHUNK * (c % 2 + 1))
                    for j in range(GH):
                        ins = te.matmul(psf[rows, o0 + DV * j:o0 + DV * (j + 1)],
                                        qT[:, j, CHUNK * c:CHUNK * (c + 1)], state[:, c % 2, j, :],
                                        start=False, stop=True, skip_group_check=True)
                    ins.then_inc(M["inter_done"], 1)
            dense(4, 8, False)
            pe.wait_ge(A["o_out"], NT)
            dense(5, 10, False)
            transposed(1, lambda: pe.wait_ge(V["og_ready"], NT))
            dense(6, 12, False)
            dense(7, 14, False)

            def x_transposed(S, i, slot, loads, reuse=True):
                pe.wait_ge((S["x_loaded0"], S["x_loaded1"])[slot], 16 * loads)
                for f in (0, 1):
                    if reuse:
                        pe.wait_ge(S["x_lo"], 2 * i + (f - 1))
                    for k in range(4):
                        ins = te.transpose(ps[:, 4 + f, CAP * k:CAP * (k + 1)],
                                           xg[:, slot, P * (4 * f + k):P * (4 * f + k + 1)], ident[0:CAP, 0:CAP])
                    ins.then_inc(S["x_tr"], 1)

            def up_block(which, half, slot, used):
                for kk in range(BK):
                    k = BK * half + kk
                    wide = slice(BN * kk, BN * (kk + 1))
                    ins = three(ps[0:CAP, which, :], xg_hi[:, k, :], xg_lo[:, k, :], w_hi[:, slot, wide],
                                w_lo[:, slot, wide], start=k == 0, stop=k == KT - 1)
                ins.then_inc(used, 1)

            def down_block(half, slot, used):
                for kk in range(BK):
                    wide = slice(BN * kk, BN * (kk + 1))
                    ins = three(ps[0:CAP, 2 + half, :], ht_hi[:, kk, :], ht_lo[:, kk, :], w_hi[:, slot, wide],
                                w_lo[:, slot, wide], start=kk == 0, stop=kk == BK - 1)
                ins.then_inc(used, 1)

            def h_transposed(S, i, reuse=True):
                pe.wait_ge(S["mul"], i + 1)
                if reuse:
                    pe.wait_ge(S["h_lo"], i)
                for k in range(BK):
                    ins = te.transpose(ps[:, 6, CAP * k:CAP * (k + 1)], hid[:, P * k:P * (k + 1)], ident[0:CAP, 0:CAP])
                ins.then_inc(S["h_tr"], 1)

            def experts(layer):
                B, I = blocks_of(layer), NE * layer
                first_load = 8 * layer + 1

                def up(i, c, g=0, reuse=True):
                    pe.wait_ge(E["x_lo"], 2 * i + 2)
                    for n in range(4):
                        if n == 0 and reuse:
                            pe.wait_ge(E["silu"], i)
                        if n == 2 and reuse:
                            pe.wait_ge(E["mul"], i)
                        pe.wait_ge(V["lo_done"], number(c + n + 1, g))
                        up_block(n // 2, n % 2, (c + n) % SPLIT, M["blk_used"])

                def down(i, c, g=0):
                    pe.wait_ge(E["h_lo"], i + 1)
                    for n in range(2):
                        pe.wait_ge(V["lo_done"], number(c + n + 1, g))
                        down_block(n, (c + n) % SPLIT, M["blk_used"])

                x_transposed(E, I, 0, first_load, layer > 0)
                up(I, B, 0, layer > 0)
                x_transposed(E, I + 1, 1, first_load)
                h_transposed(E, I, layer > 0)
                with pe.Fori(0, PAIRS) as g:
                    for k in range(2):
                        i, c = 2 * g + (I + 1 + k), B + 4 + E_BLOCKS * k
                        up(i, c, g)
                        x_transposed(E, i + 1, k, g + (first_load + 1))
                        down(i - 1, c + 4, g)
                        h_transposed(E, i)
                i, c = I + NE - 1, B + LAST
                up(i, c)
                down(i - 1, c + 4)
                h_transposed(E, i)
                down(i, c + 6)

                S, W = O[layer], OW[layer]

                def tile(j):
                    pe.wait_ge(E["y_out"], NE * (layer + 1))
                    x_transposed(S, j, 0, j + 1, False)
                    pe.wait_ge(S["x_lo"], 2 * j + 2)
                    for b in range(6):
                        pe.wait_ge(W["lo"], 6 * j + (b + 1))
                        if b == 4:
                            pe.wait_ge(S["h_lo"], j + 1)
                        if b < 4:
                            up_block(b // 2, b % 2, b % SPLIT, W["used"])
                        else:
                            down_block(b - 4, b % SPLIT, W["used"])
                        if b == 3:
                            h_transposed(S, j, False)
                    pe.wait_ge(S["y_stored"], 16 * j + 16)

                over_loop(pe, layer, tile)

            def router(layer):
                pe.wait_ge(V["r_lo_done"], layer + 1)
                for i in range(NT):
                    t = slice(P * i, P * (i + 1))
                    for k in range(KT):
                        ins = three(ps[:, 7, NR * i:NR * (i + 1)], xT_hi[:, k, t], xT_lo[:, k, t],
                                    r_hi[:, k, :], r_lo[:, k, :], start=k == 0, stop=k == KT - 1)
                ins.then_inc(M["logits_done"], 1)
                pe.wait_ge(V["sel_ready"], layer + 1)
                for i in range(NT):
                    o = ps[:, 6, NE * i:NE * (i + 1)]
                    for j in range(i):
                        te.matmul(o, ones_b[:, :], sel_b[:, j, :], start=j == 0, stop=False)
                    te.matmul(o, before[:, :], sel_b[:, i, :], start=i == 0, stop=True)
                o = ps[:, 6, NE * NT:NE * (NT + 1)]
                for j in range(NT):
                    ins = te.matmul(o, ones_b[:, :], sel_b[:, j, :], start=j == 0, stop=j == NT - 1)
                ins.then_inc(M["ranks_done"], 1)

            transposed(2, lambda: pe.wait_ge(V["xn_ready"], 2 * NT))
            router(0)
            experts(0)

            B = L_BLOCKS
            transposed(3, lambda: pe.wait_ge(V["xn_ready"], 3 * NT))
            dense(8, B, True)
            dense(9, B + 2, True)
            pe.wait_ge(A["panel_out"], 7)
            dense(10, B + 4, False)
            pe.wait_ge(A["panel_out"], 8)
            dense(11, B + 6, False)
            pe.wait_ge(A["panel_out"], 9)
            transposed(4, lambda: pe.wait_ge(V["xn_ready"], 4 * NT))
            dense(12, B + 8, True)
            pe.wait_ge(A["panel_out"], 10)
            dense(13, B + 10, True)

            def scores(hd, r, b, pair, reuse=True):
                if reuse:
                    pe.wait_ge(A["weights_done"], hd - 1)
                pe.wait_ge(G["staged"], 3 * pair + 3)
                rows = slice(SD * r, SD * (r + 1))
                for i in (0, 1, 3, 2):
                    z = psf[:, 1536 * r + ZO[i]:1536 * r + ZO[i] + ZW[i]]
                    te.matmul(z, kst[rows, b, P * i:P * (i + 1)], qst[rows, b, P * i:T], start=i != 3, stop=True,
                              skip_group_check=True)
                for i in range(NT):
                    z = psf[:, 1536 * r + ZO[i]:1536 * r + ZO[i] + P]
                    ins = te.matmul(z, ident_b[:, :], neg_mask[:, :], start=False, stop=True, skip_group_check=True)
                ins.then_inc(M["z_done"], 1)

            def sums(hd, r):
                pe.wait_ge(V["L_lo_done"], hd + 1)
                for i in range(NT):
                    for j in range(i, NT):
                        o = psf[:, 1536 * r + ZO[i] + P * (j - i):1536 * r + ZO[i] + ZW[i]]
                        for part in (s_hi, s_lo):
                            ins = te.matmul(o, (neg_tri if i == j else neg_one)[:, :], part[:, ZO[j]:ZO[j] + ZW[j]],
                                            start=False, stop=True, skip_group_check=True)
                ins.then_inc(M["sums_done"], 1)

            def values(hd, r, b, pair, reuse=True):
                pe.wait_ge(A["weights_done"], hd + 1)
                if reuse:
                    pe.wait_ge(V["oT_lo_done"], pair - 1)
                rows = slice(SD * r, SD * (r + 1))
                for j in range(NT):
                    ins = te.matmul(ps[rows, 6 + b, P * j:T], vst[:, b, j, SD * r:SD * (r + 1)],
                                    zt[r][:, ZO[j]:ZO[j] + ZW[j]], start=j == 0, stop=j == NT - 1,
                                    skip_group_check=True)
                ins.then_inc(M["av_done"], 1)

            scores(0, 0, 0, 0, False)
            scores(1, 1, 0, 0, False)
            sums(0, 0)

            def heads(g, first=False):
                for r in range(4):
                    hd = 4 * g + r
                    values(hd, r % 2, r // 2, 2 * g + r // 2, not first)
                    scores(hd + 2, r % 2, (r // 2 + 1) % 2, 2 * g + (r // 2 + 1))
                    sums(hd + 1, (r + 1) % 2)

            heads(0, True)
            with pe.Fori(1, 3) as g:
                heads(g)
            for hd in (12, 13):
                values(hd, hd % 2, 0, 6)
                scores(hd + 2, hd % 2, 1, 7)
                sums(hd + 1, (hd + 1) % 2)
            values(14, 0, 1, 7)
            sums(15, 1)
            values(15, 1, 1, 7)
            pe.wait_ge(V["oT_lo_done"], 8)
            dense(14, B + 12, False)
            dense(15, B + 14, False)
            transposed(5, lambda: pe.wait_ge(V["xn_ready"], 5 * NT))
            router(1)
            experts(1)

        @block.gpsimd
        def _(pool):
            link = Chain(pool, G["pool_chain"])
            gains = [a_norm[0], m_norm[0], kv_norm, b_norm[0], m_norm[1], final_norm]

            def load_gain(use):
                if use:
                    pool.wait_ge(V["xn_ready"], NT * use)
                pool.dma_start(gain[:, :], gains[use].partition_broadcast(P)).then_inc(G["gain_loaded"], 16)

            def hold(sem_, value):
                pool.wait_ge(sem_, value)
                ge.tensor_tensor(zeros[:, 0:1], zeros[:, 1:2], zeros[:, 2:3], ALU.add)

            load_gain(0)
            ge.memset(s_hi[:, :].bitcast(F32), 0.0)
            link(ge.memset(s_lo[:, :].bitcast(F32), 0.0))
            ge.memset(zeros[:, :], 0.0).then_inc(G["consts"], 1)

            def select(dst, src, op, fill, step, channel, base=0):
                return ge.affine_select(out=dst, in_=src, compare_op=op, fill=fill, base=base,
                                        pattern=[[step, dst.shape[-1]]], channel_multiplier=channel)

            for t, val in ((ident, 0.0), (ident_b, 0.0), (neg_mask, 0.0), (before, 1.0), (ones_b, 1.0), (one16, 1.0)):
                ge.memset(t[:, :], val)
            ge.memset(neg_tri[:, :].bitcast(F32), -1.0)
            ge.memset(neg_one[:, :].bitcast(F32), -1.0)
            link(ge.memset(reset, 1.0))
            select(ident[:, :], ident[:, :], ALU.not_equal, 1.0, -1, 1)
            select(ident_b[:, :], ident_b[:, :], ALU.not_equal, 1.0, -1, 1)
            select(neg_mask[:, :], neg_mask[:, :], ALU.is_gt, -1e30, 1, -1)
            select(before[:, :], before[:, :], ALU.is_gt, 0.0, 1, -1)
            select(neg_tri[:, :], neg_tri[:, :].bitcast(F32), ALU.is_ge, 0.0, -1, 1)
            ge.memset(reset.rearrange("p (c t) -> p c t", t=CHUNK)[:, :, 0:1], 0.0)
            for t, step, base in ((desc4, -1, NG), (desc16, -1, NE), (first_row, CAP, 0),
                                  (over_row, -CAP, CAP * (NE - 1)), (j_idx, 1, 0)):
                last = ge.iota(t[:, :], pattern=[[step, t.shape[-1]]], base=base, channel_multiplier=0,
                               allow_small_or_imprecise_dtypes=True)
            last.then_inc(G["consts"], 1)

            zero_row = zeros[0:CAP, :].unsqueeze(1).broadcast_to([CAP, D // 256, 256])
            with pool.Fori(0, NE + MAX_OVER) as i:
                pool.dma_start(table[bass.ds(i * CAP, CAP), :].rearrange("p (r n) -> p r n", n=256),
                               zero_row).then_inc(G["zeroed"], 16)
            load_gain(1)
            pool.wait_ge(V["att_out"], 1)
            att3 = kT.rearrange("p h t -> p (h t)").rearrange("p (a q) -> p a q", q=P)
            ge.affine_select(out=att3, in_=att3, compare_op=ALU.is_ge, fill=0.0, base=0,
                             pattern=[[0, NT * GH], [1, P]], channel_multiplier=-1).then_inc(G["masked"], 1)
            pool.wait_ge(G["masked"], 1)
            ge.memset(att3[0:CHUNK, :, CHUNK:P], 0.0).then_inc(G["masked"], 1)
            pool.wait_ge(A["panel_out"], 6)
            sg3 = sg.rearrange("p i (j e) -> p (i j) e", e=DV)
            ge.tensor_tensor(sg3, sg3, onorm.unsqueeze(1).broadcast_to([P, NT * GH, DV]), ALU.mult).then_inc(G["sg_ready"], 1)

            def experts(layer):
                I = NE * layer
                pool.wait_ge(V["pos_ready"], layer + 1)
                pool.wait_ge(V["xn_ready"], NT * (1 if layer == 0 else 4) + NT)
                pool.wait_ge(G["zeroed"], 16 * (NE + MAX_OVER))
                for i in range(NT):
                    for k in range(2):
                        pool.indirect_dma_start(out=table, out_offset=bass.IndirectOffsetOnAxis(ap=pos[:, k, i:i + 1], axis=0),
                                                in_=xn[:, i, :], in_offset=None).then_inc(G["scattered"], 16)
                load_gain(2 if layer == 0 else 5)
                pool.wait_ge(G["scattered"], 16 * 2 * NT * (layer + 1))

                def load(S, row, slot):
                    pool.dma_start(xg[:, slot, :], table[bass.ds(row, CAP), :]).then_inc((S["x_loaded0"], S["x_loaded1"])[slot], 16)

                def store(S, row):
                    pool.dma_start(table[bass.ds(row, CAP), :], y_sb).then_inc(S["y_stored"], 16)

                load(E, 0, 0)
                load(E, CAP, 1)
                with pool.Fori(0, PAIRS) as g:
                    for k in range(2):
                        i = 2 * g + (1 + k)
                        pool.wait_ge(E["x_tr"], 2 * i + 2 * I)
                        load(E, (i + 1) * CAP, k)
                        pool.wait_ge(E["y_out"], i + I)
                        store(E, (i - 1) * CAP)
                for i in (NE - 2, NE - 1):
                    pool.wait_ge(E["y_out"], I + i + 1)
                    store(E, i * CAP)
                pool.wait_ge(E["y_stored"], 16 * (I + NE))
                S = O[layer]

                def tile(j):
                    load(S, (j + NE) * CAP, 0)
                    hold(S["y_out"], j + 1)
                    store(S, (j + NE) * CAP)
                    hold(S["y_stored"], 16 * j + 16)

                over_loop(pool, layer, tile)
                for i in range(NT):
                    for k in range(2):
                        n = 2 * i + k
                        if n >= 4:
                            pool.wait_ge(V["combined"], 2 * NT * layer + n - 3)
                        pool.indirect_dma_start(out=xn[:, n % 4, :], out_offset=None, in_=table,
                                                in_offset=bass.IndirectOffsetOnAxis(ap=pos[:, k, i:i + 1], axis=0)).then_inc(gathered[n % 4], 16)

            experts(0)
            load_gain(3)
            load_gain(4)
            pool.wait_ge(A["panel_out"], 12)

            def stage(q, b):
                ge.tensor_copy(kst[:, b, :], kT1[:, bass.ds(q, 1), :].rearrange("p o t -> p (o t)")).then_inc(G["staged"], 1)
                ge.tensor_copy(qst[:, b, :], qT1[:, bass.ds(q, 1), :].rearrange("p o t -> p (o t)")).then_inc(G["staged"], 1)
                ge.tensor_copy(vst[:, b, :, :], v[:, :, bass.ds(q * P, P)]).then_inc(G["staged"], 1)

            stage(0, 0)
            stage(1, 1)
            with pool.Fori(1, 4) as g:
                for b in range(2):
                    pool.wait_ge(M["av_done"], 4 * g + (2 * b - 2))
                    stage(2 * g + b, b)
            experts(1)


_INS = ["x", "a_norm", "a_w_in", "a_w_gk2", "a_b_gk2", "a_o_norm", "a_w_out", "kv_norm", "w_kv", "b_norm",
        "b_w_q", "b_w_out", "m_norm", "m_w_group", "m_b_group", "m_w_expert", "m_b_expert", "m_w_gate",
        "m_w_up", "m_w_down", "final_norm"]


def kernel(**inputs):
    import numpy as np
    import concourse.bacc as bacc
    from concourse.bass_utils import run_bass_kernel_spmd

    nc = bacc.Bacc("TRN2", target_bir_lowering=False, num_devices=1)
    arrays, args = {}, []
    for name in _INS:
        a = np.ascontiguousarray(inputs[name])
        arrays[f"in_{name}"] = a
        args.append(nc.dram_tensor(f"in_{name}", a.shape, mybir.dt.from_np(a.dtype), kind="ExternalInput").ap())
    args.append(nc.dram_tensor("out_h", [1, T, D], F32, kind="ExternalOutput").ap())
    trunk(nc, *args)
    return run_bass_kernel_spmd(nc, [arrays], core_ids=[0]).results[0]["out_h"]
```

```python
from contextlib import ExitStack

import concourse.bass as bass
import numpy as np
from concourse import mybir

F32 = mybir.dt.float32
F32R = mybir.dt.float32r
BF16 = mybir.dt.bfloat16
I32 = mybir.dt.int32
U32 = mybir.dt.uint32
ALU = mybir.AluOpType
ACT = mybir.ActivationFunctionType
AX = mybir.AxisListType

P = 128
D = 1024
T = 512
NT = T // P
KT = D // P
EPS = 1e-6
LAYERS = 2

GH, DK, DV, RANK, CHUNK = 4, 128, 256, 16, 64
GATE_NORM = 16.0
QK = GH * DK
GK0 = 2 * QK + D
G0 = GK0 + RANK
NCH = T // CHUNK

SH, SD = 16, 64
ZW = [T - P * i for i in range(NT)]
ZO = [0, T, 2 * T, 2 * T - P]
ZC = 2 * T + 2 * P
ZPARTS = [slice(T, ZC), slice(0, T)]
ZBLOCKS = [(1, 3, 2), (0,)]

NG, EG = 4, 4
NE = NG * EG
F = 512
NR = NG + NE
CAP = 96
MAX_OVER = 10
TILES = NE + MAX_OVER
ROWS = TILES * CAP
STEPS_OVER = (T - 1) // CAP

BK = 4
BN = 512
BW = BK * BN
RAW, RAW_E = 4, 6
SPLIT, SPLIT_E = 2, 4
A_BLOCKS = 16
E_BLOCKS = 6
L_BLOCKS = A_BLOCKS + NE * E_BLOCKS


class Chain:

    def __init__(self, eng, sem):
        self.eng, self.sem, self.n = eng, sem, 0

    def __call__(self, *instructions):
        for ins in instructions:
            ins.then_inc(self.sem, 1)
        self.n = self.n + len(instructions)
        self.eng.wait_ge(self.sem, self.n)


def trunk(nc, x, a_norm, a_w_in, a_w_gk2, a_b_gk2, a_o_norm, a_w_out, kv_norm, w_kv, b_norm, b_w_q,
          b_w_out, m_norm, m_w_group, m_b_group, m_w_expert, m_b_expert, m_w_gate, m_w_up, m_w_down,
          final_norm, out):
    with ExitStack() as ctx:
        def sb(name, shape, dt=F32):
            return ctx.enter_context(nc.sbuf_tensor(name, shape, dt))

        def sem(name):
            return ctx.enter_context(nc.semaphore(name))

        rows = nc.dram_tensor("normed_rows", [T, D], F32).ap()
        table = nc.dram_tensor("output_table", [ROWS, D], F32).ap()
        h = sb("h", [P, NT, D])
        xn = sb("xn", [P, NT, D])
        xT_hi = sb("xT_hi", [P, KT, T], F32R)
        xT_lo = sb("xT_lo", [P, KT, T], F32R)
        raw = sb("raw", [P, RAW, BW])
        w_hi = sb("w_hi", [P, SPLIT, BW], F32R)
        w_lo = sb("w_lo", [P, SPLIT, BW], F32R)
        s_hi = sb("s_hi", [P, ZC], F32R)
        s_lo = sb("s_lo", [P, ZC], F32R)
        r_hi = sb("r_hi", [P, KT, NR], F32R)
        r_lo = sb("r_lo", [P, KT, NR], F32R)
        gain = sb("gain", [P, D])
        pad = sb("pad", [P, 14336 + DV])
        zeros = sb("zeros", [P, 256])
        ident = sb("ident", [P, P])
        ident_b = sb("ident_b", [P, P], BF16)
        neg_mask = sb("neg_mask", [P, P], BF16)
        before = sb("before", [P, P], BF16)
        ones_b = sb("ones_b", [P, P], BF16)
        neg_tri = sb("neg_tri", [P, P], F32R)
        neg_one = sb("neg_one", [P, P], F32R)
        lr_raw = sb("lr_raw", [P, KT, RANK])
        bgk = sb("bgk", [P, GH])
        r_raw = sb("r_raw", [P, LAYERS, KT, NR])
        r_bias = sb("r_bias", [P, LAYERS, NR])
        ss = sb("ss", [P, 16])
        ms = sb("ms", [P, 16])
        y0 = sb("y0", [P, 16])
        y1 = sb("y1", [P, 16])
        rstd = sb("rstd", [P, 16])
        decay = sb("decay", [P, GH, NCH])
        w12 = sb("w12", [P, 2, NT])
        pos = sb("pos", [P, 2, NT], U32)
        token = sb("token", [CAP, TILES], U32)
        token_now = sb("token_now", [CAP, 2], U32)
        gainT = sb("gainT", [P, 5 * KT])
        over = sb("over", [1, MAX_OVER + 1], I32)

        def region(start, width):
            return pad[:, start:start + width]

        raw_slots = [raw[:, s, :] for s in range(RAW)] + [
            xn[:, 2 * s:2 * s + 2, :].rearrange("p i n -> p (i n)") for s in range(RAW_E - RAW)]
        hi_slots, lo_slots = ([w[:, s, :] for s in range(SPLIT)] + [
            x_t[:, BK * s:BK * (s + 1), :].rearrange("p k t -> p (k t)") for s in range(SPLIT_E - SPLIT)]
            for w, x_t in ((w_hi, xT_hi), (w_lo, xT_lo)))
        qT = region(0, 2048).rearrange("p (h t) -> p h t", h=GH)
        kT = region(2048, 2048).rearrange("p (h t) -> p h t", h=GH)
        kinv = region(4096, 2048).rearrange("p (h t) -> p h t", h=GH)
        gate = region(6144, 2048).rearrange("p (h t) -> p h t", h=GH)
        lrT = pad[0:RANK, 4096:4096 + T]
        wgk2 = pad[0:RANK, 4096 + T:4096 + 2 * T]
        v = region(8192, 4096).rearrange("p (i n) -> p i n", i=NT)
        state = region(12288, 2048).rearrange("p (b h e) -> p b h e", b=2, h=GH)
        reset = region(12288, T)
        onorm = region(14336, DV)
        sg = region(0, 4096).rearrange("p (i n) -> p i n", i=NT)
        cum = xn[:, 0:2, :].rearrange("p a (b t) -> p (a b) t", b=2)
        kT1 = region(0, 4096).rearrange("p (q t) -> p q t", q=KT)
        qT1 = region(4096, 4096).rearrange("p (q t) -> p q t", q=KT)
        kst = region(12288, 2 * T).rearrange("p (b t) -> p b t", b=2)
        qst = region(12288 + 2 * T, 2 * T).rearrange("p (b t) -> p b t", b=2)
        xnf = xn[:, :, :].rearrange("p i n -> p (i n)")
        vst = xnf[:, 2 * ZC:2 * ZC + 2 * T].rearrange("p (b i e) -> p b i e", b=2, i=NT)
        zt = [xnf[:, 0:ZC], xnf[:, ZC:2 * ZC]]
        wt = [raw[:, 0, 0:ZC], raw[:, 1, 0:ZC]]
        xg = pad[0:CAP, 0:2 * D].rearrange("p (b n) -> p b n", b=2)
        sil = pad[0:CAP, 2048:2048 + F]
        hid = pad[0:CAP, 2560:2560 + F]
        y_sb = pad[0:CAP, 3072:3072 + D]
        over_raw = region(4096, BW)
        y_rows = [xn[:, i, :] for i in range(NT)] + [
            xT_hi[:, 2 * i:2 * i + 2, :].rearrange("p k t -> p (k t)").bitcast(F32) for i in range(NT)]
        xg_hi, xg_lo = (t[:, 0:KT * CAP].rearrange("p (k c) -> p k c", k=KT) for t in (s_hi, s_lo))
        ht_hi, ht_lo = (t[:, KT * CAP:(KT + BK) * CAP].rearrange("p (k c) -> p k c", k=BK)
                        for t in (s_hi, s_lo))
        lr_hi, lr_lo = (t[:, 0:KT * RANK].rearrange("p (k c) -> p k c", k=KT) for t in (s_hi, s_lo))
        diag = region(13312 + P, NT * P).rearrange("p (i t) -> p i t", i=NT)
        gain_rows = pad[0:5 * KT, 13312:13312 + P]
        free = [6144]

        def scratch(*shape):
            n = int(np.prod(shape))
            free[0] += n
            t = region(free[0] - n, n)
            if len(shape) == 2:
                return t.rearrange("p (a b) -> p a b", b=shape[1])
            return t.rearrange("p (a b c) -> p a b c", b=shape[1], c=shape[2]) if len(shape) == 3 else t

        lg = scratch(NT, NR)
        gd, geq, gv, goh, gneg = (scratch(NT, NG) for _ in range(5))
        em, eq, ev, em2 = (scratch(NT, NE) for _ in range(4))
        oh = scratch(2, NT * NE)
        oh_k = oh.rearrange("p k (i e) -> p (k i) e", e=NE)
        rank, tmp_rank, tmp_base = scratch(2, NT * NE), scratch(2 * NT, NE), scratch(2 * NT, NE)
        gm, gvm, gs, gw, dd, ex, denom, rs = (scratch(NT) for _ in range(8))
        m12, evm = scratch(2, NT), scratch(2, NT)
        cnt, ovn, ovend, ovbase = (scratch(NE) for _ in range(4))
        cnt_over = scratch(NE, STEPS_OVER)
        e_k, rank_k, o_k, base_k, tile_k, row_k, step_k, p_k = (scratch(2 * NT) for _ in range(8))
        rank_over = scratch(2 * NT, STEPS_OVER)
        at_row, at_tile, at_tile_t = scratch(2 * NT, CAP), scratch(2 * NT, TILES), scratch(2 * NT, TILES)
        over_cmp, over_f = scratch(MAX_OVER, NE), scratch(MAX_OVER + 1)
        logitsT = pad[0:NR, 9216:9216 + T]
        desc4 = sb("desc4", [P, NG])
        desc16 = sb("desc16", [P, NE])
        caps = sb("caps", [P, STEPS_OVER])
        index = sb("index", [P, CAP])
        token_id = sb("token_id", [P, NT])
        one16 = sb("one16", [P, NE])
        sel_b = sb("sel_b", [P, NT, NE], BF16)

        ps = ctx.enter_context(nc.psum_tensor("ps", [P, 8, 512], F32))
        psf = ps[:, :, :].rearrange("p b n -> p (b n)")

        def sems(names):
            return {n: sem(n) for n in names.split()}

        x_loaded = [sem(f"x_loaded{i}") for i in range(NT)]
        raw_loaded = [sem(f"raw_loaded{i}") for i in range(RAW_E)]
        out_stored = sem("out_stored")
        A = sems("small_loaded hi_done act_chain ssq_done rs_first xT_hi_done panel_out lr_hi_done "
                 "gate_ln gate_exp ktok_out o_out r_hi_done group_exp second_exp z_exp z_ln L_hi_done "
                 "weights_done oT_hi_done logits_out router_loaded rows_stored")
        V = sems("lo_done dve_chain gains_out ms_ready diag_ready xn_ready xT_lo_done h_added lr_lo_done lr_out gates_in "
                 "gate_abs gate_cum q_dec k_inv gate_toend k_toend att_out state_done og_ready r_lo_done "
                 "group_diff second_diff sel_ready places_ready tokens_ready pos_ready combined z_abs L_done L_lo_done oT_lo_done")
        M = sems("gains_tr blk_used xT_tr lr_done gates_done ktok_tr att_done upd_done inter_done logits_done logits_tr "
                 "ranks_done lists_done z_done sums_done av_done")
        G = sems("consts pool_chain masked sg_ready staged gain_loaded zeroed over_ended")
        gathered = [sem(f"gathered{i}") for i in range(2 * NT)]

        def expert_sems(tag):
            names = "x_loaded0 x_loaded1 x_tr x_hi x_lo silu mul h_tr h_hi h_lo y_out y_stored turn out_seen column column_seen"
            return {n: sem(f"{tag}_{n}") for n in names.split()}

        E = expert_sems("first")
        O = [expert_sems(f"over{l}") for l in range(LAYERS)]
        OW = [{n: sem(f"over{l}_w_{n}") for n in "loaded hi lo used".split()}
              for l in range(LAYERS)]

        block = ctx.enter_context(nc.Block())
        ve, se, te, ge = nc.vector, nc.scalar, nc.tensor, nc.gpsimd

        def number(c, g=0):
            return 12 * g + c

        def expert_part(c):
            return c % L_BLOCKS - A_BLOCKS, c // L_BLOCKS

        def raw_slot(c):
            e = expert_part(c)[0]
            return e % RAW_E if e >= 0 else (e + A_BLOCKS) % RAW

        def raw_loads(c, g=0):
            e, layer = expert_part(c)
            both = (NE * E_BLOCKS // RAW_E, A_BLOCKS // RAW if raw_slot(c) < RAW else 0)
            n = sum(both) * layer + (e // RAW_E + both[1] if e >= 0 else (e + A_BLOCKS) // RAW)
            return 16 * (12 // RAW_E * g + (n + 1))

        def raw_before(c):
            e = expert_part(c)[0]
            return c - (RAW_E if e >= RAW or e < RAW - A_BLOCKS else RAW)

        def split_slot(c):
            e = expert_part(c)[0]
            return e % SPLIT_E if e >= 0 else (e + A_BLOCKS) % SPLIT

        def split_before(c):
            e = expert_part(c)[0]
            return c - (SPLIT_E if e >= SPLIT or e < SPLIT - A_BLOCKS else SPLIT)

        def panel(w, col, k0):
            return w[k0 * P:(k0 + BK) * P, col:col + BN].rearrange("(k p) n -> p k n", p=P)

        a_cols = [0, QK, 2 * QK, 2 * QK + BN, G0, G0 + BN]
        halves = (0, BK)
        streams = [[panel(a_w_in[0], c, k0) for c in a_cols for k0 in halves]
                   + [panel(a_w_out[0], c, k0) for c in (0, BN) for k0 in halves],
                   [panel(w_kv, c, k0) for c in range(0, 2 * D, BN) for k0 in halves]
                   + [panel(b_w_q[0], c, k0) for c in (0, BN) for k0 in halves]
                   + [panel(b_w_out[0], c, k0) for c in (0, BN) for k0 in halves]]

        def expert_block(layer, kind, e, half):
            w = {"g": m_w_gate, "u": m_w_up, "d": m_w_down}[kind][layer]
            w = w[bass.ds(e, 1), :, :].rearrange("o k n -> (o k) n")
            if kind == "d":
                return w[:, half * BN:(half + 1) * BN].rearrange("(k p) n -> p k n", p=P)
            return w[half * BK * P:(half + 1) * BK * P, :].rearrange("(k p) n -> p k n", p=P)

        def blocks_of(layer):
            return layer * L_BLOCKS + A_BLOCKS

        PAIRS = (NE - 2) // 2
        LAST = 4 + E_BLOCKS * (NE - 2)

        def panel_banks(p):
            return slice(4 * (p % 2), 4 * (p % 2) + 4)

        def z_of(r):
            return psf[:, 1536 * r:1536 * r + ZC]

        def wait_h(eng, event, i):
            if event == 0:
                eng.wait_ge(x_loaded[i], 16)
            elif event % 2:
                eng.wait_ge(V["h_added"], NT * (event // 2) + i + 1)
            else:
                eng.wait_ge(V["combined"], 2 * NT * (event // 2 - 1) + 2 * (i + 1))

        pool_engine = nc.gpsimd

        def over_loop(eng, layer, tile):
            eng.wait_ge(V["pos_ready"], layer + 1)
            n = eng.value_load(over[0:1, MAX_OVER:MAX_OVER + 1], min_val=0, max_val=MAX_OVER)
            with eng.If(n > 0):
                with eng.Fori(0, n) as j:
                    tile(j)
            with eng.Else():
                eng.nop()
            if eng.engine != pool_engine.engine:
                eng.wait_ge(G["over_ended"], layer + 1)

        @block.sync
        def _(sp):
            def load(src, c, g=0):
                if raw_before(c) >= 0:
                    sp.wait_ge(V["lo_done"], number(raw_before(c) + 1, g))
                sp.dma_start(raw_slots[raw_slot(c)].rearrange("p (k n) -> p k n", k=BK),
                             src).then_inc(raw_loaded[raw_slot(c)], 16)

            for i in range(NT):
                sp.dma_start(h[:, i, :], x[0, i * P:(i + 1) * P, :]).then_inc(x_loaded[i], 16)
            for layer in range(LAYERS):
                for n, src in enumerate(streams[layer]):
                    load(src, layer * L_BLOCKS + n)
                B = blocks_of(layer)
                for n, (kind, half) in enumerate((k, f) for k in "gu" for f in (0, 1)):
                    if layer and n == 0:
                        sp.wait_ge(M["av_done"], SH)
                    load(expert_block(layer, kind, 0, half), B + n)

                def step(e, c, g=0):
                    for n, (kind, back, half) in enumerate((k, b, f) for k, b in zip("gud", (0, 0, 1)) for f in (0, 1)):
                        load(expert_block(layer, kind, e - back, half), c + n, g)

                sp.wait_ge(A["rows_stored"], 16 * NT * (layer + 1))
                with sp.Fori(0, PAIRS) as g:
                    for k in range(2):
                        step(2 * g + (k + 1), B + 4 + E_BLOCKS * k, g)
                step(NE - 1, B + LAST)
                for half in (0, 1):
                    load(expert_block(layer, "d", NE - 1, half), B + LAST + E_BLOCKS + half)
            for i in range(NT):
                sp.wait_ge(V["xn_ready"], NT * 2 + i + 1)
                sp.dma_start(out[0, i * P:(i + 1) * P, :], xn[:, i, :]).then_inc(out_stored, 16)
            sp.wait_ge(out_stored, 16 * NT)

        @block.scalar
        def _(act):
            def split(c, g=0):
                act.wait_ge(raw_loaded[raw_slot(c)], raw_loads(c, g))
                if split_before(c) >= 0:
                    act.wait_ge(M["blk_used"], number(split_before(c) + 1, g))
                se.copy(hi_slots[split_slot(c)], raw_slots[raw_slot(c)]).then_inc(A["hi_done"], 1)

            loads = [(lr_raw[:, :, :], a_w_in[0, :, GK0:GK0 + RANK].rearrange("(k p) r -> p k r", p=P))]
            loads += [(gain_rows[KT * n:KT * (n + 1), :], g.rearrange("(k p) -> k p", p=P))
                      for n, g in enumerate((a_norm[0], m_norm[0], kv_norm, b_norm[0], m_norm[1]))]
            loads += [(wgk2, a_w_gk2[0]),
                      (bgk[:, :], a_b_gk2[0].rearrange("(h p) -> p h", p=P)),
                      (onorm, a_o_norm[0].partition_broadcast(P))]
            router_loads = []
            for l in range(LAYERS):
                router_loads += [(r_raw[:, l, :, 0:NG], m_w_group[l].rearrange("(k p) n -> p k n", p=P)),
                                 (r_raw[:, l, :, NG:NR], m_w_expert[l].rearrange("(k p) n -> p k n", p=P)),
                                 (r_bias[:, l, 0:NG], m_b_group[l].partition_broadcast(P)),
                                 (r_bias[:, l, NG:NR], m_b_expert[l].partition_broadcast(P))]

            def load_small(pairs, done):
                with nc.allow_non_contiguous_dma(reason="512 gate biases and 20 router columns a row"):
                    for dst, src in pairs:
                        act.dma_start(dst, src).then_inc(done, 16)

            load_small(loads, A["small_loaded"])

            norms = [0]

            def rsqrt_first(width):
                norms[0] += 1
                act.wait_ge(V["ms_ready"], norms[0])
                se.activation(y1[:, 0:width], ms[:, 0:width], ACT.Ln).then_inc(A["act_chain"], 1)
                act.wait_ge(A["act_chain"], norms[0])
                se.activation(y0[:, 0:width], y1[:, 0:width], ACT.Exp, scale=-0.5).then_inc(A["rs_first"], 1)

            def norm_squares(event):
                for i in range(NT):
                    wait_h(act, event, i)
                    if event == 0 and i == NT - 1:
                        act.wait_ge(V["gains_out"], 1)
                    se.activation(psf[:, D * i:D * (i + 1)], h[:, i, :], ACT.Square,
                                  accum_out=ss[:, i:i + 1]).then_inc(A["ssq_done"], 1)
                rsqrt_first(NT)

            def transposed_hi(turn, gain_no=None):
                for k in range(KT):
                    act.wait_ge(M["xT_tr"], KT * turn + k + 1)
                    if gain_no is None:
                        se.copy(xT_hi[:, k, :], ps[:, k % 4, :]).then_inc(A["xT_hi_done"], 1)
                    else:
                        n = KT * gain_no + k
                        se.activation(xT_hi[:, k, :], ps[:, k % 4, :], ACT.Copy,
                                      scale=gainT[:, n:n + 1]).then_inc(A["xT_hi_done"], 1)

            def panel_out(p, last_block, dst, func=ACT.Copy, scale=1.0):
                act.wait_ge(M["blk_used"], last_block + 1)
                se.activation(dst, ps[:, panel_banks(p), :], func, scale=scale).then_inc(A["panel_out"], 1)

            LN_EXP = "natural_log_exp_and_others"
            se.preload_act_table_set(LN_EXP)
            act.wait_ge(A["small_loaded"], 16 * len(loads))
            se.copy(lr_hi, lr_raw[:, :, :]).then_inc(A["lr_hi_done"], 1)
            norm_squares(0)
            split(0)
            split(1)
            transposed_hi(0, 0)
            load_small(router_loads, A["router_loaded"])
            act.wait_ge(V["gate_abs"], 1)
            se.activation(cum, cum, ACT.Exp, scale=-1.0).then_inc(A["gate_ln"], 1)
            act.wait_ge(A["gate_ln"], 1)
            se.activation(cum, cum, ACT.Ln, bias=1.0).then_inc(A["gate_ln"], 1)
            split(2)
            act.wait_ge(V["gate_cum"], GH)
            se.activation(gate, cum, ACT.Exp, scale=1.0 / GATE_NORM).then_inc(A["gate_exp"], 1)
            se.activation(kinv, cum, ACT.Exp, scale=-1.0 / GATE_NORM).then_inc(A["gate_exp"], 1)
            panel_out(0, 1, qT, scale=DK ** -0.5)
            split(3)
            split(4)
            panel_out(1, 3, kT)
            split(5)
            act.wait_ge(V["gate_toend"], 1)
            se.activation(gate, gate, ACT.Exp, scale=1.0 / GATE_NORM).then_inc(A["gate_exp"], 1)
            split(6)
            panel_out(2, 5, v[:, :, 0:BN])
            split(7)
            split(8)
            panel_out(3, 7, v[:, :, BN:2 * BN])
            split(9)
            act.wait_ge(M["ktok_tr"], 1)
            se.copy(gate, ps[:, 0:4, :]).then_inc(A["ktok_out"], 1)
            for i in range(NT):
                act.wait_ge(M["inter_done"], 2 * i + 1)
                se.copy(xn[:, i, :], psf[:, 2048 + 1024 * (i % 2):3072 + 1024 * (i % 2)]).then_inc(A["o_out"], 1)
            rsqrt_first(NT * GH)
            for p in (4, 5):
                split(2 * p + 2)
                panel_out(p, 2 * p + 1, sg[:, :, (p - 4) * BN:(p - 3) * BN], ACT.Silu)
                split(2 * p + 3)
            transposed_hi(1)
            for n in range(A_BLOCKS - 2, A_BLOCKS + 2):
                split(n)

            def x_hi(S, i):
                for f in (0, 1):
                    act.wait_ge(S["x_tr"], 2 * i + (f + 1))
                    se.copy(xg_hi[:, 4 * f:4 * f + 4, :],
                            ps[:, 4 + f, 0:4 * CAP].rearrange("p (k c) -> p k c", k=4)).then_inc(S["x_hi"], 1)

            def silu(S, i, reuse=True):
                if reuse:
                    act.wait_ge(S["mul"], i)
                se.activation(sil, ps[0:CAP, 0, :], ACT.Silu).then_inc(S["silu"], 1)

            def h_hi(S, i):
                act.wait_ge(S["h_tr"], i + 1)
                se.copy(ht_hi, ps[:, 6, 0:BK * CAP].rearrange("p (k c) -> p k c", k=BK)).then_inc(S["h_hi"], 1)

            def y_out(S, i, reuse=True):
                if reuse:
                    act.wait_ge(S["y_stored"], 16 * i)
                se.copy(y_sb, psf[0:CAP, 1024:2048]).then_inc(S["y_out"], 1)

            def experts(layer):
                B, I = blocks_of(layer), NE * layer
                split(B + 2)
                split(B + 3)
                x_hi(E, I)
                split(B + 4)
                split(B + 5)
                silu(E, I, layer > 0)
                split(B + 6)
                split(B + 7)
                x_hi(E, I + 1)
                h_hi(E, I)

                def step(i, c, g, more):
                    split(c + 4, g)
                    split(c + 5, g)
                    silu(E, i)
                    split(c + 6, g)
                    split(c + 7, g)
                    if more:
                        x_hi(E, i + 1)
                        split(c + 8, g)
                        split(c + 9, g)
                    else:
                        act.wait_ge(M["blk_used"], number(c + 6, g))
                    y_out(E, i - 1, not (isinstance(i, int) and i == 1))
                    h_hi(E, i)

                for k in range(2):
                    step(I + 1 + k, B + 4 + E_BLOCKS * k, 0, True)
                with act.Fori(1, PAIRS) as g:
                    for k in range(2):
                        step(2 * g + (I + 1 + k), B + 4 + E_BLOCKS * k, g, True)
                step(I + NE - 1, B + LAST, 0, False)
                act.wait_ge(M["blk_used"], B + NE * E_BLOCKS)
                y_out(E, I + NE - 1)

                S, W = O[layer], OW[layer]

                def tile(j):
                    act.wait_ge(S["turn"], j + 1)
                    e = act.value_load(over[0:1, bass.ds(j, 1)], min_val=0, max_val=NE - 1)
                    x_hi(S, j)
                    for b, (kind, half) in enumerate((k, f) for k in "gud" for f in (0, 1)):
                        if b:
                            act.wait_ge(W["lo"], 6 * j + b)
                        act.dma_start(over_raw.rearrange("p (k n) -> p k n", k=BK),
                                      expert_block(layer, kind, e, half)).then_inc(W["loaded"], 16)
                        act.wait_ge(W["loaded"], 96 * j + 16 * (b + 1))
                        if b >= SPLIT:
                            act.wait_ge(W["used"], 6 * j + (b - SPLIT + 1))
                        se.copy(w_hi[:, b % SPLIT, :], over_raw).then_inc(W["hi"], 1)
                        if b == 3:
                            silu(S, j, False)
                            h_hi(S, j)
                    act.wait_ge(W["used"], 6 * j + 6)
                    y_out(S, j, False)

                over_loop(act, layer, tile)

            def router_weights(layer):
                act.wait_ge(A["router_loaded"], 16 * len(router_loads))
                se.copy(r_hi[:, :, :], r_raw[:, layer, :, :]).then_inc(A["r_hi_done"], 1)

            def router(layer):
                act.wait_ge(M["logits_done"], layer + 1)
                se.copy(logitsT, ps[0:NR, 7, :]).then_inc(A["logits_out"], 1)
                for i in range(NT):
                    act.wait_ge(V["xn_ready"], NT * layer + i + 1)
                    act.dma_start(rows[i * P:(i + 1) * P, :], xn[:, i, :]).then_inc(A["rows_stored"], 16)
                act.wait_ge(V["group_diff"], layer + 1)
                se.activation(gd, gd, ACT.Exp).then_inc(A["group_exp"], 1)
                act.wait_ge(V["second_diff"], layer + 1)
                se.activation(ex, dd, ACT.Exp).then_inc(A["second_exp"], 1)

            se.preload_act_table_set(LN_EXP)
            router_weights(0)
            norm_squares(1)
            transposed_hi(2, 1)
            router(0)
            experts(0)

            B = L_BLOCKS
            split(B)
            split(B + 1)
            se.preload_act_table_set(LN_EXP)
            norm_squares(2)
            transposed_hi(3, 2)
            for q, dst in enumerate((kT1[:, 0:4, :], kT1[:, 4:8, :], v[:, :, 0:BN], v[:, :, BN:2 * BN])):
                split(B + 2 * q + 2)
                panel_out(8 + q, B + 2 * q + 1, dst)
                split(B + 2 * q + 3)
            transposed_hi(4, 3)
            for q in (4, 5):
                split(B + 2 * q + 2)
                panel_out(8 + q, B + 2 * q + 1, qT1[:, 4 * (q - 4):4 * (q - 3), :], scale=SD ** -0.5)
                split(B + 2 * q + 3)

            def softplus(hd, r):
                for p, cols in enumerate(ZPARTS):
                    act.wait_ge(V["z_abs"], 2 * hd + (p + 1))
                    se.activation(zt[r][:, cols], zt[r][:, cols], ACT.Exp, scale=-1.0).then_inc(A["z_exp"], 1)
                    act.wait_ge(A["z_exp"], 2 * hd + (p + 1))
                    se.activation(zt[r][:, cols], zt[r][:, cols], ACT.Ln, bias=1.0).then_inc(A["z_ln"], 1)

            def L_hi(hd, r):
                for p, cols in enumerate(ZPARTS):
                    act.wait_ge(V["L_done"], 2 * hd + (p + 1))
                    se.copy(s_hi[:, cols], zt[r][:, cols]).then_inc(A["L_hi_done"], 1)

            def weights(hd, r, reuse=True):
                if reuse:
                    act.wait_ge(M["av_done"], hd - 1)
                for p, cols in enumerate(ZPARTS):
                    act.wait_ge(M["sums_done"], 2 * hd + (p + 1))
                    se.activation(wt[r][:, cols], z_of(r)[:, cols], ACT.Exp).then_inc(A["weights_done"], 1)

            def oT_hi(q, b):
                act.wait_ge(M["av_done"], 2 * q + 2)
                se.copy(xT_hi[:, bass.ds(q, 1), :].rearrange("p o t -> p (o t)"), ps[:, 6 + b, :]).then_inc(A["oT_hi_done"], 1)

            softplus(0, 0)
            L_hi(0, 0)
            softplus(1, 1)

            def head(hd, r, pair, reuse=True, more=2):
                weights(hd, r % 2, reuse)
                if more > 0:
                    L_hi(hd + 1, (r + 1) % 2)
                if more > 1:
                    softplus(hd + 2, r % 2)
                if r % 2:
                    oT_hi(pair, r // 2)

            for hd in range(4):
                head(hd, hd, hd // 2, hd >= 2)
            with act.Fori(1, 3) as g:
                for r in range(4):
                    head(4 * g + r, r, 2 * g + r // 2)
            for hd in range(12, 16):
                head(hd, hd - 12, hd // 2, more=15 - hd)
            for n in range(A_BLOCKS - 2, A_BLOCKS + 2):
                split(B + n)
            router_weights(1)
            norm_squares(3)
            transposed_hi(5, 4)
            router(1)
            experts(1)
            se.preload_act_table_set(LN_EXP)
            norm_squares(4)

        @block.vector
        def _(dve):
            link = Chain(dve, V["dve_chain"])

            def split(c, g=0):
                dve.wait_ge(A["hi_done"], number(c + 1, g))
                ve.tensor_tensor(lo_slots[split_slot(c)], raw_slots[raw_slot(c)], hi_slots[split_slot(c)],
                                 ALU.subtract).then_inc(V["lo_done"], 1)

            norms = [0]

            def refine(width):
                norms[0] += 1
                dve.wait_ge(A["rs_first"], norms[0])
                a, b, m, o = (t[:, 0:width] for t in (y0, y1, ms, rstd))
                link(ve.tensor_tensor(b, a, a, ALU.mult))
                link(ve.tensor_tensor(b, b, m, ALU.mult))
                link(ve.tensor_scalar(b, b, -0.5, 1.5, ALU.mult, ALU.add))
                link(ve.tensor_tensor(o, a, b, ALU.mult))

            def norm_scale(event):
                dve.wait_ge(A["ssq_done"], NT * (event + 1))
                ve.tensor_scalar(ms[:, 0:NT], ss[:, 0:NT], 1.0 / D, EPS, ALU.mult, ALU.add).then_inc(V["ms_ready"], 1)
                refine(NT)

            def diagonals():
                for i in range(NT):
                    ve.tensor_scalar(diag[:, i, :], ident[:, :], rstd[:, i:i + 1], None, ALU.mult).then_inc(V["diag_ready"], 1)

            def normed(use, tiles=range(NT)):
                dve.wait_ge(G["gain_loaded"], 16 * (use + 1))
                for i in tiles:
                    ve.scalar_tensor_tensor(xn[:, i, :], h[:, i, :], rstd[:, i:i + 1], gain[:, :],
                                            ALU.mult, ALU.mult).then_inc(V["xn_ready"], 1)

            def transposed_lo(turn, gain_no=None):
                for k in range(KT):
                    dve.wait_ge(A["xT_hi_done"], KT * turn + k + 1)
                    if gain_no is None:
                        ve.tensor_tensor(xT_lo[:, k, :], ps[:, k % 4, :], xT_hi[:, k, :],
                                         ALU.subtract).then_inc(V["xT_lo_done"], 1)
                    else:
                        n = KT * gain_no + k
                        ve.scalar_tensor_tensor(xT_lo[:, k, :], ps[:, k % 4, :], gainT[:, n:n + 1], xT_hi[:, k, :],
                                                ALU.mult, ALU.subtract).then_inc(V["xT_lo_done"], 1)

            def add_panel(p, last_block, half):
                dve.wait_ge(M["blk_used"], last_block + 1)
                for i in range(NT):
                    d = h[:, i, half * BN:(half + 1) * BN]
                    ins = ve.tensor_tensor(d, d, ps[:, 4 * (p % 2) + i, :], ALU.add)
                    if half:
                        ins.then_inc(V["h_added"], 1)

            dve.wait_ge(M["gains_tr"], 1)
            ve.tensor_copy(gainT[:, :], ps[:, 7, 0:5 * KT]).then_inc(V["gains_out"], 1)
            dve.wait_ge(A["lr_hi_done"], 1)
            ve.tensor_tensor(lr_lo, lr_raw[:, :, :], lr_hi, ALU.subtract).then_inc(V["lr_lo_done"], 1)
            norm_scale(0)
            diagonals()
            split(0)
            transposed_lo(0, 0)
            dve.wait_ge(M["lr_done"], 1)
            ve.tensor_copy(lrT, ps[0:RANK, 7, :]).then_inc(V["lr_out"], 1)
            split(1)
            dve.wait_ge(M["gates_done"], 1)
            for i in range(GH):
                ve.tensor_scalar(gate[:, i, :], ps[:, 4 + i, :], bgk[:, i:i + 1], None, ALU.add).then_inc(V["gates_in"], 1)
            dve.wait_ge(V["gates_in"], GH)
            ve.scalar_tensor_tensor(cum, gate, -1.0, gate, ALU.mult, ALU.max).then_inc(V["gate_abs"], 1)
            dve.wait_ge(A["gate_ln"], 2)
            link(ve.scalar_tensor_tensor(gate, gate, 0.0, cum, ALU.min, ALU.subtract))
            for i in range(GH):
                ve.tensor_tensor_scan(cum[:, i, :], reset, gate[:, i, :], 0.0, ALU.mult, ALU.add).then_inc(V["gate_cum"], 1)
            split(2)
            dve.wait_ge(A["gate_exp"], 1)
            dve.wait_ge(A["panel_out"], 1)
            ve.tensor_tensor(qT, qT, gate, ALU.mult).then_inc(V["q_dec"], 1)
            by_chunk = "p h (c t) -> p (h c) t"
            gate_c, cum_c = gate.rearrange(by_chunk, t=CHUNK), cum.rearrange(by_chunk, t=CHUNK)
            link(ve.tensor_copy(decay[:, :, :].rearrange("p h c -> p (h c)").unsqueeze(2), gate_c[:, :, CHUNK - 1:CHUNK]))
            ve.tensor_tensor(gate_c, cum_c[:, :, CHUNK - 1:CHUNK].broadcast_to([P, GH * NCH, CHUNK]), cum_c,
                             ALU.subtract).then_inc(V["gate_toend"], 1)
            split(3)
            split(4)
            dve.wait_ge(A["gate_exp"], 2)
            dve.wait_ge(A["panel_out"], 2)
            ve.tensor_tensor(kinv, kT, kinv, ALU.mult).then_inc(V["k_inv"], 1)
            split(5)
            dve.wait_ge(A["gate_exp"], 3)
            ve.tensor_tensor(kT, kT, gate, ALU.mult).then_inc(V["k_toend"], 1)
            for n in range(6, 10):
                split(n)
            dve.wait_ge(M["att_done"], 1)
            ve.tensor_copy(kT, ps[:, 4:8, :]).then_inc(V["att_out"], 1)
            for c in range(NCH - 1):
                dve.wait_ge(M["upd_done"], c + 1)
                if c >= 2:
                    dve.wait_ge(M["inter_done"], c - 1)
                u = psf[:, 1024 * (c % 2):1024 * (c % 2) + 1024].rearrange("p (h e) -> p h e", h=GH)
                s0, s1 = state[:, c % 2], state[:, (c + 1) % 2]
                if c == 0:
                    ve.tensor_copy(s1, u).then_inc(V["state_done"], GH)
                else:
                    dve.wait_ge(V["state_done"], GH * c)
                    for i in range(GH):
                        ve.scalar_tensor_tensor(s1[:, i, :], s0[:, i, :], decay[:, i, c:c + 1], u[:, i, :],
                                                ALU.mult, ALU.add).then_inc(V["state_done"], 1)
            o_sq = kinv[:, 0:2, :].rearrange("p a t -> p (a t)")
            for i in range(NT):
                dve.wait_ge(A["o_out"], i + 1)
                link(ve.tensor_tensor(o_sq, xn[:, i, :], xn[:, i, :], ALU.mult))
                link(ve.tensor_reduce(ss[:, GH * i:GH * i + GH], o_sq.rearrange("p (h e) -> p h e", h=GH), AX.X, ALU.add))
            ve.tensor_scalar(ms[:, 0:NT * GH], ss[:, 0:NT * GH], 1.0 / DV, EPS, ALU.mult, ALU.add).then_inc(V["ms_ready"], 1)
            refine(NT * GH)
            for n in range(10, 14):
                split(n)
            dve.wait_ge(G["sg_ready"], 1)
            for i in range(NT):
                for j in range(GH):
                    o = xn[:, i, DV * j:DV * (j + 1)]
                    ins = ve.scalar_tensor_tensor(o, o, rstd[:, GH * i + j:GH * i + j + 1],
                                                  sg[:, i, DV * j:DV * (j + 1)], ALU.mult, ALU.mult)
                ins.then_inc(V["og_ready"], 1)
            transposed_lo(1)
            split(14)
            add_panel(6, 13, 0)
            split(15)
            split(16)
            add_panel(7, 15, 1)
            split(17)

            def x_lo(S, i):
                for f in (0, 1):
                    dve.wait_ge(S["x_hi"], 2 * i + (f + 1))
                    ve.tensor_tensor(xg_lo[:, 4 * f:4 * f + 4, :],
                                     ps[:, 4 + f, 0:4 * CAP].rearrange("p (k c) -> p k c", k=4),
                                     xg_hi[:, 4 * f:4 * f + 4, :], ALU.subtract).then_inc(S["x_lo"], 1)

            def mul(S, i, reuse=True):
                dve.wait_ge(S["silu"], i + 1)
                if reuse:
                    dve.wait_ge(S["h_tr"], i)
                ve.tensor_tensor(hid, sil, ps[0:CAP, 1, :], ALU.mult).then_inc(S["mul"], 1)

            def h_lo(S, i):
                dve.wait_ge(S["h_hi"], i + 1)
                ve.tensor_tensor(ht_lo, ps[:, 6, 0:BK * CAP].rearrange("p (k c) -> p k c", k=BK), ht_hi,
                                 ALU.subtract).then_inc(S["h_lo"], 1)

            def experts(layer):
                B, I = blocks_of(layer), NE * layer
                split(B + 2)
                split(B + 3)
                x_lo(E, I)
                for n in range(4, 8):
                    split(B + n)
                dve.wait_ge(M["blk_used"], B + 4)
                mul(E, I, layer > 0)
                x_lo(E, I + 1)
                h_lo(E, I)

                def step(i, c, g, more):
                    for n in range(4, 8):
                        split(c + n, g)
                    mul(E, i)
                    if more:
                        x_lo(E, i + 1)
                        split(c + 8, g)
                        split(c + 9, g)
                    h_lo(E, i)

                with dve.Fori(0, PAIRS) as g:
                    for k in range(2):
                        step(2 * g + (I + 1 + k), B + 4 + E_BLOCKS * k, g, True)
                step(I + NE - 1, B + LAST, 0, False)

                S, W = O[layer], OW[layer]

                def tile(j):
                    dve.wait_ge(S["turn"], j + 1)
                    x_lo(S, j)
                    for b in range(6):
                        dve.wait_ge(W["hi"], 6 * j + (b + 1))
                        ve.tensor_tensor(w_lo[:, b % SPLIT, :], over_raw, w_hi[:, b % SPLIT, :],
                                         ALU.subtract).then_inc(W["lo"], 1)
                        if b == 3:
                            dve.wait_ge(W["used"], 6 * j + 4)
                            mul(S, j, False)
                            h_lo(S, j)

                over_loop(dve, layer, tile)

            def over4(a, n):
                return a.unsqueeze(2).broadcast_to([P, NT, n])

            def per_expert(a):
                return a.unsqueeze(1).broadcast_to([P, NT, NE])

            def router_weights(layer):
                dve.wait_ge(A["r_hi_done"], layer + 1)
                ve.tensor_tensor(r_lo[:, :, :], r_raw[:, layer, :, :], r_hi[:, :, :], ALU.subtract).then_inc(V["r_lo_done"], 1)

            def router(layer):
                tt, ts, red, stt = ve.tensor_tensor, ve.tensor_scalar, ve.tensor_reduce, ve.scalar_tensor_tensor
                normed(layer, (0, 1))
                dve.wait_ge(M["logits_tr"], layer + 1)
                link(tt(lg, ps[:, 6, 0:NT * NR].rearrange("p (i e) -> p i e", i=NT),
                        r_bias[:, layer, :].unsqueeze(1).broadcast_to([P, NT, NR]), ALU.add))
                lgg = lg[:, :, 0:NG]
                link(red(gm, lgg, AX.X, ALU.max))
                tt(gd, lgg, over4(gm, NG), ALU.subtract).then_inc(V["group_diff"], 1)
                link(tt(geq, lgg, over4(gm, NG), ALU.is_equal))
                link(tt(gv, geq, desc4[:, :].unsqueeze(1).broadcast_to([P, NT, NG]), ALU.mult))
                link(red(gvm, gv, AX.X, ALU.max))
                link(tt(goh, gv, over4(gvm, NG), ALU.is_equal))
                def by_group(t, i):
                    return t[:, i, :].rearrange("p (g e) -> p g e", g=NG)

                def each_expert(t, i):
                    return t[:, i, :].unsqueeze(2).broadcast_to([P, NG, EG])

                link(ts(gneg, goh, 1e30, -1e30, ALU.mult, ALU.add),
                     *[tt(by_group(em, i), lg[:, i, NG:NR].rearrange("p (g e) -> p g e", g=NG), each_expert(goh, i), ALU.mult)
                       for i in range(NT)])
                link(*[tt(by_group(em, i), by_group(em, i), each_expert(gneg, i), ALU.add) for i in range(NT)])

                def first_max(src, k):
                    one_hot = oh[:, k, :].rearrange("p (i e) -> p i e", i=NT)
                    link(red(m12[:, k, :], src, AX.X, ALU.max))
                    link(tt(eq, src, over4(m12[:, k, :], NE), ALU.is_equal))
                    link(tt(ev, eq, per_expert(desc16[:, :]), ALU.mult))
                    link(red(evm[:, k, :], ev, AX.X, ALU.max))
                    link(tt(one_hot, ev, over4(evm[:, k, :], NE), ALU.is_equal))
                    return one_hot

                oh1 = first_max(em, 0)
                link(stt(em2, oh1, -2e30, em, ALU.mult, ALU.add))
                oh2 = first_max(em2, 1)
                tt(sel_b[:, :, :], oh1, oh2, ALU.add).then_inc(V["sel_ready"], 1)
                tt(dd, m12[:, 1, :], m12[:, 0, :], ALU.subtract).then_inc(V["second_diff"], 1)
                normed(layer, (2, 3))
                dve.wait_ge(M["ranks_done"], layer + 1)
                rank_e = ps[:, 5, 0:NT * NE]
                by_choice = "p (k i) e -> p k (i e)"
                link(ve.tensor_copy(cnt, ps[:, 5, NT * NE:(NT + 1) * NE]),
                     tt(tmp_rank.rearrange(by_choice, k=2), oh, rank_e.unsqueeze(1).broadcast_to([P, 2, NT * NE]), ALU.mult))
                link(red(rank_k, tmp_rank, AX.X, ALU.add),
                     tt(cnt_over, cnt.unsqueeze(2).broadcast_to([P, NE, STEPS_OVER]),
                        caps[:, :].unsqueeze(1).broadcast_to([P, NE, STEPS_OVER]), ALU.is_gt))
                link(red(ovn, cnt_over, AX.X, ALU.add),
                     tt(rank_over, rank_k.unsqueeze(2).broadcast_to([P, 2 * NT, STEPS_OVER]),
                        caps[:, :].unsqueeze(1).broadcast_to([P, 2 * NT, STEPS_OVER]), ALU.is_ge))
                link(ve.tensor_tensor_scan(ovend, one16[:, :], ovn, 0.0, ALU.mult, ALU.add),
                     red(o_k, rank_over, AX.X, ALU.add),
                     ts(e_k, evm.rearrange("p k i -> p (k i)"), -1.0, float(NE), ALU.mult, ALU.add))
                link(tt(ovbase, ovend, ovn, ALU.subtract),
                     stt(row_k, o_k, -float(CAP), rank_k, ALU.mult, ALU.add),
                     ts(step_k, o_k, 0.0, None, ALU.is_gt))
                link(tt(tmp_base, oh_k, ovbase.unsqueeze(1).broadcast_to([P, 2 * NT, NE]), ALU.mult),
                     tt(at_row, index[:, :].unsqueeze(1).broadcast_to([P, 2 * NT, CAP]),
                        row_k.unsqueeze(2).broadcast_to([P, 2 * NT, CAP]), ALU.is_equal))
                link(red(base_k, tmp_base, AX.X, ALU.add))
                link(tt(base_k, base_k, o_k, ALU.add))
                link(stt(base_k, base_k, float(NE - 1), e_k, ALU.add, ALU.subtract))
                link(tt(base_k, base_k, step_k, ALU.mult))
                link(tt(tile_k, base_k, e_k, ALU.add))
                link(tt(at_tile, index[:, 0:TILES].unsqueeze(1).broadcast_to([P, 2 * NT, TILES]),
                        tile_k.unsqueeze(2).broadcast_to([P, 2 * NT, TILES]), ALU.is_equal))
                for k in range(2):
                    half = slice(NT * k, NT * (k + 1))
                    tt(at_tile_t[:, half, :], at_tile[:, half, :],
                       token_id[:, :].unsqueeze(2).broadcast_to([P, NT, TILES]), ALU.mult).then_inc(V["places_ready"], 1)
                link(stt(p_k, tile_k, float(CAP), row_k, ALU.mult, ALU.add),
                     tt(over_cmp, ovend.unsqueeze(1).broadcast_to([P, MAX_OVER, NE]),
                        index[:, 0:MAX_OVER].unsqueeze(2).broadcast_to([P, MAX_OVER, NE]), ALU.is_le))
                dve.wait_ge(M["lists_done"], layer + 1)
                ve.tensor_copy(token[:, :], ps[0:CAP, 4, 0:TILES]).then_inc(V["tokens_ready"], 1)
                link(red(over_f[:, 0:MAX_OVER], over_cmp, AX.X, ALU.add),
                     ve.tensor_copy(pos[:, :, :].rearrange("p k i -> p (k i)"), p_k))
                link(ts(over_f[:, 0:MAX_OVER], over_f[:, 0:MAX_OVER], float(NE - 1), None, ALU.min),
                     ve.tensor_copy(over_f[:, MAX_OVER:MAX_OVER + 1], ovend[:, NE - 1:NE]))
                ve.tensor_copy(over[:, :], over_f[0:1, :]).then_inc(V["pos_ready"], 1)
                dve.wait_ge(A["group_exp"], layer + 1)
                dve.wait_ge(A["second_exp"], layer + 1)
                link(red(gs, gd, AX.X, ALU.add),
                     ts(denom, ex, 1.0, None, ALU.add))
                link(ve.reciprocal(gw, gs),
                     ve.reciprocal(rs, denom))
                link(tt(w12[:, 0, :], rs, gw, ALU.mult))
                link(tt(w12[:, 1, :], w12[:, 0, :], ex, ALU.mult))

            def combine(layer):
                for i in range(NT):
                    for k in range(2):
                        n = 2 * i + k
                        dve.wait_ge(gathered[n], 16 * (layer + 1))
                        if k:
                            dve.wait_ge(V["combined"], 2 * NT * layer + n)
                        ve.scalar_tensor_tensor(h[:, i, :], y_rows[n], w12[:, k, i:i + 1], h[:, i, :],
                                                ALU.mult, ALU.add).then_inc(V["combined"], 1)

            router_weights(0)
            norm_scale(1)
            diagonals()
            transposed_lo(2, 1)
            router(0)
            experts(0)

            B = L_BLOCKS
            split(B)
            combine(0)
            norm_scale(2)
            diagonals()
            split(B + 1)
            transposed_lo(3, 2)
            for n in range(2, 10):
                split(B + n)
            transposed_lo(4, 3)
            for n in range(10, 14):
                split(B + n)

            def log_om(hd, r):
                for p, cols in enumerate(ZPARTS):
                    dve.wait_ge(M["z_done"], 2 * hd + (p + 1))
                    ve.tensor_scalar(zt[r][:, cols].bitcast(I32), z_of(r)[:, cols].bitcast(I32), 0x7FFFFFFF, None,
                                     ALU.bitwise_and).then_inc(V["z_abs"], 1)
                for p, cols in enumerate(ZPARTS):
                    dve.wait_ge(A["z_ln"], 2 * hd + (p + 1))
                    ve.scalar_tensor_tensor(zt[r][:, cols], z_of(r)[:, cols], 0.0, zt[r][:, cols], ALU.max,
                                            ALU.add).then_inc(V["L_done"], 1)

            def L_lo(hd, r):
                for p, cols in enumerate(ZPARTS):
                    dve.wait_ge(A["L_hi_done"], 2 * hd + (p + 1))
                    ve.tensor_tensor(s_lo[:, cols], zt[r][:, cols], s_hi[:, cols], ALU.subtract).then_inc(V["L_lo_done"], 1)

            def oT_lo(q, b):
                dve.wait_ge(A["oT_hi_done"], q + 1)
                hi, lo = (t[:, bass.ds(q, 1), :].rearrange("p o t -> p (o t)") for t in (xT_hi, xT_lo))
                ve.tensor_tensor(lo, ps[:, 6 + b, :], hi, ALU.subtract).then_inc(V["oT_lo_done"], 1)

            log_om(0, 0)
            L_lo(0, 0)
            log_om(1, 1)

            def head(hd, r, pair, more=2):
                if more > 0:
                    L_lo(hd + 1, (r + 1) % 2)
                if more > 1:
                    log_om(hd + 2, r % 2)
                if r % 2:
                    oT_lo(pair, r // 2)

            for hd in range(4):
                head(hd, hd, hd // 2)
            with dve.Fori(1, 3) as g:
                for r in range(4):
                    head(4 * g + r, r, 2 * g + r // 2)
            for hd in range(12, 16):
                head(hd, hd - 12, hd // 2, 15 - hd)
            split(B + 14)
            add_panel(14, B + 13, 0)
            split(B + 15)
            split(B + 16)
            add_panel(15, B + 15, 1)
            split(B + 17)
            router_weights(1)
            norm_scale(3)
            diagonals()
            transposed_lo(5, 4)
            router(1)
            experts(1)
            combine(1)
            norm_scale(4)
            normed(2)

        @block.tensor
        def _(pe):
            def three(o, a_hi, a_lo, b_hi, b_lo, start, stop):
                te.matmul(o, a_hi, b_hi, start=start, stop=False)
                te.matmul(o, a_hi, b_lo, start=False, stop=False)
                return te.matmul(o, a_lo, b_hi, start=False, stop=stop)

            def transposed(turn, event=None, use=lambda k: None):
                if event is not None:
                    pe.wait_ge(V["diag_ready"], NT * (event + 1))
                for k in range(KT):
                    if k >= 4:
                        pe.wait_ge(V["xT_lo_done"], KT * turn + k - 3)
                    for i in range(NT):
                        o, cols = ps[:, k % 4, P * i:P * (i + 1)], slice(P * k, P * (k + 1))
                        if event is None:
                            ins = te.transpose(o, xn[:, i, cols], ident[:, :])
                        else:
                            ins = te.matmul(o, h[:, i, cols], diag[:, i, :], start=True, stop=True)
                    ins.then_inc(M["xT_tr"], 1)
                    if k >= 4:
                        use(k - 4)
                for k in range(KT - 4, KT):
                    pe.wait_ge(V["xT_lo_done"], KT * turn + k + 1)
                    use(k)

            def dense(p, c, feature_major):
                for n in (0, 1):
                    pe.wait_ge(V["lo_done"], c + n + 1)
                    for kk in range(BK):
                        k = BK * n + kk
                        for j in range(4):
                            part = slice(P * j, P * (j + 1))
                            wide = slice(BN * kk, BN * (kk + 1))
                            cols = slice(BN * kk + P * j, BN * kk + P * (j + 1))
                            o = ps[:, 4 * (p % 2) + j, :]
                            s = split_slot(c + n)
                            if feature_major:
                                ops = w_hi[:, s, cols], w_lo[:, s, cols], xT_hi[:, k, :], xT_lo[:, k, :]
                            else:
                                ops = xT_hi[:, k, part], xT_lo[:, k, part], w_hi[:, s, wide], w_lo[:, s, wide]
                            ins = three(o, *ops, start=k == 0, stop=k == KT - 1)
                    ins.then_inc(M["blk_used"], 1)

            pe.wait_ge(G["consts"], 1)
            pe.wait_ge(A["small_loaded"], 16 * 9)
            te.transpose(ps[:, 7, 0:5 * KT], gain_rows, ident[0:5 * KT, 0:5 * KT]).then_inc(M["gains_tr"], 1)

            def gate_input(k):
                ins = three(ps[0:RANK, 7, :], lr_hi[:, k, :], lr_lo[:, k, :], xT_hi[:, k, :], xT_lo[:, k, :],
                            start=k == 0, stop=k == KT - 1)
                if k == KT - 1:
                    ins.then_inc(M["lr_done"], 1)

            pe.wait_ge(V["lr_lo_done"], 1)
            transposed(0, 0, gate_input)
            pe.wait_ge(V["lr_out"], 1)
            for i in range(GH):
                ins = te.matmul(ps[:, 4 + i, :], wgk2[:, DK * i:DK * (i + 1)], lrT, start=True, stop=True)
            ins.then_inc(M["gates_done"], 1)
            dense(0, 0, True)
            pe.wait_ge(V["gates_in"], GH)
            dense(1, 2, True)
            pe.wait_ge(A["panel_out"], 1)
            dense(2, 4, False)
            pe.wait_ge(A["panel_out"], 2)
            dense(3, 6, False)
            pe.wait_ge(V["k_toend"], 1)
            pe.wait_ge(A["panel_out"], 3)
            for i in range(NT):
                for j in range(GH):
                    ins = te.transpose(ps[:, i, P * j:P * (j + 1)], kT[:, j, P * i:P * (i + 1)], ident[:, :])
            ins.then_inc(M["ktok_tr"], 1)
            pe.wait_ge(V["k_inv"], 1)
            pe.wait_ge(A["panel_out"], 4)
            for i in range(NT):
                for j in range(GH):
                    t = slice(P * i, P * (i + 1))
                    ins = te.matmul(ps[:, 4 + i, P * j:P * (j + 1)], kinv[:, j, t], qT[:, j, t], start=True, stop=True)
            ins.then_inc(M["att_done"], 1)
            ktok = gate
            att = kT
            pe.wait_ge(A["ktok_out"], 1)
            for i in range(NT):
                for c in (2 * i, 2 * i + 1):
                    if c == NCH - 1:
                        continue
                    if c >= 2:
                        pe.wait_ge(V["state_done"], GH * (c - 1))
                    rows = slice(CHUNK * (c % 2), CHUNK * (c % 2 + 1))
                    for j in range(GH):
                        a = 1024 * (c % 2) + DV * j
                        ins = te.matmul(psf[:, a:a + DV], ktok[rows, i, DK * j:DK * (j + 1)],
                                        v[rows, i, DV * j:DV * (j + 1)], start=True, stop=True)
                    ins.then_inc(M["upd_done"], 1)
                if i == 0:
                    pe.wait_ge(G["masked"], 2)
                if i >= 2:
                    pe.wait_ge(A["o_out"], i - 1)
                o0 = 2048 + 1024 * (i % 2)
                for j in range(GH):
                    te.matmul(psf[:, o0 + DV * j:o0 + DV * (j + 1)], att[:, i, P * j:P * (j + 1)],
                              v[:, i, DV * j:DV * (j + 1)], start=j % 2 == 0, stop=True, skip_group_check=True)
                for c in (2 * i, 2 * i + 1):
                    if c == 0:
                        continue
                    pe.wait_ge(V["state_done"], GH * c)
                    rows = slice(CHUNK * (c % 2), CHUNK * (c % 2 + 1))
                    for j in range(GH):
                        ins = te.matmul(psf[rows, o0 + DV * j:o0 + DV * (j + 1)],
                                        qT[:, j, CHUNK * c:CHUNK * (c + 1)], state[:, c % 2, j, :],
                                        start=False, stop=True, skip_group_check=True)
                    ins.then_inc(M["inter_done"], 1)
            dense(4, 8, False)
            pe.wait_ge(A["o_out"], NT)
            dense(5, 10, False)
            pe.wait_ge(V["og_ready"], NT)
            transposed(1)
            dense(6, 12, False)
            dense(7, 14, False)

            def x_transposed(S, i, slot, loads, reuse=True):
                pe.wait_ge((S["x_loaded0"], S["x_loaded1"])[slot], 16 * loads)
                for f in (0, 1):
                    if reuse:
                        pe.wait_ge(S["x_lo"], 2 * i + (f - 1))
                    for k in range(4):
                        ins = te.transpose(ps[:, 4 + f, CAP * k:CAP * (k + 1)],
                                           xg[:, slot, P * (4 * f + k):P * (4 * f + k + 1)], ident[0:CAP, 0:CAP])
                    ins.then_inc(S["x_tr"], 1)

            def up_block(which, half, slot, used):
                for kk in range(BK):
                    k = BK * half + kk
                    wide = slice(BN * kk, BN * (kk + 1))
                    ins = three(ps[0:CAP, which, :], xg_hi[:, k, :], xg_lo[:, k, :], hi_slots[slot][:, wide],
                                lo_slots[slot][:, wide], start=k == 0, stop=k == KT - 1)
                ins.then_inc(used, 1)

            def down_block(half, slot, used):
                for kk in range(BK):
                    wide = slice(BN * kk, BN * (kk + 1))
                    ins = three(ps[0:CAP, 2 + half, :], ht_hi[:, kk, :], ht_lo[:, kk, :], hi_slots[slot][:, wide],
                                lo_slots[slot][:, wide], start=kk == 0, stop=kk == BK - 1)
                ins.then_inc(used, 1)

            def h_transposed(S, i, reuse=True):
                pe.wait_ge(S["mul"], i + 1)
                if reuse:
                    pe.wait_ge(S["h_lo"], i)
                for k in range(BK):
                    ins = te.transpose(ps[:, 6, CAP * k:CAP * (k + 1)], hid[:, P * k:P * (k + 1)], ident[0:CAP, 0:CAP])
                ins.then_inc(S["h_tr"], 1)

            def experts(layer):
                B, I = blocks_of(layer), NE * layer
                first_load = 8 * layer + 1

                def up(i, c, g=0, reuse=True):
                    pe.wait_ge(E["x_lo"], 2 * i + 2)
                    for n in range(4):
                        if n == 0 and reuse:
                            pe.wait_ge(E["silu"], i)
                        if n == 2 and reuse:
                            pe.wait_ge(E["mul"], i)
                        pe.wait_ge(V["lo_done"], number(c + n + 1, g))
                        up_block(n // 2, n % 2, split_slot(c + n), M["blk_used"])

                def down(i, c, g=0):
                    pe.wait_ge(E["h_lo"], i + 1)
                    for n in range(2):
                        pe.wait_ge(V["lo_done"], number(c + n + 1, g))
                        down_block(n, split_slot(c + n), M["blk_used"])

                x_transposed(E, I, 0, first_load, layer > 0)
                up(I, B, 0, layer > 0)
                x_transposed(E, I + 1, 1, first_load)
                h_transposed(E, I, layer > 0)
                with pe.Fori(0, PAIRS) as g:
                    for k in range(2):
                        i, c = 2 * g + (I + 1 + k), B + 4 + E_BLOCKS * k
                        up(i, c, g)
                        x_transposed(E, i + 1, k, g + (first_load + 1))
                        down(i - 1, c + 4, g)
                        h_transposed(E, i)
                i, c = I + NE - 1, B + LAST
                up(i, c)
                down(i - 1, c + 4)
                h_transposed(E, i)
                down(i, c + 6)

                S, W = O[layer], OW[layer]

                def tile(j):
                    pe.wait_ge(E["y_out"], NE * (layer + 1))
                    pe.wait_ge(S["turn"], j + 1)
                    x_transposed(S, j, 0, j + 1, False)
                    pe.wait_ge(S["x_lo"], 2 * j + 2)
                    for b in range(6):
                        pe.wait_ge(W["lo"], 6 * j + (b + 1))
                        if b == 4:
                            pe.wait_ge(S["h_lo"], j + 1)
                        if b < 4:
                            up_block(b // 2, b % 2, b % SPLIT, W["used"])
                        else:
                            down_block(b - 4, b % SPLIT, W["used"])
                        if b == 3:
                            h_transposed(S, j, False)

                over_loop(pe, layer, tile)

            def logits(k):
                ins = three(ps[0:NR, 7, :], r_hi[:, k, :], r_lo[:, k, :], xT_hi[:, k, :], xT_lo[:, k, :],
                            start=k == 0, stop=k == KT - 1)
                if k == KT - 1:
                    ins.then_inc(M["logits_done"], 1)

            def router(layer):
                pe.wait_ge(A["logits_out"], layer + 1)
                for i in range(NT):
                    ins = te.transpose(ps[:, 6, NR * i:NR * (i + 1)], logitsT[:, P * i:P * (i + 1)], ident[0:NR, 0:NR])
                ins.then_inc(M["logits_tr"], 1)
                pe.wait_ge(V["sel_ready"], layer + 1)
                for i in range(NT):
                    o = ps[:, 5, NE * i:NE * (i + 1)]
                    for j in range(i):
                        te.matmul(o, ones_b[:, :], sel_b[:, j, :], start=j == 0, stop=False)
                    te.matmul(o, before[:, :], sel_b[:, i, :], start=i == 0, stop=True)
                o = ps[:, 5, NE * NT:NE * (NT + 1)]
                for j in range(NT):
                    ins = te.matmul(o, ones_b[:, :], sel_b[:, j, :], start=j == 0, stop=j == NT - 1)
                ins.then_inc(M["ranks_done"], 1)
                pe.wait_ge(V["places_ready"], 2 * layer + 2)
                for n in range(2 * NT):
                    ins = te.matmul(ps[0:CAP, 4, 0:TILES], at_row[:, n, :], at_tile_t[:, n, :], start=n == 0,
                                    stop=n == 2 * NT - 1)
                ins.then_inc(M["lists_done"], 1)

            pe.wait_ge(V["r_lo_done"], 1)
            transposed(2, 1, logits)
            router(0)
            experts(0)

            B = L_BLOCKS
            transposed(3, 2)
            dense(8, B, True)
            dense(9, B + 2, True)
            pe.wait_ge(A["panel_out"], 7)
            dense(10, B + 4, False)
            pe.wait_ge(A["panel_out"], 8)
            dense(11, B + 6, False)
            pe.wait_ge(A["panel_out"], 9)
            transposed(4, 2)
            dense(12, B + 8, True)
            pe.wait_ge(A["panel_out"], 10)
            dense(13, B + 10, True)

            def scores(hd, r, b, pair, reuse=True):
                pe.wait_ge(G["staged"], 3 * pair + 2)
                rows = slice(SD * r, SD * (r + 1))
                for p, blocks in enumerate(ZBLOCKS):
                    if reuse:
                        pe.wait_ge(A["weights_done"], 2 * hd + (p - 3))
                    for i in blocks:
                        z = z_of(r)[:, ZO[i]:ZO[i] + ZW[i]]
                        te.matmul(z, kst[rows, b, P * i:P * (i + 1)], qst[rows, b, P * i:T], start=i != 3, stop=True,
                                  skip_group_check=True)
                    for i in blocks:
                        ins = te.matmul(z_of(r)[:, ZO[i]:ZO[i] + P], ident_b[:, :], neg_mask[:, :], start=False, stop=True,
                                        skip_group_check=True)
                    ins.then_inc(M["z_done"], 1)

            def sums(hd, r):
                for p, blocks in enumerate(ZBLOCKS):
                    pe.wait_ge(V["L_lo_done"], 2 * hd + (p + 1))
                    for i in sorted(blocks):
                        for j in range(NT - 1, i - 1, -1):
                            o = z_of(r)[:, ZO[i] + P * (j - i):ZO[i] + ZW[i]]
                            for part in (s_hi, s_lo):
                                ins = te.matmul(o, (neg_tri if i == j else neg_one)[:, :], part[:, ZO[j]:ZO[j] + ZW[j]],
                                                start=False, stop=True, skip_group_check=True)
                    ins.then_inc(M["sums_done"], 1)

            def values(hd, r, b, pair, reuse=True):
                pe.wait_ge(A["weights_done"], 2 * hd + 2)
                pe.wait_ge(G["staged"], 3 * pair + 3)
                if reuse:
                    pe.wait_ge(V["oT_lo_done"], pair - 1)
                rows = slice(SD * r, SD * (r + 1))
                for j in range(NT):
                    ins = te.matmul(ps[rows, 6 + b, P * j:T], vst[:, b, j, SD * r:SD * (r + 1)],
                                    wt[r][:, ZO[j]:ZO[j] + ZW[j]], start=j == 0, stop=j == NT - 1,
                                    skip_group_check=True)
                ins.then_inc(M["av_done"], 1)

            scores(0, 0, 0, 0, False)
            scores(1, 1, 0, 0, False)

            def head(hd, r, pair, reuse=True, more=True):
                sums(hd, r % 2)
                if more:
                    scores(hd + 2, r % 2, (r // 2 + 1) % 2, pair + 1)
                values(hd, r % 2, r // 2, pair, reuse)

            for hd in range(4):
                head(hd, hd, hd // 2, False)
            with pe.Fori(1, 3) as g:
                for r in range(4):
                    head(4 * g + r, r, 2 * g + r // 2)
            for hd in range(12, 16):
                head(hd, hd - 12, hd // 2, more=hd < 14)
            pe.wait_ge(V["oT_lo_done"], 8)
            dense(14, B + 12, False)
            dense(15, B + 14, False)
            pe.wait_ge(V["r_lo_done"], 2)
            transposed(5, 3, logits)
            router(1)
            experts(1)

        @block.gpsimd
        def _(pool):
            link = Chain(pool, G["pool_chain"])
            gains = [m_norm[0], m_norm[1], final_norm]

            def load_gain(use):
                if use:
                    pool.wait_ge(V["xn_ready"], NT * use)
                pool.dma_start(gain[:, :], gains[use].partition_broadcast(P)).then_inc(G["gain_loaded"], 16)

            ge.memset(zeros[:, :], 0.0)
            def select(dst, src, op, fill, step, channel, base=0):
                return ge.affine_select(out=dst, in_=src, compare_op=op, fill=fill, base=base,
                                        pattern=[[step, dst.shape[-1]]], channel_multiplier=channel)

            for t, val in ((ident, 0.0), (ident_b, 0.0), (neg_mask, 0.0), (before, 1.0), (ones_b, 1.0), (one16, 1.0)):
                ge.memset(t[:, :], val)
            ge.memset(neg_tri[:, :].bitcast(F32), -1.0)
            ge.memset(neg_one[:, :].bitcast(F32), -1.0)
            link(ge.memset(reset, 1.0))
            select(ident[:, :], ident[:, :], ALU.not_equal, 1.0, -1, 1)
            select(ident_b[:, :], ident_b[:, :], ALU.not_equal, 1.0, -1, 1)
            select(neg_mask[:, :], neg_mask[:, :], ALU.is_gt, -1e30, 1, -1)
            select(before[:, :], before[:, :], ALU.is_gt, 0.0, 1, -1)
            select(neg_tri[:, :], neg_tri[:, :].bitcast(F32), ALU.is_ge, 0.0, -1, 1)
            ge.memset(reset.rearrange("p (c t) -> p c t", t=CHUNK)[:, :, 0:1], 0.0)
            for t, step, base, channel in ((desc4, -1, NG, 0), (desc16, -1, NE, 0), (caps, CAP, CAP, 0),
                                           (index, 1, 0, 0), (token_id, P, 0, 1)):
                last = ge.iota(t[:, :], pattern=[[step, t.shape[-1]]], base=base, channel_multiplier=channel,
                               allow_small_or_imprecise_dtypes=True)
            last.then_inc(G["consts"], 1)
            load_gain(0)
            pool.wait_ge(A["panel_out"], 1)
            zero_row = zeros[0:CAP, :].unsqueeze(1).broadcast_to([CAP, D // 256, 256])
            with pool.Fori(0, MAX_OVER) as i:
                pool.dma_start(table[bass.ds((i + NE) * CAP, CAP), :].rearrange("p (r n) -> p r n", n=256),
                               zero_row).then_inc(G["zeroed"], 16)
            pool.wait_ge(V["att_out"], 1)
            att3 = kT.rearrange("p h t -> p (h t)").rearrange("p (a q) -> p a q", q=P)
            ge.affine_select(out=att3, in_=att3, compare_op=ALU.is_ge, fill=0.0, base=0,
                             pattern=[[0, NT * GH], [1, P]], channel_multiplier=-1).then_inc(G["masked"], 1)
            pool.wait_ge(G["masked"], 1)
            ge.memset(att3[0:CHUNK, :, CHUNK:P], 0.0).then_inc(G["masked"], 1)
            pool.wait_ge(A["panel_out"], 6)
            sg3 = sg.rearrange("p i (j e) -> p (i j) e", e=DV)
            ge.tensor_tensor(sg3, sg3, onorm.unsqueeze(1).broadcast_to([P, NT * GH, DV]), ALU.mult).then_inc(G["sg_ready"], 1)

            def experts(layer):
                I = NE * layer

                def gather(S, column, slot):
                    pool.indirect_dma_start(out=xg[:, slot, :], out_offset=None, in_=rows,
                                            in_offset=bass.IndirectOffsetOnAxis(ap=column, axis=0)).then_inc((S["x_loaded0"], S["x_loaded1"])[slot], 16)

                def column_copy(S, tile, slot):
                    ge.tensor_copy(token_now[:, slot:slot + 1], token[:, bass.ds(tile, 1)]).then_inc(S["column"], 1)

                pool.wait_ge(V["tokens_ready"], layer + 1)
                pool.wait_ge(A["rows_stored"], 16 * NT * (layer + 1))
                for slot in (0, 1):
                    gather(E, token[:, slot:slot + 1], slot)
                load_gain(layer + 1)

                def store(S, row):
                    pool.dma_start(table[bass.ds(row, CAP), :], y_sb).then_inc(S["y_stored"], 16)

                with pool.Fori(0, PAIRS) as g:
                    for k in range(2):
                        i = 2 * g + (1 + k)
                        pool.wait_ge(E["x_tr"], 2 * i + 2 * I)
                        column_copy(E, i + 1, k)
                        pool.wait_ge(E["column"], i + (NE - 2) * layer)
                        pool.sem_inc(E["column_seen"], 1)
                        gather(E, token_now[:, k:k + 1], k)
                        pool.wait_ge(E["y_out"], i + I)
                        store(E, (i - 1) * CAP)
                for i in (NE - 2, NE - 1):
                    pool.wait_ge(E["y_out"], I + i + 1)
                    store(E, i * CAP)
                pool.wait_ge(E["y_stored"], 16 * (I + NE))
                S = O[layer]

                def tile(j):
                    column_copy(S, j + NE, 0)
                    pool.wait_ge(S["column"], j + 1)
                    pool.sem_inc(S["column_seen"], 1)
                    gather(S, token_now[:, 0:1], 0)
                    pool.wait_ge(S["y_out"], j + 1)
                    pool.sem_inc(S["out_seen"], 1)
                    store(S, (j + NE) * CAP)
                    pool.wait_ge(S["y_stored"], 16 * j + 16)
                    pool.sem_inc(S["turn"], 1)

                pool.sem_inc(S["turn"], 1)
                over_loop(pool, layer, tile)
                pool.sem_inc(G["over_ended"], 1)
                for i in range(NT):
                    for k in range(2):
                        n = 2 * i + k
                        pool.indirect_dma_start(out=y_rows[n], out_offset=None, in_=table,
                                                in_offset=bass.IndirectOffsetOnAxis(ap=pos[:, k, i:i + 1], axis=0)).then_inc(gathered[n], 16)

            experts(0)
            pool.wait_ge(A["panel_out"], 12)

            def stage_qk(q, b):
                ge.tensor_copy(kst[:, b, :], kT1[:, bass.ds(q, 1), :].rearrange("p o t -> p (o t)")).then_inc(G["staged"], 1)
                ge.tensor_copy(qst[:, b, :], qT1[:, bass.ds(q, 1), :].rearrange("p o t -> p (o t)")).then_inc(G["staged"], 1)

            def stage_v(q, b):
                ge.tensor_copy(vst[:, b, :, :], v[:, :, bass.ds(q * P, P)]).then_inc(G["staged"], 1)

            for q in (0, 1):
                stage_qk(q, q)
                stage_v(q, q)
            with pool.Fori(1, 4) as g:
                for b in range(2):
                    pool.wait_ge(M["z_done"], 8 * g + (4 * b - 4))
                    stage_qk(2 * g + b, b)
                    pool.wait_ge(M["av_done"], 4 * g + (2 * b - 2))
                    stage_v(2 * g + b, b)
            experts(1)


_INS = ["x", "a_norm", "a_w_in", "a_w_gk2", "a_b_gk2", "a_o_norm", "a_w_out", "kv_norm", "w_kv", "b_norm",
        "b_w_q", "b_w_out", "m_norm", "m_w_group", "m_b_group", "m_w_expert", "m_b_expert", "m_w_gate",
        "m_w_up", "m_w_down", "final_norm"]


def kernel(**inputs):
    import numpy as np
    import concourse.bacc as bacc
    from concourse.bass_utils import run_bass_kernel_spmd

    nc = bacc.Bacc("TRN2", target_bir_lowering=False, num_devices=1)
    arrays, args = {}, []
    for name in _INS:
        a = np.ascontiguousarray(inputs[name])
        arrays[f"in_{name}"] = a
        args.append(nc.dram_tensor(f"in_{name}", a.shape, mybir.dt.from_np(a.dtype), kind="ExternalInput").ap())
    args.append(nc.dram_tensor("out_h", [1, T, D], F32, kind="ExternalOutput").ap())
    trunk(nc, *args)
    return run_bass_kernel_spmd(nc, [arrays], core_ids=[0]).results[0]["out_h"]
```

```python
from contextlib import ExitStack

import concourse.bass as bass
import numpy as np
from concourse import mybir

F32 = mybir.dt.float32
F32R = mybir.dt.float32r
BF16 = mybir.dt.bfloat16
I32 = mybir.dt.int32
U32 = mybir.dt.uint32
ALU = mybir.AluOpType
ACT = mybir.ActivationFunctionType
AX = mybir.AxisListType

P = 128
D = 1024
T = 512
NT = T // P
KT = D // P
EPS = 1e-6
LAYERS = 2

GH, DK, DV, RANK, CHUNK = 4, 128, 256, 16, 64
GATE_NORM = 16.0
QK = GH * DK
GK0 = 2 * QK + D
G0 = GK0 + RANK
NCH = T // CHUNK

SH, SD = 16, 64
ZW = [T - P * i for i in range(NT)]
ZO = [0, T, 2 * T, 2 * T - P]
ZC = 2 * T + 2 * P
ZPARTS = [slice(T, ZC), slice(0, T)]
ZBLOCKS = [(1, 3, 2), (0,)]

NG, EG = 4, 4
NE = NG * EG
F = 512
NR = NG + NE
CAP = 96
MAX_OVER = 10
TILES = NE + MAX_OVER
ROWS = TILES * CAP
STEPS_OVER = (T - 1) // CAP

BK = 4
BN = 512
BW = BK * BN
RAW, RAW_E = 4, 6
SPLIT, SPLIT_E = 2, 4
A_BLOCKS = 16
E_BLOCKS = 6
L_BLOCKS = A_BLOCKS + NE * E_BLOCKS

SMALL = 9


class Chain:

    def __init__(self, eng, sem):
        self.eng, self.sem, self.n = eng, sem, 0

    def __call__(self, *instructions):
        for ins in instructions:
            ins.then_inc(self.sem, 1)
        self.n = self.n + len(instructions)
        self.eng.wait_ge(self.sem, self.n)


def trunk(nc, x, a_norm, a_w_in, a_w_gk2, a_b_gk2, a_o_norm, a_w_out, kv_norm, w_kv, b_norm, b_w_q,
          b_w_out, m_norm, m_w_group, m_b_group, m_w_expert, m_b_expert, m_w_gate, m_w_up, m_w_down,
          final_norm, out):
    with ExitStack() as ctx:
        def sb(name, shape, dt=F32):
            return ctx.enter_context(nc.sbuf_tensor(name, shape, dt))

        def sem(name):
            return ctx.enter_context(nc.semaphore(name))

        rows = nc.dram_tensor("normed_rows", [T, D], F32).ap()
        table = nc.dram_tensor("output_table", [ROWS, D], F32).ap()
        h = sb("h", [P, NT, D])
        xn = sb("xn", [P, NT, D])
        xT_hi = sb("xT_hi", [P, KT, T], F32R)
        xT_lo = sb("xT_lo", [P, KT, T], F32R)
        raw = sb("raw", [P, RAW, BW])
        w_hi = sb("w_hi", [P, SPLIT, BW], F32R)
        w_lo = sb("w_lo", [P, SPLIT, BW], F32R)
        s_hi = sb("s_hi", [P, ZC], F32R)
        s_lo = sb("s_lo", [P, ZC], F32R)
        r_hi = sb("r_hi", [P, KT, NR], F32R)
        r_lo = sb("r_lo", [P, KT, NR], F32R)
        gain = sb("gain", [P, D])
        pad = sb("pad", [P, 14336 + DV])
        zeros = sb("zeros", [P, 256])
        ident = sb("ident", [P, P])
        ident_b = sb("ident_b", [P, P], BF16)
        neg_mask = sb("neg_mask", [P, P], BF16)
        before = sb("before", [P, P], BF16)
        ones_b = sb("ones_b", [P, P], BF16)
        neg_tri = sb("neg_tri", [P, P], F32R)
        neg_one = sb("neg_one", [P, P], F32R)
        lr_raw = sb("lr_raw", [P, KT, RANK])
        bgk = sb("bgk", [P, GH])
        r_raw = sb("r_raw", [P, LAYERS, KT, NR])
        r_bias = sb("r_bias", [P, LAYERS, NR])
        ss = sb("ss", [P, 16])
        ms = sb("ms", [P, 16])
        y0 = sb("y0", [P, 16])
        y1 = sb("y1", [P, 16])
        rstd = sb("rstd", [P, 16])
        decay = sb("decay", [P, GH, NCH])
        w12 = sb("w12", [P, 2, NT])
        pos = sb("pos", [P, 2, NT], U32)
        token = sb("token", [CAP, TILES], U32)
        token_now = sb("token_now", [CAP, 2], U32)
        gainT = sb("gainT", [P, 5 * KT])
        over = sb("over", [1, MAX_OVER + 1], I32)

        def region(start, width):
            return pad[:, start:start + width]

        raw_slots = [raw[:, s, :] for s in range(RAW)] + [
            xn[:, 2 * s:2 * s + 2, :].rearrange("p i n -> p (i n)") for s in range(RAW_E - RAW)]
        hi_slots, lo_slots = ([w[:, s, :] for s in range(SPLIT)] + [
            x_t[:, BK * s:BK * (s + 1), :].rearrange("p k t -> p (k t)") for s in range(SPLIT_E - SPLIT)]
            for w, x_t in ((w_hi, xT_hi), (w_lo, xT_lo)))
        qT = region(0, 2048).rearrange("p (h t) -> p h t", h=GH)
        kT = region(2048, 2048).rearrange("p (h t) -> p h t", h=GH)
        kinv = region(4096, 2048).rearrange("p (h t) -> p h t", h=GH)
        gate = region(6144, 2048).rearrange("p (h t) -> p h t", h=GH)
        lrT = pad[0:RANK, 4096:4096 + T]
        wgk2 = pad[0:RANK, 4096 + T:4096 + 2 * T]
        v = region(8192, 4096).rearrange("p (i n) -> p i n", i=NT)
        state = region(12288, 2048).rearrange("p (b h e) -> p b h e", b=2, h=GH)
        reset = region(12288, T)
        onorm = region(14336, DV)
        sg = raw[:, 2:4, :].rearrange("p s n -> p (s n)").rearrange("p (i n) -> p i n", i=NT)
        cum = xn[:, 0:2, :].rearrange("p a (b t) -> p (a b) t", b=2)
        kT1 = region(0, 4096).rearrange("p (q t) -> p q t", q=KT)
        qT1 = region(4096, 4096).rearrange("p (q t) -> p q t", q=KT)
        kst = region(12288, 2 * T).rearrange("p (b t) -> p b t", b=2)
        qst = [region(12288 + 2 * T, 2 * T).rearrange("p (b t) -> p b t", b=2),
               gain[:, :].rearrange("p (b t) -> p b t", b=2)]
        xnf = xn[:, :, :].rearrange("p i n -> p (i n)")
        vst = xnf[:, 2 * ZC:2 * ZC + 2 * T].rearrange("p (b i e) -> p b i e", b=2, i=NT)
        zt = [xnf[:, 0:ZC], xnf[:, ZC:2 * ZC]]
        wt = [raw[:, 0, 0:ZC], raw[:, 1, 0:ZC]]
        xg = pad[0:CAP, 0:2 * D].rearrange("p (b n) -> p b n", b=2)
        sil = pad[0:CAP, 2048:2048 + F]
        hid = pad[0:CAP, 2560:2560 + F]
        y_sb = pad[0:CAP, 3072:3072 + D]
        over_raw = region(4096, BW)
        y_rows = [xn[:, i, :] for i in range(NT)] + [
            xT_hi[:, 2 * i:2 * i + 2, :].rearrange("p k t -> p (k t)").bitcast(F32) for i in range(NT)]
        xg_hi, xg_lo = (t[:, 0:KT * CAP].rearrange("p (k c) -> p k c", k=KT) for t in (s_hi, s_lo))
        ht_hi, ht_lo = (t[:, KT * CAP:(KT + BK) * CAP].rearrange("p (k c) -> p k c", k=BK)
                        for t in (s_hi, s_lo))
        lr_hi, lr_lo = (t[:, 0:KT * RANK].rearrange("p (k c) -> p k c", k=KT) for t in (s_hi, s_lo))
        diag = region(13312 + P, NT * P).rearrange("p (i t) -> p i t", i=NT)
        gain_rows = pad[0:5 * KT, 13312:13312 + P]
        free = [6144]

        def scratch(*shape):
            n = int(np.prod(shape))
            free[0] += n
            t = region(free[0] - n, n)
            if len(shape) == 2:
                return t.rearrange("p (a b) -> p a b", b=shape[1])
            return t.rearrange("p (a b c) -> p a b c", b=shape[1], c=shape[2]) if len(shape) == 3 else t

        lg = scratch(NT, NR)
        gd, geq, gv, goh, gneg = (scratch(NT, NG) for _ in range(5))
        em, eq, ev, em2 = (scratch(NT, NE) for _ in range(4))
        oh = scratch(2, NT * NE)
        oh_k = oh.rearrange("p k (i e) -> p (k i) e", e=NE)
        rank, tmp_rank, tmp_base = scratch(2, NT * NE), scratch(2 * NT, NE), scratch(2 * NT, NE)
        gm, gvm, gs, gw, dd, ex, denom, rs = (scratch(NT) for _ in range(8))
        m12, evm = scratch(2, NT), scratch(2, NT)
        cnt, ovn, ovend, ovbase = (scratch(NE) for _ in range(4))
        cnt_over = scratch(NE, STEPS_OVER)
        e_k, rank_k, o_k, base_k, tile_k, row_k, step_k, p_k = (scratch(2 * NT) for _ in range(8))
        rank_over = scratch(2 * NT, STEPS_OVER)
        at_row, at_tile, at_tile_t = scratch(2 * NT, CAP), scratch(2 * NT, TILES), scratch(2 * NT, TILES)
        over_cmp, over_f = scratch(MAX_OVER, NE), scratch(MAX_OVER + 1)
        logitsT = pad[0:NR, 9216:9216 + T]
        desc4 = sb("desc4", [P, NG])
        desc16 = sb("desc16", [P, NE])
        caps = sb("caps", [P, STEPS_OVER])
        index = sb("index", [P, CAP])
        parity = sb("parity", [P, 2])
        token_id = sb("token_id", [P, NT])
        one16 = sb("one16", [P, NE])
        sel_b = sb("sel_b", [P, NT, NE], BF16)

        ps = ctx.enter_context(nc.psum_tensor("ps", [P, 8, 512], F32))
        psf = ps[:, :, :].rearrange("p b n -> p (b n)")

        def sems(names):
            return {n: sem(n) for n in names.split()}

        x_loaded = [sem(f"x_loaded{i}") for i in range(NT)]
        raw_loaded = [sem(f"raw_loaded{i}") for i in range(RAW_E)]
        out_stored = sem("out_stored")
        A = sems("small_loaded hi_done act_chain ssq_done rs_first xT_hi_done panel_out lr_hi_done "
                 "gate_ln gate_exp ktok_out half_squared o_squared xn_scaled r_hi_done router_exp z_exp z_ln L_hi_done "
                 "weights_done oT_hi_done logits_out router_loaded rows_stored")
        V = sems("lo_done dve_chain gains_out ms_ready diag_ready xn_ready xT_lo_done h_half lr_lo_done lr_out gates_in "
                 "gate_abs gate_cum q_dec k_inv gate_toend k_toend att_out state_done og_ready r_lo_done "
                 "group_diff second_diff sel_ready places_ready tokens_ready pos_ready combined rstd_ready z_abs L_done L_lo_done oT_lo_done")
        M = sems("gains_tr blk_used xT_tr lr_done gates_done ktok_tr att_done upd_done inter_done logits_done logits_tr "
                 "ranks_done lists_done z_done sums_done av_done")
        G = sems("consts pool_chain masked sg_ready staged gain_loaded zeroed xn_normed over_ended")
        gathered = [sem(f"gathered{i}") for i in range(2 * NT)]

        def expert_sems(tag):
            names = "x_loaded0 x_loaded1 x_tr x_hi x_lo silu mul h_tr h_hi h_lo y_out y_stored turn out_seen column column_seen"
            return {n: sem(f"{tag}_{n}") for n in names.split()}

        E = expert_sems("first")
        O = [expert_sems(f"over{l}") for l in range(LAYERS)]
        OW = [{n: sem(f"over{l}_w_{n}") for n in "loaded hi lo used".split()}
              for l in range(LAYERS)]

        block = ctx.enter_context(nc.Block())
        ve, se, te, ge = nc.vector, nc.scalar, nc.tensor, nc.gpsimd

        def number(c, g=0):
            return 12 * g + c

        def expert_part(c):
            return c % L_BLOCKS - A_BLOCKS, c // L_BLOCKS

        def raw_slot(c):
            e = expert_part(c)[0]
            return e % RAW_E if e >= 0 else (e + A_BLOCKS) % RAW

        def raw_loads(c, g=0):
            e, layer = expert_part(c)
            both = (NE * E_BLOCKS // RAW_E, A_BLOCKS // RAW if raw_slot(c) < RAW else 0)
            n = sum(both) * layer + (e // RAW_E + both[1] if e >= 0 else (e + A_BLOCKS) // RAW)
            return 16 * (12 // RAW_E * g + (n + 1))

        def raw_before(c):
            e = expert_part(c)[0]
            return c - (RAW_E if e >= RAW or e < RAW - A_BLOCKS else RAW)

        def split_slot(c):
            e = expert_part(c)[0]
            return e % SPLIT_E if e >= 0 else (e + A_BLOCKS) % SPLIT

        def split_before(c):
            e = expert_part(c)[0]
            return c - (SPLIT_E if e >= SPLIT or e < SPLIT - A_BLOCKS else SPLIT)

        def panel(w, col, k0):
            return w[k0 * P:(k0 + BK) * P, col:col + BN].rearrange("(k p) n -> p k n", p=P)

        a_cols = [0, QK, 2 * QK, 2 * QK + BN, G0, G0 + BN]
        halves = (0, BK)
        streams = [[panel(a_w_in[0], c, k0) for c in a_cols for k0 in halves]
                   + [panel(a_w_out[0], c, k0) for c in (0, BN) for k0 in halves],
                   [panel(w_kv, c, k0) for c in range(0, 2 * D, BN) for k0 in halves]
                   + [panel(b_w_q[0], c, k0) for c in (0, BN) for k0 in halves]
                   + [panel(b_w_out[0], c, k0) for c in (0, BN) for k0 in halves]]

        def expert_block(layer, kind, e, half):
            w = {"g": m_w_gate, "u": m_w_up, "d": m_w_down}[kind][layer]
            w = w[bass.ds(e, 1), :, :].rearrange("o k n -> (o k) n")
            if kind == "d":
                return w[:, half * BN:(half + 1) * BN].rearrange("(k p) n -> p k n", p=P)
            return w[half * BK * P:(half + 1) * BK * P, :].rearrange("(k p) n -> p k n", p=P)

        def blocks_of(layer):
            return layer * L_BLOCKS + A_BLOCKS

        PAIRS = (NE - 2) // 2
        LAST = 4 + E_BLOCKS * (NE - 2)

        def panel_banks(p):
            return slice(4 * (p % 2), 4 * (p % 2) + 4)

        def z_of(r):
            return psf[:, 1536 * r:1536 * r + ZC]

        def o_of(i):
            return psf[:, 2048 + 1024 * (i % 2):3072 + 1024 * (i % 2)]

        O_NORMS = [(0, GH * (NT - 1)), (GH * (NT - 1), GH * NT)]

        COMBINE = [(i + d, k) for i in range(0, NT, 2) for k in range(2) for d in range(2)]

        def wait_h(eng, event, i):
            if event == 0:
                eng.wait_ge(x_loaded[i], 16)
            else:
                eng.wait_ge(V["combined"], 2 * NT * (event // 2 - 1) + COMBINE.index((i, 1)) + 1)

        pool_engine = nc.gpsimd

        def over_loop(eng, layer, tile):
            eng.wait_ge(V["pos_ready"], layer + 1)
            n = eng.value_load(over[0:1, MAX_OVER:MAX_OVER + 1], min_val=0, max_val=MAX_OVER)
            with eng.If(n > 0):
                with eng.Fori(0, n) as j:
                    tile(j)
            with eng.Else():
                eng.nop()
            if eng.engine != pool_engine.engine:
                eng.wait_ge(G["over_ended"], layer + 1)

        @block.sync
        def _(sp):
            def load(src, c, g=0):
                if raw_before(c) >= 0:
                    sp.wait_ge(V["lo_done"], number(raw_before(c) + 1, g))
                sp.dma_start(raw_slots[raw_slot(c)].rearrange("p (k n) -> p k n", k=BK),
                             src).then_inc(raw_loaded[raw_slot(c)], 16)

            for i in range(NT):
                sp.dma_start(h[:, i, :], x[0, i * P:(i + 1) * P, :]).then_inc(x_loaded[i], 16)
            sp.wait_ge(A["small_loaded"], 16 * SMALL)
            for layer in range(LAYERS):
                for n, src in enumerate(streams[layer]):
                    if layer == 0 and n == A_BLOCKS - 2:
                        sp.wait_ge(V["og_ready"], NT)
                    load(src, layer * L_BLOCKS + n)
                B = blocks_of(layer)
                for n, (kind, half) in enumerate((k, f) for k in "gu" for f in (0, 1)):
                    if layer and n == 0:
                        sp.wait_ge(M["av_done"], SH)
                    load(expert_block(layer, kind, 0, half), B + n)

                sp.wait_ge(A["rows_stored"], 16 * NT * (layer + 1))
                for half in (0, 1):
                    load(expert_block(layer, "g", 1, half), B + 4 + half)
                sp.wait_ge(E["x_loaded0"], 16 * (8 * layer + 1))

                def step(e, c, g=0, last=False):
                    for n, (kind, d) in enumerate((("u", 0), ("d", -1), ("d", 0) if last else ("g", 1))):
                        for half in (0, 1):
                            load(expert_block(layer, kind, e + d, half), c + 2 * n + half, g)

                with sp.Fori(0, PAIRS) as g:
                    for k in range(2):
                        step(2 * g + (k + 1), B + 6 + E_BLOCKS * k, g)
                step(NE - 1, B + LAST + 2, last=True)
            for i in range(NT):
                if i < NT - 1:
                    sp.wait_ge(A["xn_scaled"], 2 * LAYERS + i + 1)
                else:
                    sp.wait_ge(V["xn_ready"], 2 * LAYERS + 1)
                sp.dma_start(out[0, i * P:(i + 1) * P, :], xn[:, i, :]).then_inc(out_stored, 16)
            sp.wait_ge(out_stored, 16 * NT)

        @block.scalar
        def _(act):
            def split(c, g=0):
                act.wait_ge(raw_loaded[raw_slot(c)], raw_loads(c, g))
                if split_before(c) >= 0:
                    act.wait_ge(M["blk_used"], number(split_before(c) + 1, g))
                se.copy(hi_slots[split_slot(c)], raw_slots[raw_slot(c)]).then_inc(A["hi_done"], 1)

            loads = [(lr_raw[:, :, :], a_w_in[0, :, GK0:GK0 + RANK].rearrange("(k p) r -> p k r", p=P))]
            loads += [(gain_rows[KT * n:KT * (n + 1), :], g.rearrange("(k p) -> k p", p=P))
                      for n, g in enumerate((a_norm[0], m_norm[0], kv_norm, b_norm[0], m_norm[1]))]
            loads += [(wgk2, a_w_gk2[0]),
                      (bgk[:, :], a_b_gk2[0].rearrange("(h p) -> p h", p=P)),
                      (onorm, a_o_norm[0].partition_broadcast(P))]
            router_loads = []
            for l in range(LAYERS):
                router_loads += [(r_raw[:, l, :, 0:NG], m_w_group[l].rearrange("(k p) n -> p k n", p=P)),
                                 (r_raw[:, l, :, NG:NR], m_w_expert[l].rearrange("(k p) n -> p k n", p=P)),
                                 (r_bias[:, l, 0:NG], m_b_group[l].partition_broadcast(P)),
                                 (r_bias[:, l, NG:NR], m_b_expert[l].partition_broadcast(P))]

            def load_small(pairs, done):
                with nc.allow_non_contiguous_dma(reason="512 gate biases and 20 router columns a row"):
                    for dst, src in pairs:
                        act.dma_start(dst, src).then_inc(done, 16)

            load_small(loads, A["small_loaded"])

            norms = [0]

            def rsqrt_first(first, last):
                norms[0] += 1
                act.wait_ge(V["ms_ready"], norms[0])
                se.activation(y1[:, first:last], ms[:, first:last], ACT.Ln).then_inc(A["act_chain"], 1)
                act.wait_ge(A["act_chain"], norms[0])
                se.activation(y0[:, first:last], y1[:, first:last], ACT.Exp, scale=-0.5).then_inc(A["rs_first"], 1)

            def half_squares(event, half):
                for i in range(NT):
                    act.wait_ge(V["h_half"], NT * (event // 2 * 2 + half) + i + 1)
                    n = NT * half + i
                    se.activation(xn[:, i, half * BN:(half + 1) * BN], h[:, i, half * BN:(half + 1) * BN], ACT.Square,
                                  accum_out=ss[:, n:n + 1]).then_inc(A["half_squared"], 1)
                if half:
                    rsqrt_first(0, NT)

            def norm_squares(event, first=0, last=NT):
                for i in range(first, last):
                    wait_h(act, event, i)
                    if event == 0 and i == NT - 1:
                        act.wait_ge(V["gains_out"], 1)
                    se.activation(psf[:, D * i:D * (i + 1)], h[:, i, :], ACT.Square,
                                  accum_out=ss[:, i:i + 1]).then_inc(A["ssq_done"], 1)
                rsqrt_first(first, last)

            def transposed_hi(turn, gain_no=None):
                for k in range(KT):
                    act.wait_ge(M["xT_tr"], KT * turn + k + 1)
                    if gain_no is None:
                        se.copy(xT_hi[:, k, :], ps[:, k % 4, :]).then_inc(A["xT_hi_done"], 1)
                    else:
                        n = KT * gain_no + k
                        se.activation(xT_hi[:, k, :], ps[:, k % 4, :], ACT.Copy,
                                      scale=gainT[:, n:n + 1]).then_inc(A["xT_hi_done"], 1)

            def panel_out(p, last_block, dst, func=ACT.Copy, scale=1.0):
                act.wait_ge(M["blk_used"], last_block + 1)
                se.activation(dst, ps[:, panel_banks(p), :], func, scale=scale).then_inc(A["panel_out"], 1)

            LN_EXP = "natural_log_exp_and_others"
            se.preload_act_table_set(LN_EXP)
            norm_squares(0)
            act.wait_ge(A["small_loaded"], 16 * SMALL)
            se.copy(lr_hi, lr_raw[:, :, :]).then_inc(A["lr_hi_done"], 1)
            split(0)
            split(1)
            transposed_hi(0, 0)
            load_small(router_loads, A["router_loaded"])
            act.wait_ge(V["gate_abs"], 1)
            se.activation(cum, cum, ACT.Exp, scale=-1.0).then_inc(A["gate_ln"], 1)
            act.wait_ge(A["gate_ln"], 1)
            se.activation(cum, cum, ACT.Ln, bias=1.0).then_inc(A["gate_ln"], 1)
            split(2)
            act.wait_ge(V["gate_cum"], GH)
            se.activation(gate, cum, ACT.Exp, scale=1.0 / GATE_NORM).then_inc(A["gate_exp"], 1)
            se.activation(kinv, cum, ACT.Exp, scale=-1.0 / GATE_NORM).then_inc(A["gate_exp"], 1)
            panel_out(0, 1, qT, scale=DK ** -0.5)
            split(3)
            split(4)
            panel_out(1, 3, kT)
            split(5)
            act.wait_ge(V["gate_toend"], 1)
            se.activation(gate, gate, ACT.Exp, scale=1.0 / GATE_NORM).then_inc(A["gate_exp"], 1)
            split(6)
            panel_out(2, 5, v[:, :, 0:BN])
            split(7)
            split(8)
            panel_out(3, 7, v[:, :, BN:2 * BN])
            split(9)
            split(10)
            split(11)
            act.wait_ge(V["lo_done"], 12)
            panel_out(4, 9, sg[:, :, 0:BN], ACT.Silu)
            split(12)
            panel_out(5, 11, sg[:, :, BN:2 * BN], ACT.Silu)
            split(13)
            se.preload_act_table_set(LN_EXP)
            act.wait_ge(M["ktok_tr"], 1)
            se.copy(gate, ps[:, 0:4, :]).then_inc(A["ktok_out"], 1)
            for i in range(NT):
                act.wait_ge(M["inter_done"], 2 * i + 1)
                o = o_of(i)
                if i < NT - 1:
                    se.copy(xn[:, i, :], o)
                if i >= 2:
                    act.wait_ge(A["o_squared"], GH * (i - 1))
                for j in range(GH):
                    se.activation(kinv[:, 2 * (i % 2) + j // 2, DV * (j % 2):DV * (j % 2 + 1)], o[:, DV * j:DV * (j + 1)], ACT.Square,
                                  accum_out=ss[:, GH * i + j:GH * i + j + 1]).then_inc(A["o_squared"], 1)
                if i >= NT - 2:
                    rsqrt_first(*O_NORMS[i - (NT - 2)])
            transposed_hi(1)
            split(14)
            split(15)
            half_squares(1, 0)
            split(16)

            def x_hi(S, i):
                for f in (0, 1):
                    act.wait_ge(S["x_tr"], 2 * i + (f + 1))
                    se.copy(xg_hi[:, 4 * f:4 * f + 4, :],
                            ps[:, 4 + f, 0:4 * CAP].rearrange("p (k c) -> p k c", k=4)).then_inc(S["x_hi"], 1)

            def silu(S, i, reuse=True):
                if reuse:
                    act.wait_ge(S["mul"], i)
                se.activation(sil, ps[0:CAP, 0, :], ACT.Silu).then_inc(S["silu"], 1)

            def h_hi(S, i):
                act.wait_ge(S["h_tr"], i + 1)
                se.copy(ht_hi, ps[:, 6, 0:BK * CAP].rearrange("p (k c) -> p k c", k=BK)).then_inc(S["h_hi"], 1)

            def y_out(S, i, reuse=True):
                if reuse:
                    act.wait_ge(S["y_stored"], 16 * i)
                se.copy(y_sb, psf[0:CAP, 1024:2048]).then_inc(S["y_out"], 1)

            def experts(layer):
                B, I = blocks_of(layer), NE * layer
                se.preload_act_table_set("silu_and_others")
                split(B + 2)
                split(B + 3)
                x_hi(E, I)
                split(B + 4)
                split(B + 5)
                silu(E, I, layer > 0)
                x_hi(E, I + 1)
                split(B + 6)
                split(B + 7)

                def step(i, c, g, more, first=False):
                    split(c + 4, g)
                    split(c + 5, g)
                    silu(E, i)
                    if first:
                        h_hi(E, i - 1)
                    split(c + 6, g)
                    split(c + 7, g)
                    if more:
                        x_hi(E, i + 1)
                        split(c + 8, g)
                        split(c + 9, g)
                    else:
                        act.wait_ge(M["blk_used"], number(c + 6, g))
                    y_out(E, i - 1, not (isinstance(i, int) and i == 1))
                    h_hi(E, i)

                for k in range(2):
                    step(I + 1 + k, B + 4 + E_BLOCKS * k, 0, True, first=k == 0)
                with act.Fori(1, PAIRS) as g:
                    for k in range(2):
                        step(2 * g + (I + 1 + k), B + 4 + E_BLOCKS * k, g, True)
                step(I + NE - 1, B + LAST, 0, False)
                act.wait_ge(M["blk_used"], B + NE * E_BLOCKS)
                y_out(E, I + NE - 1)

                S, W = O[layer], OW[layer]

                def tile(j):
                    act.wait_ge(S["turn"], j + 1)
                    e = act.value_load(over[0:1, bass.ds(j, 1)], min_val=0, max_val=NE - 1)
                    x_hi(S, j)
                    for b, (kind, half) in enumerate((k, f) for k in "gud" for f in (0, 1)):
                        if b:
                            act.wait_ge(W["lo"], 6 * j + b)
                        act.dma_start(over_raw.rearrange("p (k n) -> p k n", k=BK),
                                      expert_block(layer, kind, e, half)).then_inc(W["loaded"], 16)
                        act.wait_ge(W["loaded"], 96 * j + 16 * (b + 1))
                        if b >= SPLIT:
                            act.wait_ge(W["used"], 6 * j + (b - SPLIT + 1))
                        se.copy(w_hi[:, b % SPLIT, :], over_raw).then_inc(W["hi"], 1)
                        if b == 3:
                            silu(S, j, False)
                            h_hi(S, j)
                    act.wait_ge(W["used"], 6 * j + 6)
                    y_out(S, j, False)

                over_loop(act, layer, tile)

            def router_weights(layer):
                act.wait_ge(A["router_loaded"], 16 * len(router_loads))
                se.copy(r_hi[:, :, :], r_raw[:, layer, :, :]).then_inc(A["r_hi_done"], 1)

            def router(layer):
                for i in (2, 3):
                    se.activation(xn[:, i, :], h[:, i, :], ACT.Copy, scale=rstd[:, i:i + 1]).then_inc(A["xn_scaled"], 1)
                act.wait_ge(M["logits_done"], layer + 1)
                se.copy(logitsT, ps[0:NR, 7, :]).then_inc(A["logits_out"], 1)
                for i in range(NT):
                    act.wait_ge((V["xn_ready"], G["xn_normed"])[i // 2], 2 * layer + i % 2 + 1)
                    act.dma_start(rows[i * P:(i + 1) * P, :], xn[:, i, :]).then_inc(A["rows_stored"], 16)
                act.wait_ge(V["group_diff"], layer + 1)
                se.activation(gd, gd, ACT.Exp).then_inc(A["router_exp"], 1)
                act.wait_ge(V["second_diff"], layer + 1)
                se.activation(ex, dd, ACT.Exp).then_inc(A["router_exp"], 1)

            se.preload_act_table_set(LN_EXP)
            router_weights(0)
            half_squares(1, 1)
            split(A_BLOCKS + 1)
            transposed_hi(2, 1)
            router(0)
            experts(0)

            B = L_BLOCKS
            split(B)
            se.preload_act_table_set(LN_EXP)
            norm_squares(2)
            split(B + 1)
            transposed_hi(3, 2)
            for q, dst in enumerate((kT1[:, 0:4, :], kT1[:, 4:8, :], v[:, :, 0:BN], v[:, :, BN:2 * BN])):
                split(B + 2 * q + 2)
                panel_out(8 + q, B + 2 * q + 1, dst)
                split(B + 2 * q + 3)
            transposed_hi(4, 3)
            for q in (4, 5):
                split(B + 2 * q + 2)
                panel_out(8 + q, B + 2 * q + 1, qT1[:, 4 * (q - 4):4 * (q - 3), :], scale=SD ** -0.5)
                split(B + 2 * q + 3)

            def z_exp(hd, r, p):
                act.wait_ge(V["z_abs"], 2 * hd + (p + 1))
                z = zt[r][:, ZPARTS[p]]
                se.activation(z, z, ACT.Exp, scale=-1.0).then_inc(A["z_exp"], 1)

            def z_ln(hd, r, p):
                act.wait_ge(A["z_exp"], 2 * hd + (p + 1))
                z = zt[r][:, ZPARTS[p]]
                se.activation(z, z, ACT.Ln, bias=1.0).then_inc(A["z_ln"], 1)

            def L_hi(hd, r):
                for p, cols in enumerate(ZPARTS):
                    act.wait_ge(V["L_done"], 2 * hd + (p + 1))
                    se.copy(s_hi[:, cols], zt[r][:, cols]).then_inc(A["L_hi_done"], 1)

            def weights(hd, r, p, reuse=True):
                if reuse and p == 0:
                    act.wait_ge(M["av_done"], hd - 1)
                act.wait_ge(M["sums_done"], 2 * hd + (p + 1))
                se.activation(wt[r][:, ZPARTS[p]], z_of(r)[:, ZPARTS[p]], ACT.Exp).then_inc(A["weights_done"], 1)

            def oT_hi(q, b):
                act.wait_ge(M["av_done"], 2 * q + 2)
                se.copy(xT_hi[:, bass.ds(q, 1), :].rearrange("p o t -> p (o t)"), ps[:, 6 + b, :]).then_inc(A["oT_hi_done"], 1)

            for p in (0, 1):
                z_exp(0, 0, p)
                z_ln(0, 0, p)

            def head(hd, r, pair=None, reuse=True, more=True):
                L_hi(hd, r % 2)
                for p in (0, 1):
                    if more:
                        z_exp(hd + 1, (r + 1) % 2, p)
                    weights(hd, r % 2, p, reuse)
                    if more:
                        z_ln(hd + 1, (r + 1) % 2, p)
                if pair is not None:
                    oT_hi(pair, (r // 2 + 1) % 2)

            for hd in range(4):
                head(hd, hd, 0 if hd == 2 else None, hd >= 2)
            with act.Fori(1, 3) as g:
                for r in range(4):
                    head(4 * g + r, r, None if r % 2 else 2 * g + (r // 2 - 1))
            for hd in range(12, 16):
                head(hd, hd - 12, None if hd % 2 else hd // 2 - 1, more=hd < 15)
            oT_hi(7, 1)
            split(B + 14)
            split(B + 15)
            half_squares(3, 0)
            split(B + 16)
            router_weights(1)
            half_squares(3, 1)
            split(B + A_BLOCKS + 1)
            transposed_hi(5, 4)
            router(1)
            experts(1)
            se.preload_act_table_set(LN_EXP)
            norm_squares(4, 0, 2)

            def final_scale(tiles, part):
                act.wait_ge(V["rstd_ready"], part)
                for i in tiles:
                    act.wait_ge(G["xn_normed"], 2 * LAYERS + i + 1)
                    se.activation(xn[:, i, :], xn[:, i, :], ACT.Copy, scale=rstd[:, i:i + 1]).then_inc(A["xn_scaled"], 1)

            final_scale((0, 1), 1)
            norm_squares(4, 2, NT)
            final_scale((2,), 2)

        @block.vector
        def _(dve):
            link = Chain(dve, V["dve_chain"])

            def split(c, g=0):
                dve.wait_ge(A["hi_done"], number(c + 1, g))
                ve.tensor_tensor(lo_slots[split_slot(c)], raw_slots[raw_slot(c)], hi_slots[split_slot(c)],
                                 ALU.subtract).then_inc(V["lo_done"], 1)

            norms = [0]

            def refine(first, last, final=0):
                norms[0] += 1
                dve.wait_ge(A["rs_first"], norms[0])
                a, b, m, o = (t[:, first:last] for t in (y0, y1, ms, rstd))
                link(ve.tensor_tensor(b, a, a, ALU.mult))
                link(ve.tensor_tensor(b, b, m, ALU.mult))
                link(ve.tensor_scalar(b, b, -0.5, 1.5, ALU.mult, ALU.add))
                if final:
                    ve.tensor_tensor(o, a, b, ALU.mult).then_inc(V["rstd_ready"], 1)
                    dve.wait_ge(V["rstd_ready"], final)
                else:
                    link(ve.tensor_tensor(o, a, b, ALU.mult))

            def mean_square(event, first, last):
                if event % 2 == 0:
                    dve.wait_ge(A["ssq_done"], NT * (event // 2) + last)
                ve.tensor_scalar(ms[:, first:last], ss[:, first:last], 1.0 / D, EPS, ALU.mult, ALU.add).then_inc(V["ms_ready"], 1)

            def norm_scale(event):
                if event % 2:
                    dve.wait_ge(A["half_squared"], NT * (event + 1))
                    link(ve.tensor_tensor(ss[:, 0:NT], ss[:, 0:NT], ss[:, NT:2 * NT], ALU.add))
                mean_square(event, 0, NT)
                refine(0, NT)

            def diagonals():
                for i in range(NT):
                    ve.tensor_scalar(diag[:, i, :], ident[:, :], rstd[:, i:i + 1], None, ALU.mult).then_inc(V["diag_ready"], 1)

            def normed(use, tiles=range(NT)):
                dve.wait_ge(G["gain_loaded"], 16 * (use + 1))
                for i in tiles:
                    ve.scalar_tensor_tensor(xn[:, i, :], h[:, i, :], rstd[:, i:i + 1], gain[:, :],
                                            ALU.mult, ALU.mult).then_inc(V["xn_ready"], 1)

            def transposed_lo(turn, gain_no=None):
                for k in range(KT):
                    dve.wait_ge(A["xT_hi_done"], KT * turn + k + 1)
                    if gain_no is None:
                        ve.tensor_tensor(xT_lo[:, k, :], ps[:, k % 4, :], xT_hi[:, k, :],
                                         ALU.subtract).then_inc(V["xT_lo_done"], 1)
                    else:
                        n = KT * gain_no + k
                        ve.scalar_tensor_tensor(xT_lo[:, k, :], ps[:, k % 4, :], gainT[:, n:n + 1], xT_hi[:, k, :],
                                                ALU.mult, ALU.subtract).then_inc(V["xT_lo_done"], 1)

            def add_panel(p, last_block, half):
                dve.wait_ge(M["blk_used"], last_block + 1)
                for i in range(NT):
                    d = h[:, i, half * BN:(half + 1) * BN]
                    ins = ve.tensor_tensor(d, d, ps[:, 4 * (p % 2) + i, :], ALU.add)
                    ins.then_inc(V["h_half"], 1)

            dve.wait_ge(M["gains_tr"], 1)
            ve.tensor_copy(gainT[:, :], ps[:, 7, 0:5 * KT]).then_inc(V["gains_out"], 1)
            norm_scale(0)
            diagonals()
            dve.wait_ge(A["lr_hi_done"], 1)
            ve.tensor_tensor(lr_lo, lr_raw[:, :, :], lr_hi, ALU.subtract).then_inc(V["lr_lo_done"], 1)
            split(0)
            transposed_lo(0, 0)
            dve.wait_ge(M["lr_done"], 1)
            ve.tensor_copy(lrT, ps[0:RANK, 7, :]).then_inc(V["lr_out"], 1)
            split(1)
            dve.wait_ge(M["gates_done"], 1)
            for i in range(GH):
                ve.tensor_scalar(gate[:, i, :], ps[:, 4 + i, :], bgk[:, i:i + 1], None, ALU.add).then_inc(V["gates_in"], 1)
            dve.wait_ge(V["gates_in"], GH)
            ve.scalar_tensor_tensor(cum, gate, -1.0, gate, ALU.mult, ALU.max).then_inc(V["gate_abs"], 1)
            dve.wait_ge(A["gate_ln"], 2)
            link(ve.scalar_tensor_tensor(gate, gate, 0.0, cum, ALU.min, ALU.subtract))
            for i in range(GH):
                ve.tensor_tensor_scan(cum[:, i, :], reset, gate[:, i, :], 0.0, ALU.mult, ALU.add).then_inc(V["gate_cum"], 1)
            split(2)
            dve.wait_ge(A["gate_exp"], 1)
            dve.wait_ge(A["panel_out"], 1)
            ve.tensor_tensor(qT, qT, gate, ALU.mult).then_inc(V["q_dec"], 1)
            by_chunk = "p h (c t) -> p (h c) t"
            gate_c, cum_c = gate.rearrange(by_chunk, t=CHUNK), cum.rearrange(by_chunk, t=CHUNK)
            link(ve.tensor_copy(decay[:, :, :].rearrange("p h c -> p (h c)").unsqueeze(2), gate_c[:, :, CHUNK - 1:CHUNK]))
            ve.tensor_tensor(gate_c, cum_c[:, :, CHUNK - 1:CHUNK].broadcast_to([P, GH * NCH, CHUNK]), cum_c,
                             ALU.subtract).then_inc(V["gate_toend"], 1)
            split(3)
            split(4)
            dve.wait_ge(A["gate_exp"], 2)
            dve.wait_ge(A["panel_out"], 2)
            ve.tensor_tensor(kinv, kT, kinv, ALU.mult).then_inc(V["k_inv"], 1)
            split(5)
            dve.wait_ge(A["gate_exp"], 3)
            ve.tensor_tensor(kT, kT, gate, ALU.mult).then_inc(V["k_toend"], 1)
            for n in range(6, 14):
                split(n)
            for i in range(NT):
                dve.wait_ge(M["att_done"], i + 1)
                ve.tensor_copy(kT[:, i, :], ps[:, 4 + i, :]).then_inc(V["att_out"], 1)
            for c in range(NCH - 1):
                dve.wait_ge(M["upd_done"], c + 1)
                if c >= 2:
                    dve.wait_ge(M["inter_done"], c - 1)
                u = psf[:, 1024 * (c % 2):1024 * (c % 2) + 1024].rearrange("p (h e) -> p h e", h=GH)
                s0, s1 = state[:, c % 2], state[:, (c + 1) % 2]
                if c == 0:
                    ve.tensor_copy(s1, u).then_inc(V["state_done"], GH)
                else:
                    dve.wait_ge(V["state_done"], GH * c)
                    for i in range(GH):
                        ve.scalar_tensor_tensor(s1[:, i, :], s0[:, i, :], decay[:, i, c:c + 1], u[:, i, :],
                                                ALU.mult, ALU.add).then_inc(V["state_done"], 1)

            def gated(i):
                for j in range(GH):
                    o = xn[:, i, DV * j:DV * (j + 1)]
                    src = o if i < NT - 1 else o_of(i)[:, DV * j:DV * (j + 1)]
                    ins = ve.scalar_tensor_tensor(o, src, rstd[:, GH * i + j:GH * i + j + 1],
                                                  sg[:, i, DV * j:DV * (j + 1)], ALU.mult, ALU.mult)
                ins.then_inc(V["og_ready"], 1)

            for (first, last), tiles in zip(O_NORMS, (range(NT - 1), (NT - 1,))):
                dve.wait_ge(A["o_squared"], last)
                ve.tensor_scalar(ms[:, first:last], ss[:, first:last], 1.0 / DV, EPS, ALU.mult, ALU.add).then_inc(V["ms_ready"], 1)
                refine(first, last)
                dve.wait_ge(G["sg_ready"], 1)
                for i in tiles:
                    gated(i)
            transposed_lo(1)
            split(14)
            add_panel(6, 13, 0)
            split(15)
            split(16)
            add_panel(7, 15, 1)

            def x_lo(S, i):
                for f in (0, 1):
                    dve.wait_ge(S["x_hi"], 2 * i + (f + 1))
                    ve.tensor_tensor(xg_lo[:, 4 * f:4 * f + 4, :],
                                     ps[:, 4 + f, 0:4 * CAP].rearrange("p (k c) -> p k c", k=4),
                                     xg_hi[:, 4 * f:4 * f + 4, :], ALU.subtract).then_inc(S["x_lo"], 1)

            def mul(S, i, reuse=True):
                dve.wait_ge(S["silu"], i + 1)
                if reuse:
                    dve.wait_ge(S["h_tr"], i)
                ve.tensor_tensor(hid, sil, ps[0:CAP, 1, :], ALU.mult).then_inc(S["mul"], 1)

            def h_lo(S, i):
                dve.wait_ge(S["h_hi"], i + 1)
                ve.tensor_tensor(ht_lo, ps[:, 6, 0:BK * CAP].rearrange("p (k c) -> p k c", k=BK), ht_hi,
                                 ALU.subtract).then_inc(S["h_lo"], 1)

            def experts(layer):
                B, I = blocks_of(layer), NE * layer
                split(B + 2)
                split(B + 3)
                x_lo(E, I)
                split(B + 4)
                split(B + 5)
                dve.wait_ge(M["blk_used"], B + 4)
                mul(E, I, layer > 0)
                x_lo(E, I + 1)
                split(B + 6)
                split(B + 7)

                def step(i, c, g, more, first=False):
                    for n in range(4, 8):
                        split(c + n, g)
                        if first and n == 5:
                            h_lo(E, i - 1)
                    mul(E, i)
                    if more:
                        x_lo(E, i + 1)
                        split(c + 8, g)
                        split(c + 9, g)
                    h_lo(E, i)

                for k in range(2):
                    step(I + 1 + k, B + 4 + E_BLOCKS * k, 0, True, first=k == 0)
                with dve.Fori(1, PAIRS) as g:
                    for k in range(2):
                        step(2 * g + (I + 1 + k), B + 4 + E_BLOCKS * k, g, True)
                step(I + NE - 1, B + LAST, 0, False)

                S, W = O[layer], OW[layer]

                def tile(j):
                    dve.wait_ge(S["turn"], j + 1)
                    x_lo(S, j)
                    for b in range(6):
                        dve.wait_ge(W["hi"], 6 * j + (b + 1))
                        ve.tensor_tensor(w_lo[:, b % SPLIT, :], over_raw, w_hi[:, b % SPLIT, :],
                                         ALU.subtract).then_inc(W["lo"], 1)
                        if b == 3:
                            dve.wait_ge(W["used"], 6 * j + 4)
                            mul(S, j, False)
                            h_lo(S, j)

                over_loop(dve, layer, tile)

            def over4(a, n):
                return a.unsqueeze(2).broadcast_to([P, NT, n])

            def per_expert(a):
                return a.unsqueeze(1).broadcast_to([P, NT, NE])

            def router_weights(layer):
                dve.wait_ge(A["r_hi_done"], layer + 1)
                ve.tensor_tensor(r_lo[:, :, :], r_raw[:, layer, :, :], r_hi[:, :, :], ALU.subtract).then_inc(V["r_lo_done"], 1)

            def router(layer):
                tt, ts, red, stt = ve.tensor_tensor, ve.tensor_scalar, ve.tensor_reduce, ve.scalar_tensor_tensor
                normed(layer, (0, 1))
                dve.wait_ge(M["logits_tr"], layer + 1)
                link(tt(lg, ps[:, 6, 0:NT * NR].rearrange("p (i e) -> p i e", i=NT),
                        r_bias[:, layer, :].unsqueeze(1).broadcast_to([P, NT, NR]), ALU.add))
                lgg = lg[:, :, 0:NG]
                link(red(gm, lgg, AX.X, ALU.max))
                tt(gd, lgg, over4(gm, NG), ALU.subtract).then_inc(V["group_diff"], 1)
                link(tt(geq, lgg, over4(gm, NG), ALU.is_equal))
                link(tt(gv, geq, desc4[:, :].unsqueeze(1).broadcast_to([P, NT, NG]), ALU.mult))
                link(red(gvm, gv, AX.X, ALU.max))
                link(tt(goh, gv, over4(gvm, NG), ALU.is_equal))
                def by_group(t, i):
                    return t[:, i, :].rearrange("p (g e) -> p g e", g=NG)

                def each_expert(t, i):
                    return t[:, i, :].unsqueeze(2).broadcast_to([P, NG, EG])

                link(ts(gneg, goh, 1e30, -1e30, ALU.mult, ALU.add),
                     *[tt(by_group(em, i), lg[:, i, NG:NR].rearrange("p (g e) -> p g e", g=NG), each_expert(goh, i), ALU.mult)
                       for i in range(NT)])
                link(*[tt(by_group(em, i), by_group(em, i), each_expert(gneg, i), ALU.add) for i in range(NT)])

                def first_max(src, k):
                    one_hot = oh[:, k, :].rearrange("p (i e) -> p i e", i=NT)
                    link(red(m12[:, k, :], src, AX.X, ALU.max))
                    link(tt(eq, src, over4(m12[:, k, :], NE), ALU.is_equal))
                    link(tt(ev, eq, per_expert(desc16[:, :]), ALU.mult))
                    link(red(evm[:, k, :], ev, AX.X, ALU.max))
                    link(tt(one_hot, ev, over4(evm[:, k, :], NE), ALU.is_equal))
                    return one_hot

                oh1 = first_max(em, 0)
                link(stt(em2, oh1, -2e30, em, ALU.mult, ALU.add))
                oh2 = first_max(em2, 1)
                tt(sel_b[:, :, :], oh1, oh2, ALU.add).then_inc(V["sel_ready"], 1)
                tt(dd, m12[:, 1, :], m12[:, 0, :], ALU.subtract).then_inc(V["second_diff"], 1)
                dve.wait_ge(M["ranks_done"], layer + 1)
                rank_e = ps[:, 5, 0:NT * NE]
                by_choice = "p (k i) e -> p k (i e)"
                link(ve.tensor_copy(cnt, ps[:, 5, NT * NE:(NT + 1) * NE]),
                     tt(tmp_rank.rearrange(by_choice, k=2), oh, rank_e.unsqueeze(1).broadcast_to([P, 2, NT * NE]), ALU.mult))
                link(red(rank_k, tmp_rank, AX.X, ALU.add),
                     tt(cnt_over, cnt.unsqueeze(2).broadcast_to([P, NE, STEPS_OVER]),
                        caps[:, :].unsqueeze(1).broadcast_to([P, NE, STEPS_OVER]), ALU.is_gt))
                link(red(ovn, cnt_over, AX.X, ALU.add),
                     tt(rank_over, rank_k.unsqueeze(2).broadcast_to([P, 2 * NT, STEPS_OVER]),
                        caps[:, :].unsqueeze(1).broadcast_to([P, 2 * NT, STEPS_OVER]), ALU.is_ge))
                link(ve.tensor_tensor_scan(ovend, one16[:, :], ovn, 0.0, ALU.mult, ALU.add),
                     red(o_k, rank_over, AX.X, ALU.add),
                     ts(e_k, evm.rearrange("p k i -> p (k i)"), -1.0, float(NE), ALU.mult, ALU.add))
                link(tt(ovbase, ovend, ovn, ALU.subtract),
                     stt(row_k, o_k, -float(CAP), rank_k, ALU.mult, ALU.add),
                     ts(step_k, o_k, 0.0, None, ALU.is_gt))
                link(tt(tmp_base, oh_k, ovbase.unsqueeze(1).broadcast_to([P, 2 * NT, NE]), ALU.mult),
                     tt(at_row, index[:, :].unsqueeze(1).broadcast_to([P, 2 * NT, CAP]),
                        row_k.unsqueeze(2).broadcast_to([P, 2 * NT, CAP]), ALU.is_equal))
                link(red(base_k, tmp_base, AX.X, ALU.add))
                link(tt(base_k, base_k, o_k, ALU.add))
                link(stt(base_k, base_k, float(NE - 1), e_k, ALU.add, ALU.subtract))
                link(tt(base_k, base_k, step_k, ALU.mult))
                link(tt(tile_k, base_k, e_k, ALU.add))
                link(tt(at_tile, index[:, 0:TILES].unsqueeze(1).broadcast_to([P, 2 * NT, TILES]),
                        tile_k.unsqueeze(2).broadcast_to([P, 2 * NT, TILES]), ALU.is_equal))
                for k in range(2):
                    half = slice(NT * k, NT * (k + 1))
                    tt(at_tile_t[:, half, :], at_tile[:, half, :],
                       token_id[:, :].unsqueeze(2).broadcast_to([P, NT, TILES]), ALU.mult).then_inc(V["places_ready"], 1)
                link(stt(p_k, tile_k, float(CAP), row_k, ALU.mult, ALU.add),
                     tt(over_cmp, ovend.unsqueeze(1).broadcast_to([P, MAX_OVER, NE]),
                        index[:, 0:MAX_OVER].unsqueeze(2).broadcast_to([P, MAX_OVER, NE]), ALU.is_le))
                dve.wait_ge(M["lists_done"], layer + 1)
                ve.tensor_copy(token[:, :], ps[0:CAP, 4, 0:TILES]).then_inc(V["tokens_ready"], 1)
                link(red(over_f[:, 0:MAX_OVER], over_cmp, AX.X, ALU.add),
                     ve.tensor_copy(pos[:, :, :].rearrange("p k i -> p (k i)"), p_k))
                link(ts(over_f[:, 0:MAX_OVER], over_f[:, 0:MAX_OVER], float(NE - 1), None, ALU.min),
                     ve.tensor_copy(over_f[:, MAX_OVER:MAX_OVER + 1], ovend[:, NE - 1:NE]))
                ve.tensor_copy(over[:, :], over_f[0:1, :]).then_inc(V["pos_ready"], 1)
                dve.wait_ge(A["router_exp"], 2 * layer + 2)
                link(red(gs, gd, AX.X, ALU.add),
                     ts(denom, ex, 1.0, None, ALU.add))
                link(ve.reciprocal(gw, gs),
                     ve.reciprocal(rs, denom))
                link(tt(w12[:, 0, :], rs, gw, ALU.mult))
                link(tt(w12[:, 1, :], w12[:, 0, :], ex, ALU.mult))

            def combine(layer, first=0, last=2 * NT):
                for n in range(first, last):
                    i, k = COMBINE[n]
                    dve.wait_ge(gathered[n], 16 * (layer + 1))
                    if k:
                        dve.wait_ge(V["combined"], 2 * NT * layer + n - 1)
                    ve.scalar_tensor_tensor(h[:, i, :], y_rows[n], w12[:, k, i:i + 1], h[:, i, :],
                                            ALU.mult, ALU.add).then_inc(V["combined"], 1)

            router_weights(0)
            norm_scale(1)
            diagonals()
            split(17)
            transposed_lo(2, 1)
            router(0)
            experts(0)

            B = L_BLOCKS
            split(B)
            combine(0)
            norm_scale(2)
            diagonals()
            split(B + 1)
            transposed_lo(3, 2)
            for n in range(2, 10):
                split(B + n)
            transposed_lo(4, 3)
            for n in range(10, 14):
                split(B + n)

            def z_abs(hd, r, p):
                z = ZPARTS[p]
                dve.wait_ge(M["z_done"], 2 * hd + (p + 1))
                ve.tensor_scalar(zt[r][:, z].bitcast(I32), z_of(r)[:, z].bitcast(I32), 0x7FFFFFFF, None,
                                 ALU.bitwise_and).then_inc(V["z_abs"], 1)

            def log_om(hd, r, p):
                z = ZPARTS[p]
                dve.wait_ge(A["z_ln"], 2 * hd + (p + 1))
                ve.scalar_tensor_tensor(zt[r][:, z], z_of(r)[:, z], 0.0, zt[r][:, z], ALU.max, ALU.add).then_inc(V["L_done"], 1)

            def L_lo(hd, r, p):
                z = ZPARTS[p]
                dve.wait_ge(A["L_hi_done"], 2 * hd + (p + 1))
                ve.tensor_tensor(s_lo[:, z], zt[r][:, z], s_hi[:, z], ALU.subtract).then_inc(V["L_lo_done"], 1)

            def oT_lo(q, b):
                dve.wait_ge(A["oT_hi_done"], q + 1)
                hi, lo = (t[:, bass.ds(q, 1), :].rearrange("p o t -> p (o t)") for t in (xT_hi, xT_lo))
                ve.tensor_tensor(lo, ps[:, 6 + b, :], hi, ALU.subtract).then_inc(V["oT_lo_done"], 1)

            for p in (0, 1):
                z_abs(0, 0, p)
            for p in (0, 1):
                log_om(0, 0, p)

            def head(hd, r, pair=None, more=True):
                n = (r + 1) % 2
                for p in (0, 1):
                    L_lo(hd, r % 2, p)
                    if more:
                        z_abs(hd + 1, n, p)
                if more:
                    for p in (0, 1):
                        log_om(hd + 1, n, p)
                if pair is not None:
                    oT_lo(pair, (r // 2 + 1) % 2)

            for hd in range(4):
                head(hd, hd, 0 if hd == 2 else None)
            with dve.Fori(1, 3) as g:
                for r in range(4):
                    head(4 * g + r, r, None if r % 2 else 2 * g + (r // 2 - 1))
            for hd in range(12, 16):
                head(hd, hd - 12, None if hd % 2 else hd // 2 - 1, hd < 15)
            oT_lo(7, 1)
            split(B + 14)
            add_panel(14, B + 13, 0)
            split(B + 15)
            split(B + 16)
            add_panel(15, B + 15, 1)
            router_weights(1)
            norm_scale(3)
            diagonals()
            split(B + 17)
            transposed_lo(5, 4)
            router(1)
            experts(1)
            combine(1, 0, 5)
            mean_square(4, 0, 2)
            combine(1, 5, 6)
            refine(0, 2, final=1)
            combine(1, 6, 8)
            mean_square(4, 2, NT)
            refine(2, NT, final=2)
            normed(2, [NT - 1])

        @block.tensor
        def _(pe):
            def three(o, a_hi, a_lo, b_hi, b_lo, start, stop):
                te.matmul(o, a_hi, b_hi, start=start, stop=False)
                te.matmul(o, a_hi, b_lo, start=False, stop=False)
                return te.matmul(o, a_lo, b_hi, start=False, stop=stop)

            def transposed(turn, event=None, use=lambda k: None):
                if event is not None:
                    pe.wait_ge(V["diag_ready"], NT * (event + 1))
                for k in range(KT):
                    if k >= 4:
                        pe.wait_ge(V["xT_lo_done"], KT * turn + k - 3)
                    for i in range(NT):
                        o, cols = ps[:, k % 4, P * i:P * (i + 1)], slice(P * k, P * (k + 1))
                        if event is None:
                            ins = te.transpose(o, xn[:, i, cols], ident[:, :])
                        else:
                            ins = te.matmul(o, h[:, i, cols], diag[:, i, :], start=True, stop=True)
                    ins.then_inc(M["xT_tr"], 1)
                    if k >= 4:
                        use(k - 4)
                for k in range(KT - 4, KT):
                    pe.wait_ge(V["xT_lo_done"], KT * turn + k + 1)
                    use(k)

            def dense(p, c, feature_major):
                for n in (0, 1):
                    pe.wait_ge(V["lo_done"], c + n + 1)
                    for kk in range(BK):
                        k = BK * n + kk
                        for j in range(4):
                            part = slice(P * j, P * (j + 1))
                            wide = slice(BN * kk, BN * (kk + 1))
                            cols = slice(BN * kk + P * j, BN * kk + P * (j + 1))
                            o = ps[:, 4 * (p % 2) + j, :]
                            s = split_slot(c + n)
                            if feature_major:
                                ops = w_hi[:, s, cols], w_lo[:, s, cols], xT_hi[:, k, :], xT_lo[:, k, :]
                            else:
                                ops = xT_hi[:, k, part], xT_lo[:, k, part], w_hi[:, s, wide], w_lo[:, s, wide]
                            ins = three(o, *ops, start=k == 0, stop=k == KT - 1)
                    ins.then_inc(M["blk_used"], 1)

            pe.wait_ge(G["consts"], 1)
            pe.wait_ge(A["small_loaded"], 16 * SMALL)
            te.transpose(ps[:, 7, 0:5 * KT], gain_rows, ident[0:5 * KT, 0:5 * KT]).then_inc(M["gains_tr"], 1)

            def gate_input(k):
                if k == 0:
                    pe.wait_ge(V["lr_lo_done"], 1)
                ins = three(ps[0:RANK, 7, :], lr_hi[:, k, :], lr_lo[:, k, :], xT_hi[:, k, :], xT_lo[:, k, :],
                            start=k == 0, stop=k == KT - 1)
                if k == KT - 1:
                    ins.then_inc(M["lr_done"], 1)

            transposed(0, 0, gate_input)
            pe.wait_ge(V["lr_out"], 1)
            for i in range(GH):
                ins = te.matmul(ps[:, 4 + i, :], wgk2[:, DK * i:DK * (i + 1)], lrT, start=True, stop=True)
            ins.then_inc(M["gates_done"], 1)
            dense(0, 0, True)
            pe.wait_ge(V["gates_in"], GH)
            dense(1, 2, True)
            pe.wait_ge(A["panel_out"], 1)
            dense(2, 4, False)
            pe.wait_ge(A["panel_out"], 2)
            dense(3, 6, False)
            pe.wait_ge(A["panel_out"], 3)
            dense(4, 8, False)
            pe.wait_ge(A["panel_out"], 4)
            dense(5, 10, False)
            pe.wait_ge(V["k_toend"], 1)
            pe.wait_ge(A["panel_out"], 5)
            for i in range(NT):
                for j in range(GH):
                    ins = te.transpose(ps[:, i, P * j:P * (j + 1)], kT[:, j, P * i:P * (i + 1)], ident[:, :])
            ins.then_inc(M["ktok_tr"], 1)
            pe.wait_ge(V["k_inv"], 1)
            pe.wait_ge(A["panel_out"], 6)
            for i in range(NT):
                for j in range(GH):
                    t = slice(P * i, P * (i + 1))
                    ins = te.matmul(ps[:, 4 + i, P * j:P * (j + 1)], kinv[:, j, t], qT[:, j, t], start=True, stop=True)
                ins.then_inc(M["att_done"], 1)
            ktok = gate
            att = kT
            pe.wait_ge(A["ktok_out"], 1)
            for i in range(NT):
                for c in (2 * i, 2 * i + 1):
                    if c == NCH - 1:
                        continue
                    if c >= 2:
                        pe.wait_ge(V["state_done"], GH * (c - 1))
                    rows = slice(CHUNK * (c % 2), CHUNK * (c % 2 + 1))
                    for j in range(GH):
                        a = 1024 * (c % 2) + DV * j
                        ins = te.matmul(psf[:, a:a + DV], ktok[rows, i, DK * j:DK * (j + 1)],
                                        v[rows, i, DV * j:DV * (j + 1)], start=True, stop=True)
                    ins.then_inc(M["upd_done"], 1)
                if i == 0:
                    pe.wait_ge(V["att_out"], NT)
                pe.wait_ge(G["masked"], 2 * i + 2)
                if i >= 2:
                    pe.wait_ge(A["o_squared"], GH * (i - 1))
                o0 = 2048 + 1024 * (i % 2)
                for j in range(GH):
                    te.matmul(psf[:, o0 + DV * j:o0 + DV * (j + 1)], att[:, i, P * j:P * (j + 1)],
                              v[:, i, DV * j:DV * (j + 1)], start=j % 2 == 0, stop=True, skip_group_check=True)
                for c in (2 * i, 2 * i + 1):
                    if c == 0:
                        continue
                    pe.wait_ge(V["state_done"], GH * c)
                    rows = slice(CHUNK * (c % 2), CHUNK * (c % 2 + 1))
                    for j in range(GH):
                        ins = te.matmul(psf[rows, o0 + DV * j:o0 + DV * (j + 1)],
                                        qT[:, j, CHUNK * c:CHUNK * (c + 1)], state[:, c % 2, j, :],
                                        start=False, stop=True, skip_group_check=True)
                    ins.then_inc(M["inter_done"], 1)
            pe.wait_ge(V["og_ready"], NT)
            transposed(1)
            dense(6, 12, False)
            dense(7, 14, False)

            def x_transposed(S, i, slot, loads, reuse=True):
                pe.wait_ge((S["x_loaded0"], S["x_loaded1"])[slot], 16 * loads)
                for f in (0, 1):
                    if reuse:
                        pe.wait_ge(S["x_lo"], 2 * i + (f - 1))
                    for k in range(4):
                        ins = te.transpose(ps[:, 4 + f, CAP * k:CAP * (k + 1)],
                                           xg[:, slot, P * (4 * f + k):P * (4 * f + k + 1)], ident[0:CAP, 0:CAP])
                    ins.then_inc(S["x_tr"], 1)

            def up_block(which, half, slot, used):
                for kk in range(BK):
                    k = BK * half + kk
                    wide = slice(BN * kk, BN * (kk + 1))
                    ins = three(ps[0:CAP, which, :], xg_hi[:, k, :], xg_lo[:, k, :], hi_slots[slot][:, wide],
                                lo_slots[slot][:, wide], start=k == 0, stop=k == KT - 1)
                ins.then_inc(used, 1)

            def down_block(half, slot, used):
                for kk in range(BK):
                    wide = slice(BN * kk, BN * (kk + 1))
                    ins = three(ps[0:CAP, 2 + half, :], ht_hi[:, kk, :], ht_lo[:, kk, :], hi_slots[slot][:, wide],
                                lo_slots[slot][:, wide], start=kk == 0, stop=kk == BK - 1)
                ins.then_inc(used, 1)

            def h_transposed(S, i, reuse=True):
                pe.wait_ge(S["mul"], i + 1)
                if reuse:
                    pe.wait_ge(S["h_lo"], i)
                for k in range(BK):
                    ins = te.transpose(ps[:, 6, CAP * k:CAP * (k + 1)], hid[:, P * k:P * (k + 1)], ident[0:CAP, 0:CAP])
                ins.then_inc(S["h_tr"], 1)

            def experts(layer):
                B, I = blocks_of(layer), NE * layer
                first_load = 8 * layer + 1

                def up(i, c, g=0, reuse=True, parts=range(4)):
                    pe.wait_ge(E["x_lo"], 2 * i + 2)
                    for n in parts:
                        if n == 0 and reuse:
                            pe.wait_ge(E["silu"], i)
                        if n == 2 and reuse:
                            pe.wait_ge(E["mul"], i)
                        pe.wait_ge(V["lo_done"], number(c + n + 1, g))
                        up_block(n // 2, n % 2, split_slot(c + n), M["blk_used"])

                def down(i, c, g=0):
                    pe.wait_ge(E["h_lo"], i + 1)
                    for n in range(2):
                        pe.wait_ge(V["lo_done"], number(c + n + 1, g))
                        down_block(n, split_slot(c + n), M["blk_used"])

                x_transposed(E, I, 0, first_load, layer > 0)
                up(I, B, 0, layer > 0)
                x_transposed(E, I + 1, 1, first_load)

                def step(g, k, first=False):
                    i, c = 2 * g + (I + 1 + k), B + 4 + E_BLOCKS * k
                    if first:
                        up(i, c, g, parts=(0, 1))
                        h_transposed(E, i - 1, layer > 0)
                        up(i, c, g, parts=(2, 3))
                    else:
                        up(i, c, g)
                    x_transposed(E, i + 1, k, g + (first_load + 1))
                    down(i - 1, c + 4, g)
                    h_transposed(E, i)

                for k in range(2):
                    step(0, k, first=k == 0)
                with pe.Fori(1, PAIRS) as g:
                    for k in range(2):
                        step(g, k)
                i, c = I + NE - 1, B + LAST
                up(i, c)
                down(i - 1, c + 4)
                h_transposed(E, i)
                down(i, c + 6)

                S, W = O[layer], OW[layer]

                def tile(j):
                    pe.wait_ge(E["y_out"], NE * (layer + 1))
                    pe.wait_ge(S["turn"], j + 1)
                    x_transposed(S, j, 0, j + 1, False)
                    pe.wait_ge(S["x_lo"], 2 * j + 2)
                    for b in range(6):
                        pe.wait_ge(W["lo"], 6 * j + (b + 1))
                        if b == 4:
                            pe.wait_ge(S["h_lo"], j + 1)
                        if b < 4:
                            up_block(b // 2, b % 2, b % SPLIT, W["used"])
                        else:
                            down_block(b - 4, b % SPLIT, W["used"])
                        if b == 3:
                            h_transposed(S, j, False)

                over_loop(pe, layer, tile)

            def logits(k):
                ins = three(ps[0:NR, 7, :], r_hi[:, k, :], r_lo[:, k, :], xT_hi[:, k, :], xT_lo[:, k, :],
                            start=k == 0, stop=k == KT - 1)
                if k == KT - 1:
                    ins.then_inc(M["logits_done"], 1)

            def router(layer):
                pe.wait_ge(A["logits_out"], layer + 1)
                for i in range(NT):
                    ins = te.transpose(ps[:, 6, NR * i:NR * (i + 1)], logitsT[:, P * i:P * (i + 1)], ident[0:NR, 0:NR])
                ins.then_inc(M["logits_tr"], 1)
                pe.wait_ge(V["sel_ready"], layer + 1)
                for i in range(NT):
                    o = ps[:, 5, NE * i:NE * (i + 1)]
                    for j in range(i):
                        te.matmul(o, ones_b[:, :], sel_b[:, j, :], start=j == 0, stop=False)
                    te.matmul(o, before[:, :], sel_b[:, i, :], start=i == 0, stop=True)
                o = ps[:, 5, NE * NT:NE * (NT + 1)]
                for j in range(NT):
                    ins = te.matmul(o, ones_b[:, :], sel_b[:, j, :], start=j == 0, stop=j == NT - 1)
                ins.then_inc(M["ranks_done"], 1)
                pe.wait_ge(V["places_ready"], 2 * layer + 2)
                for n in range(2 * NT):
                    ins = te.matmul(ps[0:CAP, 4, 0:TILES], at_row[:, n, :], at_tile_t[:, n, :], start=n == 0,
                                    stop=n == 2 * NT - 1)
                ins.then_inc(M["lists_done"], 1)

            pe.wait_ge(V["r_lo_done"], 1)
            transposed(2, 1, logits)
            router(0)
            experts(0)

            B = L_BLOCKS
            transposed(3, 2)
            dense(8, B, True)
            dense(9, B + 2, True)
            pe.wait_ge(A["panel_out"], 7)
            dense(10, B + 4, False)
            pe.wait_ge(A["panel_out"], 8)
            dense(11, B + 6, False)
            pe.wait_ge(A["panel_out"], 9)
            transposed(4, 2)
            dense(12, B + 8, True)
            pe.wait_ge(A["panel_out"], 10)
            dense(13, B + 10, True)

            def scores(hd, r, b, pair, reuse=True):
                pe.wait_ge(G["staged"], 4 * pair + 3)
                for p, blocks in enumerate(ZBLOCKS):
                    if reuse:
                        pe.wait_ge(A["weights_done"], 2 * hd + (p - 3))
                    for i in blocks:
                        z = z_of(r)[:, ZO[i]:ZO[i] + ZW[i]]
                        te.matmul(z, kst[:, b, P * i:P * (i + 1)], qst[r][:, b, P * i:T], start=i != 3, stop=True,
                                  skip_group_check=True)
                    for i in blocks:
                        ins = te.matmul(z_of(r)[:, ZO[i]:ZO[i] + P], ident_b[:, :], neg_mask[:, :], start=False, stop=True,
                                        skip_group_check=True)
                    ins.then_inc(M["z_done"], 1)

            def sums(hd, r):
                for p, blocks in enumerate(ZBLOCKS):
                    pe.wait_ge(V["L_lo_done"], 2 * hd + (p + 1))
                    for i in sorted(blocks):
                        for j in range(NT - 1, i - 1, -1):
                            o = z_of(r)[:, ZO[i] + P * (j - i):ZO[i] + ZW[i]]
                            for part in (s_hi, s_lo):
                                ins = te.matmul(o, (neg_tri if i == j else neg_one)[:, :], part[:, ZO[j]:ZO[j] + ZW[j]],
                                                start=False, stop=True, skip_group_check=True)
                    ins.then_inc(M["sums_done"], 1)

            def values(hd, r, b, pair, reuse=True):
                pe.wait_ge(A["weights_done"], 2 * hd + 2)
                pe.wait_ge(G["staged"], 4 * pair + 4)
                if reuse:
                    pe.wait_ge(V["oT_lo_done"], pair - 1)
                rows = slice(SD * r, SD * (r + 1))
                for j in range(NT):
                    ins = te.matmul(ps[rows, 6 + b, P * j:T], vst[:, b, j, SD * r:SD * (r + 1)],
                                    wt[r][:, ZO[j]:ZO[j] + ZW[j]], start=j == 0, stop=j == NT - 1,
                                    skip_group_check=True)
                ins.then_inc(M["av_done"], 1)

            scores(0, 0, 0, 0, False)
            scores(1, 1, 0, 0, False)

            def head(hd, r, pair, reuse=True, more=True):
                sums(hd, r % 2)
                if more:
                    scores(hd + 2, r % 2, (r // 2 + 1) % 2, pair + 1)
                values(hd, r % 2, r // 2, pair, reuse)

            for hd in range(4):
                head(hd, hd, hd // 2, False)
            with pe.Fori(1, 3) as g:
                for r in range(4):
                    head(4 * g + r, r, 2 * g + r // 2)
            for hd in range(12, 16):
                head(hd, hd - 12, hd // 2, more=hd < 14)
            pe.wait_ge(V["oT_lo_done"], 8)
            dense(14, B + 12, False)
            dense(15, B + 14, False)
            pe.wait_ge(V["r_lo_done"], 2)
            transposed(5, 3, logits)
            router(1)
            experts(1)

        @block.gpsimd
        def _(pool):
            link = Chain(pool, G["pool_chain"])
            gains = [m_norm[0], m_norm[1], final_norm]

            def load_gain(use):
                if use:
                    pool.wait_ge(V["xn_ready"], 2 * use)
                    pool.wait_ge(G["xn_normed"], 2 * use)
                pool.dma_start(gain[:, :], gains[use].partition_broadcast(P)).then_inc(G["gain_loaded"], 16)

            ge.memset(zeros[:, :], 0.0)
            def select(dst, src, op, fill, step, channel, base=0):
                return ge.affine_select(out=dst, in_=src, compare_op=op, fill=fill, base=base,
                                        pattern=[[step, dst.shape[-1]]], channel_multiplier=channel)

            for t, val in ((ident, 0.0), (ident_b, 0.0), (neg_mask, 0.0), (before, 1.0), (ones_b, 1.0), (one16, 1.0)):
                ge.memset(t[:, :], val)
            ge.memset(neg_tri[:, :].bitcast(F32), -1.0)
            ge.memset(neg_one[:, :].bitcast(F32), -1.0)
            ge.memset(parity[:, :], 0.0)
            link(ge.memset(reset, 1.0))
            link(ge.memset(parity[0:SD, 0:1], 1.0))
            link(ge.memset(parity[SD:P, 1:2], 1.0))
            select(ident[:, :], ident[:, :], ALU.not_equal, 1.0, -1, 1)
            select(ident_b[:, :], ident_b[:, :], ALU.not_equal, 1.0, -1, 1)
            select(neg_mask[:, :], neg_mask[:, :], ALU.is_gt, -1e30, 1, -1)
            select(before[:, :], before[:, :], ALU.is_gt, 0.0, 1, -1)
            select(neg_tri[:, :], neg_tri[:, :].bitcast(F32), ALU.is_ge, 0.0, -1, 1)
            ge.memset(reset.rearrange("p (c t) -> p c t", t=CHUNK)[:, :, 0:1], 0.0)
            for t, step, base, channel in ((desc4, -1, NG, 0), (desc16, -1, NE, 0), (caps, CAP, CAP, 0),
                                           (index, 1, 0, 0), (token_id, P, 0, 1)):
                last = ge.iota(t[:, :], pattern=[[step, t.shape[-1]]], base=base, channel_multiplier=channel,
                               allow_small_or_imprecise_dtypes=True)
            last.then_inc(G["consts"], 1)
            load_gain(0)
            pool.wait_ge(A["panel_out"], 1)
            zero_row = zeros[0:CAP, :].unsqueeze(1).broadcast_to([CAP, D // 256, 256])
            with pool.Fori(0, MAX_OVER) as i:
                pool.dma_start(table[bass.ds((i + NE) * CAP, CAP), :].rearrange("p (r n) -> p r n", n=256),
                               zero_row).then_inc(G["zeroed"], 16)
            for i in range(NT):
                pool.wait_ge(V["att_out"], i + 1)
                att = kT[:, i, :].rearrange("p (a q) -> p a q", q=P)
                ge.affine_select(out=att, in_=att, compare_op=ALU.is_ge, fill=0.0, base=0,
                                 pattern=[[0, GH], [1, P]], channel_multiplier=-1).then_inc(G["masked"], 1)
                pool.wait_ge(G["masked"], 2 * i + 1)
                ge.memset(att[0:CHUNK, :, CHUNK:P], 0.0).then_inc(G["masked"], 1)
            pool.wait_ge(A["panel_out"], 6)
            sg3 = sg.rearrange("p i (j e) -> p (i j) e", e=DV)
            ge.tensor_tensor(sg3, sg3, onorm.unsqueeze(1).broadcast_to([P, NT * GH, DV]), ALU.mult).then_inc(G["sg_ready"], 1)

            def experts(layer):
                I = NE * layer

                def gather(S, column, slot):
                    pool.indirect_dma_start(out=xg[:, slot, :], out_offset=None, in_=rows,
                                            in_offset=bass.IndirectOffsetOnAxis(ap=column, axis=0)).then_inc((S["x_loaded0"], S["x_loaded1"])[slot], 16)

                def column_copy(S, tile, slot):
                    ge.tensor_copy(token_now[:, slot:slot + 1], token[:, bass.ds(tile, 1)]).then_inc(S["column"], 1)

                pool.wait_ge(G["gain_loaded"], 16 * (layer + 1))
                for i in (2, 3):
                    pool.wait_ge(A["xn_scaled"], 2 * layer + i - 1)
                    ge.tensor_tensor(xn[:, i, :], xn[:, i, :], gain[:, :], ALU.mult).then_inc(G["xn_normed"], 1)
                pool.wait_ge(V["tokens_ready"], layer + 1)
                pool.wait_ge(A["rows_stored"], 16 * NT * (layer + 1))
                for slot in (0, 1):
                    gather(E, token[:, slot:slot + 1], slot)
                if layer:
                    load_gain(2)

                def store(S, row):
                    pool.dma_start(table[bass.ds(row, CAP), :], y_sb).then_inc(S["y_stored"], 16)

                with pool.Fori(0, PAIRS) as g:
                    for k in range(2):
                        i = 2 * g + (1 + k)
                        pool.wait_ge(E["x_tr"], 2 * i + 2 * I)
                        column_copy(E, i + 1, k)
                        pool.wait_ge(E["column"], i + (NE - 2) * layer)
                        pool.sem_inc(E["column_seen"], 1)
                        gather(E, token_now[:, k:k + 1], k)
                        pool.wait_ge(E["y_out"], i + I)
                        store(E, (i - 1) * CAP)
                for i in (NE - 2, NE - 1):
                    pool.wait_ge(E["y_out"], I + i + 1)
                    store(E, i * CAP)
                pool.wait_ge(E["y_stored"], 16 * (I + NE))
                S = O[layer]

                def tile(j):
                    column_copy(S, j + NE, 0)
                    pool.wait_ge(S["column"], j + 1)
                    pool.sem_inc(S["column_seen"], 1)
                    gather(S, token_now[:, 0:1], 0)
                    pool.wait_ge(S["y_out"], j + 1)
                    pool.sem_inc(S["out_seen"], 1)
                    store(S, (j + NE) * CAP)
                    pool.wait_ge(S["y_stored"], 16 * j + 16)
                    pool.sem_inc(S["turn"], 1)

                pool.sem_inc(S["turn"], 1)
                over_loop(pool, layer, tile)
                pool.sem_inc(G["over_ended"], 1)
                for n, (i, k) in enumerate(COMBINE):
                    pool.indirect_dma_start(out=y_rows[n], out_offset=None, in_=table,
                                            in_offset=bass.IndirectOffsetOnAxis(ap=pos[:, k, i:i + 1], axis=0)).then_inc(gathered[n], 16)

            experts(0)
            pool.wait_ge(A["panel_out"], 12)

            def stage_qk(q, b):
                ge.tensor_copy(kst[:, b, :], kT1[:, bass.ds(q, 1), :].rearrange("p o t -> p (o t)")).then_inc(G["staged"], 1)
                for r in range(2):
                    ge.tensor_tensor(qst[r][:, b, :], qT1[:, bass.ds(q, 1), :].rearrange("p o t -> p (o t)"),
                                     parity[:, r:r + 1].broadcast_to([P, T]), ALU.mult).then_inc(G["staged"], 1)

            def stage_v(q, b):
                ge.tensor_copy(vst[:, b, :, :], v[:, :, bass.ds(q * P, P)]).then_inc(G["staged"], 1)

            for q in (0, 1):
                stage_qk(q, q)
                stage_v(q, q)
            with pool.Fori(1, 4) as g:
                for b in range(2):
                    pool.wait_ge(M["z_done"], 8 * g + (4 * b - 4))
                    stage_qk(2 * g + b, b)
                    pool.wait_ge(M["av_done"], 4 * g + (2 * b - 2))
                    stage_v(2 * g + b, b)
            pool.wait_ge(M["z_done"], 2 * SH)
            load_gain(1)
            experts(1)
            pool.wait_ge(G["gain_loaded"], 16 * 3)
            for i in range(NT - 1):
                wait_h(pool, 4, i)
                ge.tensor_tensor(xn[:, i, :], h[:, i, :], gain[:, :], ALU.mult).then_inc(G["xn_normed"], 1)


_INS = ["x", "a_norm", "a_w_in", "a_w_gk2", "a_b_gk2", "a_o_norm", "a_w_out", "kv_norm", "w_kv", "b_norm",
        "b_w_q", "b_w_out", "m_norm", "m_w_group", "m_b_group", "m_w_expert", "m_b_expert", "m_w_gate",
        "m_w_up", "m_w_down", "final_norm"]


def kernel(**inputs):
    import numpy as np
    import concourse.bacc as bacc
    from concourse.bass_utils import run_bass_kernel_spmd

    nc = bacc.Bacc("TRN2", target_bir_lowering=False, num_devices=1)
    arrays, args = {}, []
    for name in _INS:
        a = np.ascontiguousarray(inputs[name])
        arrays[f"in_{name}"] = a
        args.append(nc.dram_tensor(f"in_{name}", a.shape, mybir.dt.from_np(a.dtype), kind="ExternalInput").ap())
    args.append(nc.dram_tensor("out_h", [1, T, D], F32, kind="ExternalOutput").ap())
    trunk(nc, *args)
    return run_bass_kernel_spmd(nc, [arrays], core_ids=[0]).results[0]["out_h"]
```
